# Optimizing a Trainium2 kernel written in Bass

```python
import math
import jax
import jax.numpy as jnp
from jax import lax
import numpy as np
import jax, jax.numpy as jnp

D_MODEL = 1024
BATCH = 1
SEQ = 1024
DEPTH = 1

POOL_WIDTH = D_MODEL // 2
POOL_WINDOWS = (2, 4, 8, 16)
N_POOL_GROUPS = len(POOL_WINDOWS)
POOL_GROUP_DIM = POOL_WIDTH // N_POOL_GROUPS

DIFF_HEAD_DIM = 64
N_DIFF_HEADS = D_MODEL // (4 * DIFF_HEAD_DIM)
DIFF_QK_WIDTH = N_DIFF_HEADS * 2 * DIFF_HEAD_DIM
DIFF_V_WIDTH = N_DIFF_HEADS * 2 * DIFF_HEAD_DIM

IN_WIDTH = POOL_WIDTH + 2 * DIFF_QK_WIDTH + DIFF_V_WIDTH + 2 * D_MODEL
FFN_HIDDEN = int(math.ceil((8 * D_MODEL / 3) / 256) * 256)
Q_BLOCK = 128
NORM_EPS = 1e-6


def rms_norm(x, g):
    xf = x.astype(jnp.float32)
    y = xf * lax.rsqrt(jnp.mean(xf * xf, axis=-1, keepdims=True) + NORM_EPS)
    return (y * g.astype(jnp.float32)).astype(x.dtype)

def alibi_slopes(n):
    start = 2.0 ** (-8.0 / n)
    return jnp.asarray(np.array([start ** (i + 1) for i in range(n)], dtype=np.float32))

def pool_mixer(p, pool_mix, pool_scale):
    B, S, _ = p.shape
    pg = p.reshape(B, S, N_POOL_GROUPS, POOL_GROUP_DIM).astype(jnp.float32)
    cs = jnp.cumsum(pg, axis=1)
    t = jnp.arange(S)
    outs = []
    for g, w in enumerate(POOL_WINDOWS):
        c = cs[:, :, g]
        prev = jnp.pad(c, ((0, 0), (w, 0), (0, 0)))[:, :S]
        cnt = jnp.minimum(t + 1, w).astype(jnp.float32)[None, :, None]
        outs.append((c - prev) / cnt - pg[:, :, g])
    y = jnp.stack(outs, axis=2).astype(p.dtype)
    y = jnp.einsum('bsgc,gcd->bsgd', y, pool_mix)
    return y.reshape(B, S, POOL_WIDTH) * pool_scale

def diff_attention(q, k, v, lam_q1, lam_k1, lam_q2, lam_k2, subln_g, lambda_init):
    B, S, _ = q.shape
    H, d = N_DIFF_HEADS, DIFF_HEAD_DIM
    q = q.reshape(B, S, H, 2, d).transpose(0, 2, 3, 1, 4)
    k = k.reshape(B, S, H, 2, d).transpose(0, 2, 3, 1, 4)
    vh = v.reshape(B, S, H, 2 * d).transpose(0, 2, 1, 3)
    k1, k2 = k[:, :, 0], k[:, :, 1]
    lam = (jnp.exp(jnp.sum(lam_q1.astype(jnp.float32) * lam_k1.astype(jnp.float32)))
           - jnp.exp(jnp.sum(lam_q2.astype(jnp.float32) * lam_k2.astype(jnp.float32)))
           + lambda_init)
    slopes = alibi_slopes(H)
    scale = 1.0 / math.sqrt(d)
    nblk = S // Q_BLOCK
    q1b = q[:, :, 0].reshape(B, H, nblk, Q_BLOCK, d).transpose(2, 0, 1, 3, 4)
    q2b = q[:, :, 1].reshape(B, H, nblk, Q_BLOCK, d).transpose(2, 0, 1, 3, 4)
    starts = jnp.arange(nblk) * Q_BLOCK
    kpos = jnp.arange(S)

    def block(args):
        qa, qb, start = args
        dist = (start + jnp.arange(Q_BLOCK))[:, None] - kpos[None, :]
        causal = dist >= 0
        bias = -slopes[:, None, None] * dist.astype(jnp.float32)[None]

        def probs(qq, kk):
            s = jnp.einsum('bhqd,bhkd->bhqk', qq, kk).astype(jnp.float32) * scale + bias
            s = jnp.where(causal, s, -jnp.inf)
            return jax.nn.softmax(s, axis=-1)

        a = probs(qa, k1) - lam * probs(qb, k2)
        return jnp.einsum('bhqk,bhkd->bhqd', a.astype(vh.dtype), vh)

    o = lax.map(block, (q1b, q2b, starts))
    o = o.transpose(1, 0, 3, 2, 4).reshape(B, S, H, 2 * d)
    o = rms_norm(o, subln_g) * (1.0 - lambda_init)
    return o.reshape(B, S, H * 2 * d)

def hybrid_layer(h, layer_idx, w_in, pool_mix, pool_scale, w_branch_a,
                 lam_q1, lam_k1, lam_q2, lam_k2, subln_g, w_branch_b, w_out,
                 mix_pre_g, mix_post_g, ffn_pre_g, ffn_post_g, w_ffn_gate, w_ffn_up, w_ffn_down):
    lambda_init = 0.8 - 0.6 * math.exp(-0.3 * layer_idx)
    u = rms_norm(h, mix_pre_g)
    z = jnp.einsum('bsd,de->bse', u, w_in)
    o1 = POOL_WIDTH
    o2 = o1 + DIFF_QK_WIDTH
    o3 = o2 + DIFF_QK_WIDTH
    o4 = o3 + DIFF_V_WIDTH
    o5 = o4 + D_MODEL
    p, q, k, v = z[..., :o1], z[..., o1:o2], z[..., o2:o3], z[..., o3:o4]
    gate_a, gate_b = z[..., o4:o5], z[..., o5:]
    ya = jnp.einsum('bsc,cd->bsd', pool_mixer(p, pool_mix, pool_scale), w_branch_a)
    yb = jnp.einsum('bsc,cd->bsd',
                    diff_attention(q, k, v, lam_q1, lam_k1, lam_q2, lam_k2, subln_g, lambda_init),
                    w_branch_b)
    m = jax.nn.sigmoid(gate_a) * ya + jax.nn.sigmoid(gate_b) * yb
    h = h + rms_norm(jnp.einsum('bsd,de->bse', m, w_out), mix_post_g)
    u = rms_norm(h, ffn_pre_g)
    f = jax.nn.silu(jnp.einsum('bsd,df->bsf', u, w_ffn_gate)) * jnp.einsum('bsd,df->bsf', u, w_ffn_up)
    h = h + rms_norm(jnp.einsum('bsf,fd->bsd', f, w_ffn_down), ffn_post_g)
    return h

def first_inputs(seed: int = 0) -> dict:
    key = jax.random.key(seed)
    ks = jax.random.split(key, 20)
    L = DEPTH
    f32 = jnp.float32

    def nrm(k, shape, fan_in):
        return jax.random.normal(k, shape, f32) * (fan_in ** -0.5)

    def gain(k, shape):
        return 1.0 + 0.05 * jax.random.normal(k, shape, f32)

    return {
        'x': jax.random.normal(ks[0], (BATCH, SEQ, D_MODEL), f32),
        'w_in': nrm(ks[1], (L, D_MODEL, IN_WIDTH), D_MODEL),
        'pool_mix': nrm(ks[2], (L, N_POOL_GROUPS, POOL_GROUP_DIM, POOL_GROUP_DIM), POOL_GROUP_DIM),
        'pool_scale': gain(ks[3], (L, POOL_WIDTH)),
        'w_branch_a': nrm(ks[4], (L, POOL_WIDTH, D_MODEL), POOL_WIDTH),
        'lam_q1': 0.1 * jax.random.normal(ks[5], (L, DIFF_HEAD_DIM), f32),
        'lam_k1': 0.1 * jax.random.normal(ks[6], (L, DIFF_HEAD_DIM), f32),
        'lam_q2': 0.1 * jax.random.normal(ks[7], (L, DIFF_HEAD_DIM), f32),
        'lam_k2': 0.1 * jax.random.normal(ks[8], (L, DIFF_HEAD_DIM), f32),
        'subln_g': gain(ks[9], (L, 2 * DIFF_HEAD_DIM)),
        'w_branch_b': nrm(ks[10], (L, DIFF_V_WIDTH, D_MODEL), DIFF_V_WIDTH),
        'w_out': nrm(ks[11], (L, D_MODEL, D_MODEL), D_MODEL),
        'mix_pre_g': gain(ks[12], (L, D_MODEL)),
        'mix_post_g': gain(ks[13], (L, D_MODEL)),
        'ffn_pre_g': gain(ks[14], (L, D_MODEL)),
        'ffn_post_g': gain(ks[15], (L, D_MODEL)),
        'w_ffn_gate': nrm(ks[16], (L, D_MODEL, FFN_HIDDEN), D_MODEL),
        'w_ffn_up': nrm(ks[17], (L, D_MODEL, FFN_HIDDEN), D_MODEL),
        'w_ffn_down': nrm(ks[18], (L, FFN_HIDDEN, D_MODEL), FFN_HIDDEN),
    }

def first_block(x, w_in, pool_mix, pool_scale, w_branch_a, lam_q1, lam_k1, lam_q2, lam_k2,
              subln_g, w_branch_b, w_out, mix_pre_g, mix_post_g, ffn_pre_g, ffn_post_g,
              w_ffn_gate, w_ffn_up, w_ffn_down):
    h = x
    for l in range(DEPTH):
        h = hybrid_layer(h, l, w_in[l], pool_mix[l], pool_scale[l], w_branch_a[l],
                         lam_q1[l], lam_k1[l], lam_q2[l], lam_k2[l], subln_g[l],
                         w_branch_b[l], w_out[l], mix_pre_g[l], mix_post_g[l],
                         ffn_pre_g[l], ffn_post_g[l], w_ffn_gate[l], w_ffn_up[l], w_ffn_down[l])
    return h


MEM_LEN = 256
EPS = 1e-6
GLA_HEADS = 4
GLA_DK = 64
GLA_DV = 128
GLA_RANK = 16
GLA_TAU = 16.0
GLA_CHUNK = 64
SWA_HEADS = 8
SWA_KV_HEADS = 2
SWA_DH = 64
WINDOW = 128
REL_BUCKETS = 32
REL_MAX_DIST = 128
CROSS_HEADS = 4
CROSS_DH = D_MODEL // CROSS_HEADS
D_FF = 2816
CONV_WIDTH = 3

GLA_KW = GLA_HEADS * GLA_DK
GLA_VW = GLA_HEADS * GLA_DV
SWA_QW = SWA_HEADS * SWA_DH
SWA_KVW = SWA_KV_HEADS * SWA_DH
D_MIX = GLA_VW + SWA_QW
IN_SPLITS = (GLA_KW, GLA_KW, GLA_VW, GLA_VW, GLA_RANK, SWA_QW, SWA_KVW, SWA_KVW)
D_IN = 2320


def rms_norm_2(x, g):
    xf = x.astype(jnp.float32)
    y = xf * lax.rsqrt(jnp.mean(xf * xf, axis=-1, keepdims=True) + EPS)
    return (y * g.astype(jnp.float32)).astype(x.dtype)

def t5_bucket(dist):
    n = jnp.maximum(dist, 0)
    max_exact = REL_BUCKETS // 2
    nf = jnp.maximum(n, 1).astype(jnp.float32)
    large = max_exact + (jnp.log(nf / max_exact) / math.log(REL_MAX_DIST / max_exact)
                         * (REL_BUCKETS - max_exact)).astype(jnp.int32)
    large = jnp.minimum(large, REL_BUCKETS - 1)
    return jnp.where(n < max_exact, n, large)

def gla_mixer(q, k, v, r, a_low, w_alpha, b_alpha, gla_gain):
    f32 = jnp.float32
    B, T, _ = q.shape
    C = GLA_CHUNK
    N = T // C
    log_a = jax.nn.log_sigmoid((a_low @ w_alpha + b_alpha).astype(f32)) / GLA_TAU

    def heads(t, d):
        return t.astype(f32).reshape(B, N, C, GLA_HEADS, d).transpose(0, 3, 1, 2, 4)

    qh = heads(q, GLA_DK) * (GLA_DK ** -0.5)
    kh = heads(k, GLA_DK)
    vh = heads(v, GLA_DV)
    bcum = jnp.cumsum(heads(log_a, GLA_DK), axis=3)
    b_last = bcum[:, :, :, -1:, :]
    q_dec = qh * jnp.exp(bcum)
    k_inv = kh * jnp.exp(-bcum)
    k_to_end = kh * jnp.exp(b_last - bcum)
    causal = jnp.tril(jnp.ones((C, C), dtype=bool))
    att = jnp.where(causal, jnp.einsum('bhnik,bhnjk->bhnij', q_dec, k_inv), 0.0)
    o_intra = jnp.einsum('bhnij,bhnjv->bhniv', att, vh)
    kv = jnp.einsum('bhnck,bhncv->nbhkv', k_to_end, vh)
    decay = jnp.exp(b_last[:, :, :, 0, :]).transpose(2, 0, 1, 3)

    def step(S, inp):
        d, kv_n = inp
        return d[..., None] * S + kv_n, S

    S0 = jnp.zeros((B, GLA_HEADS, GLA_DK, GLA_DV), f32)
    _, S_prev = lax.scan(step, S0, (decay, kv))
    o_inter = jnp.einsum('bhnck,nbhkv->bhncv', q_dec, S_prev)
    o = (o_intra + o_inter).transpose(0, 2, 3, 1, 4).reshape(B, T, GLA_HEADS, GLA_DV)
    o = o * lax.rsqrt(jnp.mean(o * o, axis=-1, keepdims=True) + EPS) * gla_gain.astype(f32)
    o = o.reshape(B, T, GLA_VW) * jax.nn.silu(r.astype(f32))
    return o.astype(q.dtype)

def swa_mixer(q, k, v, rel_bias, sinks):
    f32 = jnp.float32
    B, T, _ = q.shape
    L = WINDOW
    NB = T // L
    G = SWA_HEADS // SWA_KV_HEADS
    qb = q.astype(f32).reshape(B, NB, L, SWA_KV_HEADS, G, SWA_DH) * (SWA_DH ** -0.5)
    kb = k.astype(f32).reshape(B, NB, L, SWA_KV_HEADS, SWA_DH)
    vb = v.astype(f32).reshape(B, NB, L, SWA_KV_HEADS, SWA_DH)

    def with_prev(t):
        prev = jnp.pad(t, ((0, 0), (1, 0), (0, 0), (0, 0), (0, 0)))[:, :-1]
        return jnp.concatenate([prev, t], axis=2)

    kk = with_prev(kb)
    vv = with_prev(vb)
    s = jnp.einsum('bnqhgd,bnkhd->bnhgqk', qb, kk)
    qpos = jnp.arange(L)[:, None] + L
    kpos = jnp.arange(2 * L)[None, :]
    dist = qpos - kpos
    bias = rel_bias.astype(f32)[t5_bucket(dist)]
    bias = bias.transpose(2, 0, 1).reshape(SWA_KV_HEADS, G, L, 2 * L)
    in_window = (dist >= 0) & (dist < WINDOW)
    has_prev = (jnp.arange(NB)[:, None, None] > 0) | (kpos[None] >= L)
    mask = in_window[None] & has_prev
    s = jnp.where(mask[None, :, None, None], s + bias, -jnp.inf)
    sink = sinks.astype(f32).reshape(SWA_KV_HEADS, G)[None, None, :, :, None, None]
    m = jnp.maximum(jnp.max(s, axis=-1, keepdims=True), sink)
    p = jnp.exp(s - m)
    p = p / (jnp.sum(p, axis=-1, keepdims=True) + jnp.exp(sink - m))
    o = jnp.einsum('bnhgqk,bnkhd->bnqhgd', p, vv)
    return o.reshape(B, T, SWA_QW).astype(q.dtype)

def cross_attn(h, memn, w_q, w_k, w_v, w_o):
    B, T, _ = h.shape
    q = (h @ w_q).reshape(B, T, CROSS_HEADS, CROSS_DH)
    k = (memn @ w_k).reshape(B, MEM_LEN, CROSS_HEADS, CROSS_DH)
    v = (memn @ w_v).reshape(B, MEM_LEN, CROSS_HEADS, CROSS_DH)
    s = jnp.einsum('bqhd,bkhd->bhqk', q, k).astype(jnp.float32) * (CROSS_DH ** -0.5)
    p = jax.nn.softmax(s, axis=-1).astype(v.dtype)
    o = jnp.einsum('bhqk,bkhd->bqhd', p, v).reshape(B, T, D_MODEL)
    return o @ w_o

def conv_ffn(h, w_up, conv_w, conv_b, w_down):
    u = h @ w_up
    u = lax.conv_general_dilated(u, conv_w[:, None, :].astype(u.dtype), window_strides=(1,),
                                 padding=[(CONV_WIDTH - 1, 0)],
                                 dimension_numbers=('NWC', 'WIO', 'NWC'),
                                 feature_group_count=2 * D_FF) + conv_b
    gate, val = jnp.split(u, 2, axis=-1)
    return (jax.nn.silu(gate) * val) @ w_down

def second_inputs(seed: int = 0) -> dict:
    key = jax.random.key(seed)
    ks = jax.random.split(key, 24)
    f32 = jnp.float32

    def nrm(k, shape, scale):
        return jax.random.normal(k, shape, f32) * scale

    def gain(k, shape):
        return 1.0 + 0.02 * jax.random.normal(k, shape, f32)

    return {
        "x": nrm(ks[0], (BATCH, SEQ, D_MODEL), 1.0),
        "mem": nrm(ks[1], (BATCH, MEM_LEN, D_MODEL), 1.0),
        "norm_mix": gain(ks[2], (DEPTH, D_MODEL)),
        "w_in": nrm(ks[3], (DEPTH, D_MODEL, D_IN), D_MODEL ** -0.5),
        "w_alpha": nrm(ks[4], (DEPTH, GLA_RANK, GLA_KW), GLA_RANK ** -0.5),
        "b_alpha": nrm(ks[5], (DEPTH, GLA_KW), 0.1),
        "gla_gain": gain(ks[6], (DEPTH, GLA_DV)),
        "rel_bias": nrm(ks[7], (REL_BUCKETS, SWA_HEADS), 0.5),
        "sinks": nrm(ks[8], (DEPTH, SWA_HEADS), 0.5),
        "w_out": nrm(ks[9], (DEPTH, D_MIX, D_MODEL), D_MIX ** -0.5),
        "norm_cross": gain(ks[10], (DEPTH, D_MODEL)),
        "norm_mem": gain(ks[11], (DEPTH, D_MODEL)),
        "w_q_c": nrm(ks[12], (DEPTH, D_MODEL, D_MODEL), D_MODEL ** -0.5),
        "w_k_c": nrm(ks[13], (DEPTH, D_MODEL, D_MODEL), D_MODEL ** -0.5),
        "w_v_c": nrm(ks[14], (DEPTH, D_MODEL, D_MODEL), D_MODEL ** -0.5),
        "w_o_c": nrm(ks[15], (DEPTH, D_MODEL, D_MODEL), D_MODEL ** -0.5),
        "norm_ffn": gain(ks[16], (DEPTH, D_MODEL)),
        "w_up": nrm(ks[17], (DEPTH, D_MODEL, 2 * D_FF), D_MODEL ** -0.5),
        "conv_w": nrm(ks[18], (DEPTH, CONV_WIDTH, 2 * D_FF), CONV_WIDTH ** -0.5),
        "conv_b": nrm(ks[19], (DEPTH, 2 * D_FF), 0.01),
        "w_down": nrm(ks[20], (DEPTH, D_FF, D_MODEL), D_FF ** -0.5),
        "norm_final": gain(ks[21], (D_MODEL,)),
    }

def second_block(x, mem, norm_mix, w_in, w_alpha, b_alpha, gla_gain, rel_bias, sinks, w_out,
              norm_cross, norm_mem, w_q_c, w_k_c, w_v_c, w_o_c, norm_ffn, w_up, conv_w, conv_b,
              w_down, norm_final):
    split_at = [int(s) for s in np.cumsum(IN_SPLITS)[:-1]]
    h = x
    for l in range(DEPTH):
        hn = rms_norm_2(h, norm_mix[l])
        proj = hn @ w_in[l]
        gq, gk, gv, gr, ga, sq, sk, sv = jnp.split(proj, split_at, axis=-1)
        o_gla = gla_mixer(gq, gk, gv, gr, ga, w_alpha[l], b_alpha[l], gla_gain[l])
        o_swa = swa_mixer(sq, sk, sv, rel_bias, sinks[l])
        h = h + jnp.concatenate([o_gla, o_swa], axis=-1) @ w_out[l]
        h = h + cross_attn(rms_norm_2(h, norm_cross[l]), rms_norm_2(mem, norm_mem[l]),
                           w_q_c[l], w_k_c[l], w_v_c[l], w_o_c[l])
        h = h + conv_ffn(rms_norm_2(h, norm_ffn[l]), w_up[l], conv_w[l], conv_b[l], w_down[l])
    return rms_norm_2(h, norm_final)


def setup_inputs(seed=0):
    out = dict(first_inputs(seed))
    for name, value in second_inputs(seed + 1).items():
        if name != "x":
            out[name + "_2"] = value
    return out


def reference(
    x, w_in, pool_mix, pool_scale, w_branch_a, lam_q1, lam_k1, lam_q2, lam_k2, subln_g,
    w_branch_b, w_out, mix_pre_g, mix_post_g, ffn_pre_g, ffn_post_g, w_ffn_gate, w_ffn_up,
    w_ffn_down, mem_2, norm_mix_2, w_in_2, w_alpha_2, b_alpha_2, gla_gain_2, rel_bias_2,
    sinks_2, w_out_2, norm_cross_2, norm_mem_2, w_q_c_2, w_k_c_2, w_v_c_2, w_o_c_2, norm_ffn_2,
    w_up_2, conv_w_2, conv_b_2, w_down_2, norm_final_2,
):
    x = first_block(
        x, w_in, pool_mix, pool_scale, w_branch_a, lam_q1, lam_k1, lam_q2, lam_k2, subln_g,
        w_branch_b, w_out, mix_pre_g, mix_post_g, ffn_pre_g, ffn_post_g, w_ffn_gate, w_ffn_up,
        w_ffn_down,
    )
    return second_block(
        x, mem_2, norm_mix_2, w_in_2, w_alpha_2, b_alpha_2, gla_gain_2, rel_bias_2, sinks_2,
        w_out_2, norm_cross_2, norm_mem_2, w_q_c_2, w_k_c_2, w_v_c_2, w_o_c_2, norm_ffn_2,
        w_up_2, conv_w_2, conv_b_2, w_down_2, norm_final_2,
    )


_drawn_inputs = setup_inputs


def setup_inputs(seed=0):
    import zlib

    import numpy as np

    out = dict(_drawn_inputs(seed))
    spreads = {}
    factors = {'lam_q1': 8.0,
     'norm_mix_2': 5.412,
     'b_alpha_2': 4.941,
     'gla_gain_2': 8.0,
     'sinks_2': 64.0,
     'norm_cross_2': 8.0,
     'norm_mem_2': 8.0,
     'norm_ffn_2': 5.835,
     'conv_b_2': 32.104,
     'norm_final_2': 8.07}
    for name, (base, spread) in spreads.items():
        noise = np.random.default_rng([zlib.crc32(name.encode()), seed]).standard_normal(out[name].shape)
        drawn = base * np.exp(spread * noise) if base else spread * noise
        out[name] = jnp.asarray(drawn.astype(out[name].dtype))
    for name, factor in factors.items():
        out[name] = (out[name] * factor).astype(out[name].dtype)
    return out
```

```python
import math
from contextlib import ExitStack

import numpy as np
import concourse.bass as bass
from concourse import mybir

P = 128
SEQ = 1024
D = 1024
KT = D // P
NT = SEQ // P
HALF = 512
F = 2816
FC = F // P
EPS = 1e-6
MEM = 256
KB = 1024
BASE = 1152
RING = 144 * KB
CONST = RING + 72 * KB
NEG = -3.0e38
N_PARAMS = 15
LAMBDA_INIT = 0.8 - 0.6 * math.exp(-0.3 * 0)


class Plan:

    def __init__(self):
        self.groups, self.n, self.per, self.start = {}, 0, 0, 0
        self.blocks, self.b, self.pieces, self.bper, self.pper = {}, 0, 0, 0, 0
        self.stream, self.order, self.last, self.trip_of = [], [], {}, {}
        self.body = self.stream

    def group(self, *key):
        self.groups[key] = (self.n, self.per)
        self.n += 1

    def block(self, key, pieces):
        self.blocks[key] = (self.b, self.pieces, len(pieces), self.bper, self.pper)
        self.order.append((key, self.b))
        self.body.append((key, pieces))
        self.trip_of[key] = self.trips if self.bper else 1
        self.b += 1
        self.pieces += len(pieces)

    def loop(self, trips, groups, blocks, pieces):
        assert groups % 4 == 0 and blocks % 2 == 0 and pieces % 2 == 0
        self.per, self.bper, self.pper, self.trips = groups, blocks, pieces, trips
        self.marks = (self.n, self.b, self.pieces)
        self.body = []
        self.stream.append((trips, self.body))

    def end(self):
        n, b, p = self.marks
        assert (self.n - n, self.b - b, self.pieces - p) == (self.per, self.bper, self.pper)
        more = self.trips - 1
        self.n, self.b, self.pieces = self.n + more * self.per, self.b + more * self.bper, self.pieces + more * self.pper
        self.per = self.bper = self.pper = 0
        self.body = self.stream

    def reader(self, key):
        b, bper = self.blocks[key][0], self.blocks[key][3]
        if bper:
            return self.last[key], None
        for k, n in self.order:
            per = self.blocks[k][3]
            if (n == b - 2) or (per and b - 2 >= n and (b - 2 - n) % per == 0 and (b - 2 - n) // per < self.trip_of[k]):
                return self.last[k], (b - 2 - n) // per if per else 0
        return None

    def slot(self, key):
        return self.groups[key][0] % 4

    def uses(self, key, i=0):
        n, per = self.groups[key]
        return n // 4 + i * (per // 4) if per else n // 4


class Chain:

    def __init__(self, eng, sem):
        self.eng, self.sem, self.n, self.more = eng, sem, 0, 0

    def __call__(self, ins):
        self.n += 1
        ins.then_inc(self.sem, 1)
        self.eng.wait_ge(self.sem, self.more + self.n)

    def loop(self, i, per):
        self.start, self.per, self.more = self.n, per, i * per

    def end(self, trips):
        assert self.n - self.start == self.per, (self.n - self.start, self.per)
        self.n, self.more = self.start + trips * self.per, 0


def t5_ranges(window):
    out = []
    for dist in range(window):
        b = dist if dist < 16 else min(31, 16 + int(math.log(dist / 16) / math.log(128 / 16) * 16))
        if out and out[-1][0] == b:
            out[-1][2] = dist + 1
        else:
            out.append([b, dist, dist + 1])
    return out


def build(nc, a, out):
    f32, f32r, u32 = mybir.dt.float32, mybir.dt.float32r, mybir.dt.uint32
    ALU, ACT, AX = mybir.AluOpType, mybir.ActivationFunctionType, mybir.AxisListType
    ctx = ExitStack()

    def at(name, kb, shape, dt=f32):
        return nc.alloc_sbuf_tensor_at(name, shape, dt, offset=BASE + int(kb * KB))

    used = [CONST]

    def const(name, shape, dt=f32):
        t = nc.alloc_sbuf_tensor_at(name, shape, dt, offset=BASE + used[0])
        used[0] += (int(np.prod(shape[1:])) * 4 + 31) // 32 * 32
        assert BASE + used[0] <= 229344, used
        return t

    with ctx:
        def sem(name):
            return ctx.enter_context(nc.semaphore(name))

        Uhi, Ulo = at("Uhi", 0, [P, KT, SEQ], f32r), at("Ulo", 32, [P, KT, SEQ], f32r)
        Whi = nc.alloc_sbuf_tensor_at("Whi", [P, 2, 4096], f32r, offset=BASE + RING)
        Wlo = nc.alloc_sbuf_tensor_at("Wlo", [P, 2, 4096], f32r, offset=BASE + RING + 32 * KB)
        raw = nc.alloc_sbuf_tensor_at("raw", [P, 2, 1024], f32, offset=BASE + RING + 64 * KB)
        ident = const("ident", [P, P])
        colA, colB = const("colA", [P, 96]), const("colB", [P, 88])
        mixw = const("mixw", [P, 4, P])
        walpha = const("walpha", [16, 2, P])
        causal = const("causal", [P, P])
        eps = const("eps", [P, 1])
        tiny = const("tiny", [P, 2])
        cnt = const("cnt", [P, 16])
        lam2, nlam, lame = const("lam2", [P, 2]), const("nlam", [P, 1]), const("lame", [P, 2])
        ss, rt, rs = (const(x, [P, 4]) for x in ("ss", "rt", "rs"))
        ssp, rtp, rsp = (const(x, [P, 4]) for x in ("ssp", "rtp", "rsp"))
        ssA, rtA, rsA = (const(x, [P, 32]) for x in ("ssA", "rtA", "rsA"))
        nmax, lsum, rsum, c2 = (const(x, [P, 2, 8]) for x in ("nmax", "lsum", "rsum", "c2"))
        sink, smax, sexp = const("sink", [P, 8]), const("smax", [P, 2, 8]), const("sexp", [P, 2, 8])
        decay = const("decay", [P, 2, 16])
        rowA, rowB = at("rowA", 96, [96, P]), at("rowB", 96.5, [88, P])
        lamr, lamj = at("lamr", 97, [P, 4, 64]), at("lamj", 98, [P, 2, 64])
        pT, pS, pX = at("pT", 64, [P, 4, SEQ]), at("pS", 80, [P, 4, SEQ]), at("pX", 124, [P, SEQ])
        poolhi, poollo = at("poolhi", 96, [P, 4, SEQ], f32r), at("poollo", 112, [P, 4, SEQ], f32r)
        qT = at("qT", 128, [P, 4, SEQ])
        sgA, mst = at("sgA", 64, [P, 2, SEQ]), at("mst", 72, [P, 2, SEQ])
        kTt, vt = at("kTt", 96, [P, 4, SEQ]), at("vt", 112, [P, NT, 512])
        pp, aT = at("pp", 64, [P, 2, 2, SEQ]), at("aT", 80, [P, 2, SEQ])
        dist, junk = at("dist", 88, [P, SEQ]), at("junk", 92, [P, 2, P])
        oThi, oTlo = at("oThi", 96, [P, 4, SEQ], f32r), at("oTlo", 112, [P, 4, SEQ], f32r)
        M, sgB, prB = at("M", 64, [P, KT, SEQ]), at("sgB", 128, [P, 2, SEQ]), at("prB", 136, [P, 2, SEQ])
        Hhi, Hlo = at("Hhi", 64, [P, 2, SEQ], f32r), at("Hlo", 72, [P, 2, SEQ], f32r)
        hg, hv = at("hg", 80, [P, 2, SEQ]), at("hv", 88, [P, 2, SEQ])
        acc = at("acc", 96, [P, NT, D])
        gq, gk, gv = at("gq", 64, [P, 2, SEQ]), at("gk", 72, [P, 2, SEQ]), at("gv", 80, [P, NT, 512])
        gx, gt = at("gx", 80, [P, 2, SEQ]), at("gt", 88, [P, 2, SEQ])
        rT, sq, sk = at("rT", 96, [P, 4, SEQ]), at("sq", 112, [P, 4, SEQ]), at("sk", 128, [P, SEQ])
        sv, aL, reset, kend = at("sv", 132, [P, NT, P]), at("aL", 136, [16, SEQ]), at("reset", 140, [P, SEQ]), at("kend", 136, [P, 2, SEQ])
        kendt, S, attS = at("kendt", 0, [P, NT, 256]), at("S", 8, [P, 16, 2, P]), at("attS", 24, [P, 2, 4, P])
        bias, sS, pTs = at("bias", 32, [P, 8, 256]), at("sS", 40, [P, 2, 8, 256]), at("pTs", 56, [P, 8, 2, P])
        relT, line = at("relT", 28, [8, 32]), at("line", 29, [8, 384])
        gj = at("gj", 31, [P, P])
        sw = at("sw", 140, [P, SEQ])
        Os, mixt = at("Os", 64, [P, NT, 512]), at("mixt", 136, [P, 2, 4, P])
        memhi, memlo = at("memhi", 64, [P, KT, MEM], f32r), at("memlo", 72, [P, KT, MEM], f32r)
        kC, vC, qC = at("kC", 80, [P, KT, MEM]), at("vC", 88, [P, 2, D]), at("qC", 96, [P, KT, SEQ])
        pC, pTC = at("pC", 128, [P, 2, 4, MEM]), at("pTC", 136, [P, 2, 2, HALF])

        slots = [ctx.enter_context(nc.psum_tensor(f"slot{s}", [P, SEQ], f32)) for s in range(4)]
        hd = [nc.dram_tensor(f"h{n}", (SEQ, D), f32).ap() for n in range(4)]
        m_dram = nc.dram_tensor("m_part", (D, SEQ), f32).ap()
        line_dram = nc.dram_tensor("rel_line", (P, 8, 384), f32).ap()

        loaded = [sem(f"piece_loaded{n}") for n in range(2)]
        w_hi, w_split, raw_free, dist_made = sem("weight_hi"), sem("weight_split"), sem("raw_free"), sem("dist_made")
        full = [sem(f"slot_full{s}") for s in range(4)]
        free = [sem(f"slot_free{s}") for s in range(4)]
        act_own, dve_own, pool_own = sem("act_own"), sem("dve_own"), sem("pool_own")
        consts_made, params_in, cols_in = sem("consts_made"), sem("params_in"), sem("rows_turned")
        h_loaded = [sem(f"h_loaded{n}") for n in range(3)]
        h_stored = [sem(f"h_stored{n}") for n in range(3)]
        gains_in, post_root, h_new, pre_root, xn_done, tr_hi = (sem(x) for x in (
            "gains_in", "post_root", "h_new", "pre_root", "xn_done", "turned_hi"))
        out_stored = [sem(f"out_stored{n}") for n in range(2)]
        lam_sum, lam_exp, pool_ready, pool_hi = (sem(x) for x in ("lam_sum", "lam_exp", "pool_ready", "pool_hi"))
        m_stored, m_loaded, m_final, m_hi, m_lo = [sem("m_stored0"), sem("m_stored1")], sem("m_loaded"), sem("m_final"), sem("m_hi"), sem("m_lo")
        neg_max, p_exp, a_done, o_root, o_scaled, o_hi = (sem(x) for x in (
            "neg_max", "p_exp", "a_done", "o_root", "o_scaled", "o_hi"))
        conv_done, act_done, hid_prod, hid_hi, hid_lo = (sem(x) for x in ("conv_done", "gate_act", "hidden_prod", "hidden_hi", "hidden_lo"))
        g_abs, g_ln, g_cum, g_e1, g_d, g_e2, g_k, g_e3, k_end, q_dec = (sem(x) for x in (
            "gla_abs", "gla_ln", "gla_cumsum", "gla_exp_q", "gla_to_end", "gla_exp_end", "gla_k_end_done", "gla_exp_k",
            "k_end_done", "q_k_decayed"))
        att_ok, g_ss, g_out, states = sem("att_masked"), sem("gla_root"), sem("gla_out"), sem("states_done")
        line_ok, line_in, bias_in, s_max, s_exp, s_sexp, s_out = (sem(x) for x in (
            "line_made", "line_stored", "bias_in", "swa_max", "swa_exp", "swa_sink_exp", "swa_out"))
        s_shift, keys_swapped = sem("swa_shift"), sem("keys_swapped")
        mix_t, mix_hi = sem("mix_gated"), sem("mix_hi")
        c_max, c_exp, c_norm, c_hi = (sem(x) for x in ("cross_max", "cross_exp", "cross_normed", "cross_hi"))

        plan = Plan()

        def view(x):
            return x.rearrange("(k p) n -> p k n", p=P)

        def cols(w, k0, k1, c0, step, width):
            v = view(w)
            if step:
                return (lambda i, eng: v[:, k0:k1, bass.ds(eng.snap(i * step + c0), width)]), k1 - k0, width
            return (lambda i, eng: v[:, k0:k1, c0:c0 + width]), k1 - k0, width

        def wide(w, c0):
            return [cols(w, 2 * j, 2 * j + 2, c0, 0, HALF) for j in range(4)]

        w_in, w_in2 = a["w_in"][0], a["w_in_2"][0]
        stages = {}
        loads, stores, tiles = [0, 0, 0], [0, 0, 0], 0

        def stage(name, n, kind, hin, xn, gpre, gpost=None, src=None, dst=None, Y=None, gnames=(), dest=None, fused=None):
            nonlocal tiles
            st = dict(name=name, n=n, kind=kind, src=src, dst=dst, Y=Y, gnames=gnames, dest=dest, fused=fused, first=tiles,
                      hin=at(f"hin_{name}", hin, [P, 3 if n > 2 else 2, D]), xn=at(f"xn_{name}", xn, [P, 2, D]),
                      gpre=at(f"gpre_{name}", gpre, [P, D]),
                      gpost=None if gpost is None else at(f"gpost_{name}", gpost, [P, D]), load={}, store={})
            for t in range(n):
                loads[t % 3] += 1
                st["load"][t] = loads[t % 3]
                if dst is not None:
                    stores[t % 3] += 1
                    st["store"][t] = stores[t % 3]
            st["gains"] = sum(len(s["gnames"]) for s in stages.values()) + len(gnames)
            st["posts"] = sum(s["n"] for s in stages.values() if s["kind"] == "post")
            st["news"] = sum(s["n"] for s in stages.values() if s["kind"] != "load")
            st["turns"] = sum(s["n"] for s in stages.values() if s["dest"] is not None)
            stages[name] = st
            tiles += n

        def plan_stage(st, mm=None):
            for s in range(st["n"] + 2):
                if mm and s < st["n"]:
                    plan.group(*mm, s)
                if s >= 2 and st["dest"] is not None:
                    plan.group("T", st["name"], s - 2)

        U = (Uhi, Ulo)
        x_t = a["x"][0].rearrange("(t p) d -> t p d", p=P)
        hd_t = [h.rearrange("(t p) d -> t p d", p=P) for h in hd]
        mem_t = a["mem_2"][0].rearrange("(t p) d -> t p d", p=P)
        out_t = out[0].rearrange("(t p) d -> t p d", p=P)
        yM = at("yM", 64, [P, NT, D])
        y3, y4 = at("y3", 80, [P, NT, HALF]), at("y4", 128, [P, NT, HALF])
        stage("x", 8, "load", 64, 76, 84, src=x_t, gnames=("mix_pre_g",), dest=U)
        stage("mix1", 8, "post", 96, 108, 116, 120, src=x_t, dst=hd_t[0], Y=yM, gnames=("ffn_pre_g", "mix_post_g"), dest=U, fused="copy")
        stage("ffn1", 8, "post", 128, 88, 140, 80, src=hd_t[0], dst=hd_t[1], Y=acc, gnames=("norm_mix_2", "ffn_post_g"), dest=U)
        stage("mem", 2, "load", 132, 104, 100, src=mem_t, gnames=("norm_mem_2",), dest=(memhi, memlo))
        stage("mix2", 8, "add", 112, 124, 96, src=hd_t[1], dst=hd_t[2], Y=y3, gnames=("norm_cross_2",), dest=U, fused="add")
        stage("cross", 8, "add", 112, 104, 96, src=hd_t[2], dst=hd_t[3], Y=y4, gnames=("norm_ffn_2",), dest=U, fused="add")
        stage("ffn2", 8, "add", 128, 88, 140, src=hd_t[3], Y=acc, gnames=("norm_final_2",))

        UNITS = [(h, i) for h in range(4) for i in range(NT)]
        CU = [(hf, h) for hf in range(2) for h in range(4)]

        plan.group("cols")
        plan_stage(stages["x"])
        plan.block("p", wide(w_in, 0))
        for c in range(4):
            plan.group("p", c)
        plan.block("q", wide(w_in, 512))
        for c in range(4):
            plan.group("q", c)
        plan.last.update({k: (k, 3) for k in ("p", "q", "k", "gqk", "sq", "r")})
        plan.last.update({"v": ("v", 7), "gv": ("gv", 7), "misc": ("sv",)})
        plan.last.update({("gate", half, d): ("y", half, d) for half in "ab" for d in range(2)})
        plan.last.update({(n, cb): (n, cb, 7) for n in ("w_out", "w_out2", "w_o") for cb in range(2)})
        plan.last.update({(n, cb): (n, cb) for n in ("wk", "wv") for cb in range(2)})
        plan.last.update({("wq", cb): ("wq", cb, 3) for cb in range(2)})
        plan.last.update({(n, part): (n, *g) for n in ("f1", "f2") for part, g in (("up", ("u", 1)), ("down", ("d", 7)))})
        hid_base = {"f1": 2, "f2": 2 + FC}
        hi_base = {"f1": 0, "f2": FC}
        for g in range(4):
            plan.group("pool", g)
        for half, gcol, branch in (("a", 2048, a["w_branch_a"][0]), ("b", 3072, a["w_branch_b"][0])):
            plan.loop(4, 4, 2, 4)
            for d in range(2):
                plan.block(("gate", half, d), [cols(w_in, 0, KT, gcol + P * d, 256, P), cols(branch, 0, 4, P * d, 256, P)])
                plan.group("gate", half, d)
                plan.group("y", half, d)
            plan.end()
            if half == "a":
                plan.block("k", wide(w_in, 1024))
                for c in range(4):
                    plan.group("k", c)
                plan.block("v", wide(w_in, 1536))
                for t in range(NT):
                    plan.group("v", t)
                for u in range(-1, len(UNITS)):
                    if u + 1 < len(UNITS):
                        plan.group("sc", u + 1, 0)
                        plan.group("sc", u + 1, 1)
                    if u >= 0:
                        plan.group("aT", u)
                        plan.group("pv", u)
                for h in range(4):
                    plan.group("oT", h)

        def plan_out(name, w):
            for cb in range(2):
                plan.block((name, cb), wide(w, cb * HALF))
            for t in range(NT):
                plan.group(name, 0, t)

        plan_out("w_out", a["w_out"][0])
        plan_stage(stages["mix1"], ("w_out", 1))

        def plan_ffn(name, up_src, down):
            plan.loop(FC // 2, 12, 2, 6)
            plan.block((name, "up"), [cols(w, 4 * j, 4 * j + 4, c0, 256, 256) for w, c0 in up_src for j in range(2)])
            dv = down.rearrange("(c p) n -> p c n", p=P)
            plan.block((name, "down"), [((lambda i, eng, j=j: dv[:, bass.ds(eng.snap(i * 2 + j), 1), :]), 1, D) for j in range(2)])
            for c in range(2):
                plan.group(name, "g", c)
                plan.group(name, "u", c)
            for t in range(NT):
                plan.group(name, "d", t)
            plan.end()

        plan_ffn("f1", ((a["w_ffn_gate"][0], 0), (a["w_ffn_up"][0], 0)), a["w_ffn_down"][0])
        plan_stage(stages["ffn1"])
        plan.block("misc", [cols(w_in2, 0, KT, 1536, 0, P), cols(w_in2, 0, 4, 2064, 0, 256), cols(w_in2, 4, KT, 2064, 0, 256)])
        plan.block("gqk", wide(w_in2, 0))
        for key in ("ga", "sk", "sv"):
            plan.group(key)
        for c in range(4):
            plan.group("gqk", c)
        plan.group("alpha", 0)
        plan.group("alpha", 1)
        plan.block("sq", wide(w_in2, 1552))
        plan.block("r", wide(w_in2, 1024))
        plan.block("gv", wide(w_in2, 512))
        for key in ("sq", "r"):
            for c in range(4):
                plan.group(key, c)
        for t in range(NT):
            plan.group("gv", t)
        for j in range(2):
            plan.group("kendT", j)
        for j in range(4):
            plan.group("kv", j)
        for t in range(-1, NT):
            if t + 1 < NT:
                plan.group("att", t + 1)
            if t >= 0:
                plan.group("go", t)
        for t in range(-1, NT):
            if t + 1 < NT:
                plan.group("ssc", t + 1, 0)
                plan.group("ssc", t + 1, 1)
            if t >= 0:
                plan.group("spT", t, 0)
                plan.group("spT", t, 1)
                plan.group("so", t)
        for t in range(NT):
            plan.group("mixT", t)
        plan_out("w_out2", a["w_out_2"][0])
        plan_stage(stages["mem"])
        plan_stage(stages["mix2"], ("w_out2", 1))
        for key, w in (("wk", a["w_k_c_2"][0]), ("wv", a["w_v_c_2"][0]), ("wq", a["w_q_c_2"][0])):
            for cb in range(2):
                plan.block((key, cb), wide(w, cb * HALF))
                if key == "wv":
                    plan.group(key, cb)
                elif key == "wk":
                    plan.group(key, cb)
                else:
                    for c in range(4):
                        plan.group(key, cb, c)
        for u in range(-1, len(CU)):
            if u + 1 < len(CU):
                plan.group("cs", u + 1)
            if u >= 0:
                plan.group("cT", u)
                plan.group("co", u)
        plan_out("w_o", a["w_o_c_2"][0])
        plan_stage(stages["cross"], ("w_o", 1))
        plan_ffn("f2", ((a["w_up_2"][0], 0), (a["w_up_2"][0], F)), a["w_down_2"][0])

        def slot(*key):
            return slots[plan.slot(key)]

        def wait_full(eng, *key, i=0):
            eng.wait_ge(full[plan.slot(key)], plan.uses(key, i) + 1)

        def wait_freed(eng, *key, i=0):
            eng.wait_ge(free[plan.slot(key)], plan.uses(key, i) + 1)

        def freed(ins, *key):
            ins.then_inc(free[plan.slot(key)], 1)

        block = ctx.enter_context(nc.Block())

        @block.sync
        def _(sp):
            def load(src, n, w, p, i, per):
                s = p % 2
                src = src(i, sp)
                if p >= 2 or per:
                    sp.wait_ge(w_split, i * per + p - 1)
                    sp.sem_inc(raw_free, 1)
                sp.dma_start(raw[:, s, 0:n * w].rearrange("p (k c) -> p k c", k=n), src).then_inc(loaded[s], 16)

            p = 0
            for entry in plan.stream:
                if isinstance(entry[0], int):
                    trips, body = entry
                    per = sum(len(pieces) for _, pieces in body)
                    with sp.Fori(0, trips) as i:
                        q = p
                        for _, pieces in body:
                            for src, n, w in pieces:
                                load(src, n, w, q, i, per)
                                q += 1
                    p += trips * per
                else:
                    for src, n, w in entry[1]:
                        load(src, n, w, p, 0, 0)
                        p += 1

        @block.gpsimd
        def _(pool):
            own = Chain(pool, pool_own)
            own(pool.memset(ident[:, :], 0.0))
            pool.affine_select(out=ident[:, :], in_=ident[:, :], compare_op=ALU.not_equal, fill=1.0, base=0,
                               pattern=[[-1, P]], channel_multiplier=1).then_inc(consts_made, 1)
            pool.memset(eps[:, :], EPS).then_inc(consts_made, 1)
            own(pool.memset(causal[:, :], 1.0))
            own(pool.affine_select(out=causal[:, :], in_=causal[:, :], compare_op=ALU.is_ge, fill=0.0, base=0,
                                   pattern=[[1, P]], channel_multiplier=-1))
            pool.memset(causal[0:64, 64:128], 0.0).then_inc(consts_made, 1)
            own(pool.iota(cnt[:, :], pattern=[[1, 16]], base=1, channel_multiplier=0, allow_small_or_imprecise_dtypes=True))
            own(pool.memset(tiny[:, :], 1.0))

            def split(key, dst, first, n, p, b, i, per):
                s = p % 2
                if first and plan.reader(key):
                    group, trip = plan.reader(key)
                    count = plan.uses(group, i) + 1 - plan.groups[group][1] // 4 if trip is None else plan.uses(group, trip) + 1
                    pool.wait_ge(full[plan.slot(group)], count)
                pool.wait_ge(loaded[s], i * (per * 8) + 16 * (p // 2 + 1))
                pool.tensor_tensor(tiny[:, 1:2], tiny[:, 0:1], tiny[:, 0:1], ALU.mult)
                hi, lo = Whi[:, b % 2, dst:dst + n], Wlo[:, b % 2, dst:dst + n]
                pool.tensor_scalar(hi, raw[:, s, 0:n], 1.0, 1.0, ALU.mult, ALU.mult).then_inc(w_hi, 1)
                pool.wait_ge(w_hi, i * per + p + 1)
                pool.tensor_tensor(lo, raw[:, s, 0:n], hi.bitcast(f32), ALU.subtract).then_inc(w_split, 1)

            def make_dist():
                wait_full(pool, "pool", 3)
                own(pool.iota(dist[:, :], pattern=[[1, SEQ]], base=-(SEQ - P), channel_multiplier=-1, allow_small_or_imprecise_dtypes=True))
                pool.affine_select(out=dist[:, :], in_=dist[:, :], compare_op=ALU.is_ge, fill=NEG, base=SEQ - P,
                                   pattern=[[-1, SEQ]], channel_multiplier=1).then_inc(dist_made, 1)

            def run(blocks, p, b, i, per):
                for key, pieces in blocks:
                    if key == "k":
                        make_dist()
                    dst = 0
                    for j, (_, n, w) in enumerate(pieces):
                        split(key, dst, j == 0, n * w, p, b, i, per)
                        dst += n * w
                        p += 1
                    b += 1
                return p, b

            p = b = 0
            for entry in plan.stream:
                if isinstance(entry[0], int):
                    trips, body = entry
                    per = sum(len(pieces) for _, pieces in body)
                    with pool.Fori(0, trips) as i:
                        run(body, p, b, i, per)
                    p, b = p + trips * per, b + trips * len(body)
                else:
                    p, b = run([entry], p, b, 0, 0)

        @block.tensor
        def _(pe):
            def begin(*key, i=0):
                if plan.groups[key][0] >= 4 or plan.groups[key][1]:
                    pe.wait_ge(free[plan.slot(key)], plan.uses(key, i))
                return slots[plan.slot(key)]

            def done(ins, *key):
                ins.then_inc(full[plan.slot(key)], 1)

            def weights(key, i=0):
                b, p, n, bper, pper = plan.blocks[key]
                pe.wait_ge(w_split, i * pper + p + n if pper else p + n)
                return Whi[:, b % 2, :], Wlo[:, b % 2, :]

            def mm3(o, l, r, start, stop):
                for j, (x, y) in enumerate(((0, 0), (0, 1), (1, 0))):
                    ins = pe.matmul(o, lhsT=l[x], rhs=r[y], start=start and j == 0, stop=stop and j == 2)
                return ins

            def pair(t, *idx):
                return tuple(x[idx] for x in t)

            def turn(o, src):
                return pe.transpose(o, src, ident[:, :])

            def features(w, off, width, c, src, key, i=0, n=KT, tokens=SEQ):
                o = begin(*key, i=i)
                wv = tuple(x[:, off:off + n * width].rearrange("p (k c) -> p k c", k=n) for x in w)
                step = min(HALF, tokens)
                for t0 in range(0, tokens, step):
                    for k in range(n):
                        ins = mm3(o[:, t0:t0 + step], pair(wv, slice(None), k, slice(c, c + P)),
                                  pair(src, slice(None), k, slice(t0, t0 + step)), k == 0, k == n - 1)
                return ins

            def tokens(w, t, src, o):
                wv = tuple(x.rearrange("p (k c) -> p k c", k=KT) for x in w)
                for k in range(KT):
                    ins = mm3(o, pair(src, slice(None), k, slice(t * P, t * P + P)), pair(wv, slice(None), k), k == 0, k == KT - 1)
                return ins

            def wide_features(key, src, block_key=None):
                w = weights(block_key or key[0])
                for c in range(4):
                    k = (*key, c)
                    done(features(w, 0, HALF, c * P, src, k), *k)

            def run_stage(st, mm=None, w=None, src=None):
                n = st["n"]
                for s in range(n + 2):
                    if mm and s < n:
                        key = (*mm, s)
                        o = begin(*key)
                        done(tokens(w, s, src, o[:, 0:HALF]), *key)
                    t = s - 2
                    if t >= 0 and st["dest"] is not None:
                        pe.wait_ge(xn_done, st["first"] + t + 1)
                        o = begin("T", st["name"], t)
                        for k in range(KT):
                            ins = turn(o[:, k * P:k * P + P], st["xn"][:, t % 2, k * P:k * P + P])
                        done(ins, "T", st["name"], t)

            def u_ready(name, n=NT):
                for t in range(n):
                    wait_freed(pe, "T", name, t)

            def ffn(name):
                with pe.Fori(0, FC // 2) as i:
                    w = weights((name, "up"), i)
                    for c in range(2):
                        for j, part in enumerate("gu"):
                            done(features(w, 2048 * j, 256, c * P, U, (name, part, c), i), name, part, c)
                    w = tuple(x[:, 0:2 * D].rearrange("p (c n) -> p c n", c=2) for x in weights((name, "down"), i))

                    def down(t, c, o):
                        for half in range(2):
                            cs = slice(half * HALF, half * HALF + HALF)
                            ins = mm3(o[:, cs], (Hhi[:, c, t * P:t * P + P], Hlo[:, c, t * P:t * P + P]),
                                      pair(w, slice(None), c, cs), c == 0, c == 1)
                        return ins

                    base = hid_base[name]
                    pe.wait_ge(hid_lo, i * 2 + base + 1)
                    for t in range(4):
                        down(t, 0, begin(name, "d", t, i=i))
                    pe.wait_ge(hid_lo, i * 2 + base + 2)
                    for t in range(4):
                        done(down(t, 1, slot(name, "d", t)), name, "d", t)
                    for t in range(4, NT):
                        o = begin(name, "d", t, i=i)
                        down(t, 0, o)
                        done(down(t, 1, o), name, "d", t)

            pe.wait_ge(consts_made, 3)
            pe.wait_ge(params_in, 16 * N_PARAMS)
            o = begin("cols")
            pe.transpose(o[:, 0:96], rowA[:, :], ident[0:96, 0:96])
            done(pe.transpose(o[:, HALF:HALF + 88], rowB[:, :], ident[0:88, 0:88]), "cols")
            run_stage(stages["x"])
            u_ready("x")
            wide_features(("p",), U)
            wide_features(("q",), U)
            for g in range(4):
                pe.wait_ge(pool_ready, g + 1)
                o = begin("pool", g)
                for hf in range(2):
                    ins = pe.matmul(o[:, hf * HALF:hf * HALF + HALF], lhsT=mixw[:, g, :],
                                    rhs=pS[:, g, hf * HALF:hf * HALF + HALF], start=True, stop=True)
                done(ins, "pool", g)

            def gates(half, src):
                with pe.Fori(0, 4) as i:
                    for d in range(2):
                        w = weights(("gate", half, d), i)
                        done(features(w, 0, P, 0, U, ("gate", half, d), i), "gate", half, d)
                        done(features(w, D, P, 0, src, ("y", half, d), i, n=4), "y", half, d)

            for g in range(4):
                wait_freed(pe, "pool", g)
            gates("a", (poolhi, poollo))
            wide_features(("k",), U)
            w = weights("v")
            for t in range(NT):
                done(tokens(w, t, U, begin("v", t)[:, 0:HALF]), "v", t)
            for c in range(4):
                wait_freed(pe, "k", c)
            for t in range(NT):
                wait_freed(pe, "v", t)
            for u in range(-1, len(UNITS)):
                if u + 1 < len(UNITS):
                    h, i = UNITS[u + 1]
                    for m in range(2):
                        o = begin("sc", u + 1, m)
                        r = slice(64 * m, 64 * m + 64)
                        for c0 in range(0, P * (i + 1), HALF):
                            c1 = min(c0 + HALF, P * (i + 1))
                            ins = pe.matmul(o[:, c0:c1], lhsT=qT[r, h, i * P:i * P + P], rhs=kTt[r, h, c0:c1], start=True, stop=True)
                        done(ins, "sc", u + 1, m)
                if u >= 0:
                    h, i = UNITS[u]
                    pe.wait_ge(a_done, u + 1)
                    o = begin("aT", u)
                    for j in range(i + 1):
                        ins = turn(o[:, j * P:j * P + P], pp[:, u % 2, 0, j * P:j * P + P])
                    done(ins, "aT", u)
                    wait_freed(pe, "aT", u)
                    o = begin("pv", u)
                    for j in range(i + 1):
                        ins = pe.matmul(o[:, 0:P], lhsT=aT[:, u % 2, j * P:j * P + P], rhs=vt[:, j, h * P:h * P + P],
                                        start=j == 0, stop=j == i)
                    done(ins, "pv", u)
            for h in range(4):
                pe.wait_ge(o_scaled, h + 1)
                o = begin("oT", h)
                for i in range(NT):
                    ins = turn(o[:, i * P:i * P + P], qT[:, h, i * P:i * P + P])
                done(ins, "oT", h)
            for h in range(4):
                wait_freed(pe, "oT", h)
            gates("b", (oThi, oTlo))
            w = weights(("w_out", 0))
            pe.wait_ge(m_lo, KT)
            for t in range(NT):
                done(tokens(w, t, U, begin("w_out", 0, t)[:, 0:HALF]), "w_out", 0, t)
            run_stage(stages["mix1"], ("w_out", 1), weights(("w_out", 1)), U)
            u_ready("mix1")
            ffn("f1")
            run_stage(stages["ffn1"])
            u_ready("ffn1")
            w = weights("misc")
            done(features(w, 0, P, 0, U, ("ga",)), "ga")
            done(features(w, D, 256, 0, U, ("sk",)), "sk")
            o = begin("sv")
            wv = tuple(x[:, D:D + KT * 256].rearrange("p (k c) -> p k c", k=KT) for x in w)
            for t in range(NT):
                for k in range(KT):
                    ins = mm3(o[:, t * P:t * P + P], pair(U, slice(None), k, slice(t * P, t * P + P)),
                              pair(wv, slice(None), k, slice(P, 256)), k == 0, k == KT - 1)
            done(ins, "sv")
            wide_features(("gqk",), U)
            wait_freed(pe, "ga")
            for hp in range(2):
                o = begin("alpha", hp)
                for hf in range(2):
                    ins = pe.matmul(o[:, hf * HALF:hf * HALF + HALF], lhsT=walpha[:, hp, :],
                                    rhs=aL[:, hf * HALF:hf * HALF + HALF], start=True, stop=True)
                done(ins, "alpha", hp)
            wide_features(("sq",), U)
            wide_features(("r",), U)
            w = weights("gv")
            for t in range(NT):
                done(tokens(w, t, U, begin("gv", t)[:, 0:HALF]), "gv", t)
            pe.wait_ge(q_dec, 1)
            for j in range(2):
                o = begin("kendT", j)
                for tt in range(4):
                    for hp in range(2):
                        t = 4 * j + tt
                        c = tt * 256 + hp * P
                        ins = turn(o[:, c:c + P], kend[:, hp, t * P:t * P + P])
                done(ins, "kendT", j)
            for j in range(2):
                wait_freed(pe, "kendT", j)
            for t in range(NT):
                wait_freed(pe, "gv", t)
            for j in range(4):
                o = begin("kv", j)
                for tt in range(2):
                    t = 2 * j + tt
                    for par in range(2):
                        r = slice(64 * par, 64 * par + 64)
                        for h in range(4):
                            hp, hh = h // 2, h % 2
                            c = par * HALF + tt * 256 + hp * P
                            ins = pe.matmul(o[64 * hh:64 * hh + 64, c:c + P], lhsT=kendt[r, t, h * 64:h * 64 + 64],
                                            rhs=gv[r, t, h * P:h * P + P], start=True, stop=True)
                done(ins, "kv", j)
            for t in range(-1, NT):
                if t + 1 < NT:
                    o = begin("att", t + 1)
                    ts = slice((t + 1) * P, (t + 2) * P)
                    for h in range(4):
                        hp, hh = h // 2, h % 2
                        r = slice(64 * hh, 64 * hh + 64)
                        c = hh * HALF + hp * P
                        ins = pe.matmul(o[:, c:c + P], lhsT=gk[r, hp, ts], rhs=gq[r, hp, ts], start=True, stop=True)
                    done(ins, "att", t + 1)
                if t >= 0:
                    if t == 0:
                        pe.wait_ge(states, 15)
                    pe.wait_ge(att_ok, 2 + t + 1)
                    o = begin("go", t)
                    for h in range(4):
                        hp, hh = h // 2, h % 2
                        r = slice(64 * hh, 64 * hh + 64)
                        c = hh * HALF + hp * P
                        ins = pe.matmul(o[:, c:c + P], lhsT=attS[:, t % 2, h, :], rhs=gv[:, t, h * P:h * P + P], start=True, stop=False,
                                        skip_group_check=True)
                        for par in range(2):
                            n = 2 * t + par
                            if n:
                                ins = pe.matmul(o[64 * par:64 * par + 64, c:c + P], lhsT=gq[r, hp, n * 64:n * 64 + 64],
                                                rhs=S[r, n, hp, :], start=False, stop=par == 1, skip_group_check=True)
                    done(ins, "go", t)
            pe.wait_ge(keys_swapped, 32)
            for t in range(-1, NT):
                if t + 1 < NT:
                    n = t + 1
                    k0 = max(n - 1, 0) * P
                    off = P if n == 0 else 0
                    for g in range(2):
                        o = begin("ssc", n, g)
                        for hh in range(2):
                            r = slice(64 * hh, 64 * hh + 64)
                            keys = sk if hh == g else sw
                            for c in range(2):
                                c1 = hh * HALF + c * 256
                                ins = pe.matmul(o[:, c1 + off:c1 + 256], lhsT=sq[r, 2 * g + c, n * P:n * P + P],
                                                rhs=keys[r, k0:n * P + P], start=True, stop=True)
                        done(ins, "ssc", n, g)
                if t >= 0:
                    kts = (1,) if t == 0 else (0, 1)
                    pe.wait_ge(s_exp, 8 * (t + 1))
                    for g in range(2):
                        o = begin("spT", t, g)
                        for c in range(4):
                            for kt in kts:
                                cc = c * 256 + kt * P
                                ins = turn(o[:, cc:cc + P], sS[:, t % 2, 4 * g + c, kt * P:kt * P + P])
                        done(ins, "spT", t, g)
                    o = begin("so", t)
                    for g in range(2):
                        wait_freed(pe, "spT", t, g)
                        for c in range(4):
                            h = 4 * g + c
                            for kt in kts:
                                ins = pe.matmul(o[:, h * 64:h * 64 + 64], lhsT=pTs[:, h, kt, :],
                                                rhs=sv[:, t - 1 + kt, g * 64:g * 64 + 64], start=kt == kts[0], stop=kt == 1)
                    done(ins, "so", t)
            for t in range(NT):
                pe.wait_ge(g_out, t + 1)
                wait_freed(pe, "so", t)
                o = begin("mixT", t)
                for k in range(4):
                    turn(o[:, k * P:k * P + P], gv[:, t, k * P:k * P + P])
                for k in range(4):
                    ins = turn(o[:, HALF + k * P:HALF + k * P + P], Os[:, t, k * P:k * P + P])
                done(ins, "mixT", t)
            w = weights(("w_out2", 0))
            for t in range(NT):
                wait_freed(pe, "mixT", t)
            for t in range(NT):
                done(tokens(w, t, U, begin("w_out2", 0, t)[:, 0:HALF]), "w_out2", 0, t)
            run_stage(stages["mem"])
            run_stage(stages["mix2"], ("w_out2", 1), weights(("w_out2", 1)), U)
            u_ready("mem", 2)
            for cb in range(2):
                w = weights(("wk", cb))
                o = begin("wk", cb)
                wv = tuple(x.rearrange("p (k c) -> p k c", k=KT) for x in w)
                for c in range(4):
                    for k in range(KT):
                        ins = mm3(o[:, c * MEM:c * MEM + MEM], pair(wv, slice(None), k, slice(c * P, c * P + P)),
                                  (memhi[:, k, :], memlo[:, k, :]), k == 0, k == KT - 1)
                done(ins, "wk", cb)
            for cb in range(2):
                w = weights(("wv", cb))
                o = begin("wv", cb)
                for t in range(2):
                    ins = tokens(w, t, (memhi, memlo), o[:, t * HALF:t * HALF + HALF])
                done(ins, "wv", cb)
            u_ready("mix2")
            for cb in range(2):
                wide_features(("wq", cb), U, ("wq", cb))
            for cb in range(2):
                wait_freed(pe, "wk", cb)
                wait_freed(pe, "wv", cb)
                for c in range(4):
                    wait_freed(pe, "wq", cb, c)
            for u in range(-1, len(CU)):
                if u + 1 < len(CU):
                    hf, h = CU[u + 1]
                    o = begin("cs", u + 1)
                    for j in range(4):
                        t = 4 * hf + j
                        for k in range(2):
                            ins = pe.matmul(o[:, j * MEM:j * MEM + MEM], lhsT=qC[:, 2 * h + k, t * P:t * P + P],
                                            rhs=kC[:, 2 * h + k, :], start=k == 0, stop=k == 1)
                    done(ins, "cs", u + 1)
                if u >= 0:
                    hf, h = CU[u]
                    pe.wait_ge(c_norm, u + 1)
                    o = begin("cT", u)
                    for kt in range(2):
                        for j in range(4):
                            c = kt * HALF + j * P
                            ins = turn(o[:, c:c + P], pC[:, u % 2, j, kt * P:kt * P + P])
                    done(ins, "cT", u)
                    wait_freed(pe, "cT", u)
                    o = begin("co", u)
                    for dt in range(2):
                        for kt in range(2):
                            f0 = h * 256 + dt * P
                            ins = pe.matmul(o[:, dt * HALF:dt * HALF + HALF], lhsT=vC[:, kt, f0:f0 + P],
                                            rhs=pTC[:, u % 2, kt, :], start=kt == 0, stop=kt == 1)
                    done(ins, "co", u)
            for u in range(len(CU)):
                wait_freed(pe, "co", u)
            w = weights(("w_o", 0))
            for t in range(NT):
                done(tokens(w, t, U, begin("w_o", 0, t)[:, 0:HALF]), "w_o", 0, t)
            run_stage(stages["cross"], ("w_o", 1), weights(("w_o", 1)), U)
            u_ready("cross")
            ffn("f2")

        @block.scalar
        def _(act):
            own = Chain(act, act_own)

            def load_h(st, t):
                b = t % 3
                if t >= 3:
                    act.wait_ge(xn_done, st["first"] + t - 2)
                    if st["dst"] is not None:
                        act.wait_ge(h_stored[b], 16 * st["store"][t - 3])
                act.dma_start(st["hin"][:, b, :], st["src"][t]).then_inc(h_loaded[b], 16)

            def begin_stage(st):
                gains = (st["gpre"], st["gpost"])
                for g, name in zip(gains, st["gnames"]):
                    v = a[name] if name == "norm_final_2" else a[name][0]
                    act.dma_start(g[:, :], v.partition_broadcast(P)).then_inc(gains_in, 16)
                load_h(st, 0)

            def run_stage(st, mm=None):
                n, hin, xn, Y = st["n"], st["hin"], st["xn"], st["Y"]
                for s in range(n + 2):
                    if s < n and st["kind"] == "post":
                        if st["fused"]:
                            wait_full(act, *mm, s)
                            wait_freed(act, mm[0], 0, s)
                            freed(act.activation(Y[:, s, HALF:D], slot(*mm, s)[:, 0:HALF], ACT.Copy), *mm, s)
                            wait_freed(act, *mm, s)
                        else:
                            wait_freed(act, "f1", "d", s, i=FC // 2 - 1)
                        if s >= 2:
                            act.wait_ge(xn_done, st["first"] + s - 1)
                            wait_full(act, "T", st["name"], s - 2)
                        own(act.activation(xn[:, s % 2, :], Y[:, s, :], ACT.Square, accum_out=ssp[:, s % 4:s % 4 + 1]))
                        if s >= 4:
                            act.wait_ge(h_new, st["news"] + s - 3)
                        act.activation(rtp[:, s % 4:s % 4 + 1], ssp[:, s % 4:s % 4 + 1], ACT.Sqrt, bias=eps[:, :], scale=1.0 / D).then_inc(post_root, 1)
                    t = s - 1
                    if 0 <= t < n:
                        b = t % 3
                        if st["kind"] == "load":
                            act.wait_ge(h_loaded[b], 16 * st["load"][t])
                        else:
                            act.wait_ge(h_new, st["news"] + t + 1)
                            if st["dst"] is not None:
                                act.dma_start(st["dst"][t], hin[:, b, :]).then_inc(h_stored[b], 16)
                        if t >= 2:
                            if st["dest"] is not None:
                                wait_full(act, "T", st["name"], t - 2)
                            else:
                                act.wait_ge(out_stored[t % 2], 16 * (t // 2))
                        own(act.activation(xn[:, t % 2, :], hin[:, b, :], ACT.Square, accum_out=ss[:, t % 4:t % 4 + 1]))
                        if t >= 4:
                            act.wait_ge(xn_done, st["first"] + t - 3)
                        act.activation(rt[:, t % 4:t % 4 + 1], ss[:, t % 4:t % 4 + 1], ACT.Sqrt, bias=eps[:, :], scale=1.0 / D).then_inc(pre_root, 1)
                    t = s - 2
                    if t >= 0:
                        if st["dest"] is not None:
                            wait_full(act, "T", st["name"], t)
                            act.activation(st["dest"][0][:, :, t * P:t * P + P],
                                           slot("T", st["name"], t)[:, :].rearrange("p (k c) -> p k c", k=KT), ACT.Copy).then_inc(tr_hi, 1)
                        else:
                            act.wait_ge(xn_done, st["first"] + t + 1)
                            act.dma_start(out_t[t], xn[:, t % 2, :]).then_inc(out_stored[t % 2], 16)
                    if s + 1 < n:
                        load_h(st, s + 1)
                if st["dst"] is not None:
                    for t in range(n - 3, n):
                        act.wait_ge(h_stored[t % 3], 16 * st["store"][t])

            def copy_out(dst, src, key, scale=1.0):
                wait_full(act, *key)
                freed(act.activation(dst, src, ACT.Copy, scale=scale), *key)

            def first_half(name, Y):
                for t in range(NT):
                    copy_out(Y[:, t, 0:HALF], slot(name, 0, t)[:, 0:HALF], (name, 0, t))

            cw, cb = a["conv_w_2"][0], a["conv_b_2"][0]
            params = [(rowA[0:44, :], cw[0].rearrange("(r c) -> r c", c=P)), (rowA[44:88, :], cw[1].rearrange("(r c) -> r c", c=P)),
                      (rowA[88:92, :], a["pool_scale"][0].rearrange("(r c) -> r c", c=P)), (rowA[92:93, :], a["subln_g"]),
                      (rowA[93:94, :], a["gla_gain_2"]), (rowA[94:96, :], a["b_alpha_2"][0].rearrange("(r c) -> r c", c=P)),
                      (rowB[0:44, :], cw[2].rearrange("(r c) -> r c", c=P)), (rowB[44:88, :], cb.rearrange("(r c) -> r c", c=P)),
                      (mixw[:, :, :], a["pool_mix"][0].rearrange("g c d -> c g d")),
                      (walpha[:, :, :], a["w_alpha_2"][0].rearrange("r (h c) -> r h c", c=P)),
                      (sink[:, :], a["sinks_2"][0].partition_broadcast(P))]
            params += [(lamr[:, n, :], a[x][0].partition_broadcast(P)) for n, x in enumerate(("lam_q1", "lam_k1", "lam_q2", "lam_k2"))]
            assert len(params) == N_PARAMS
            begin_stage(stages["x"])
            for dst, src in params:
                act.dma_start(dst, src).then_inc(params_in, 16)
            for s in m_stored:
                act.sem_inc(s, 16)
            act.sem_inc(hid_lo, 2)
            act.wait_ge(consts_made, 3)
            wait_full(act, "cols")
            act.activation(colA[:, :], slot("cols")[:, 0:96], ACT.Copy).then_inc(cols_in, 1)
            freed(act.activation(colB[:, :], slot("cols")[:, HALF:HALF + 88], ACT.Copy), "cols")
            run_stage(stages["x"])
            act.wait_ge(lam_sum, 2)
            act.activation(lame[:, :], lam2[:, :], ACT.Exp).then_inc(lam_exp, 1)
            for c in range(4):
                copy_out(pT[:, c, :], slot("p", c)[:, :], ("p", c))
            for c in range(4):
                copy_out(qT[:, c, :], slot("q", c)[:, :], ("q", c), scale=0.125)
            act.wait_ge(cols_in, 1)
            for g in range(4):
                wait_full(act, "pool", g)
                act.activation(poolhi[:, g, :], slot("pool", g)[:, :], ACT.Copy, scale=colA[:, 88 + g:89 + g]).then_inc(pool_hi, 1)

            with act.Fori(0, 4) as i:
                for d in range(2):
                    wait_full(act, "gate", "a", d, i=i)
                    act.wait_ge(free[plan.slot(("y", "a", d))], plan.uses(("y", "a", d), i))
                    freed(act.activation(sgA[:, d, :], slot("gate", "a", d)[:, :], ACT.Sigmoid), "gate", "a", d)
                    wait_freed(act, "y", "a", d, i=i)
                    act.dma_start(m_dram[bass.ds(i * 256 + d * P, P), :], mst[:, d, :]).then_inc(m_stored[d], 16)
            for c in range(4):
                copy_out(kTt[:, c, :], slot("k", c)[:, :], ("k", c))
            for t in range(NT):
                copy_out(vt[:, t, :], slot("v", t)[:, 0:HALF], ("v", t))
            for d in range(2):
                act.wait_ge(m_stored[d], 16 * 5)
            for u in range(-1, len(UNITS)):
                if u + 1 < len(UNITS):
                    n = u + 1
                    w = P * (UNITS[n][1] + 1)
                    for m in range(2):
                        act.wait_ge(neg_max, 2 * n + m + 1)
                        if n >= 2:
                            act.wait_ge(a_done, n - 1)
                        act.activation(pp[:, n % 2, m, 0:w], pp[:, n % 2, m, 0:w], ACT.Exp, bias=nmax[:, n % 2, m:m + 1],
                                       accum_out=lsum[:, n % 2, m:m + 1]).then_inc(p_exp, 1)
                if u >= 0:
                    h, i = UNITS[u]
                    w = P * (i + 1)
                    if u >= 2:
                        wait_full(act, "pv", u - 2)
                    copy_out(aT[:, u % 2, 0:w], slot("aT", u)[:, 0:w], ("aT", u))
                    wait_full(act, "pv", u)
                    own(act.activation(junk[:, u % 2, :], slot("pv", u)[:, 0:P], ACT.Square, accum_out=ssA[:, u:u + 1]))
                    freed(act.activation(qT[:, h, i * P:i * P + P], slot("pv", u)[:, 0:P], ACT.Copy), "pv", u)
            act.dma_start(M[:, :, :], m_dram.rearrange("(k p) n -> p k n", p=P)).then_inc(m_loaded, 16)
            act.activation(rtA[:, :], ssA[:, :], ACT.Sqrt, bias=eps[:, :], scale=1.0 / P).then_inc(o_root, 1)
            for h in range(4):
                wait_full(act, "oT", h)
                act.activation(oThi[:, h, :], slot("oT", h)[:, :], ACT.Copy, scale=colA[:, 92:93]).then_inc(o_hi, 1)
            with act.Fori(0, 4) as i:
                for d in range(2):
                    wait_full(act, "gate", "b", d, i=i)
                    act.wait_ge(free[plan.slot(("y", "b", d))], plan.uses(("y", "b", d), i))
                    freed(act.activation(sgB[:, d, :], slot("gate", "b", d)[:, :], ACT.Sigmoid), "gate", "b", d)
            act.wait_ge(m_final, 1)
            begin_stage(stages["mix1"])
            for k in range(KT):
                act.activation(Uhi[:, k, :], M[:, k, :], ACT.Copy).then_inc(m_hi, 1)
            act.wait_ge(m_lo, KT)
            first_half("w_out", yM)
            run_stage(stages["mix1"], ("w_out", 1))

            def hidden_hi(name, c, i):
                if name == "f1":
                    wait_freed(act, "f1", "u", c, i=i)
                else:
                    act.wait_ge(hid_prod, i * 2 + c + 1)
                act.wait_ge(full[plan.slot((name, "d", 7))], plan.uses((name, "d", 7), i) - 2)
                act.activation(Hhi[:, c, :], hg[:, c, :], ACT.Copy).then_inc(hid_hi, 1)

            with act.Fori(0, FC // 2) as i:
                for c in range(2):
                    wait_full(act, "f1", "g", c, i=i)
                    act.wait_ge(hid_lo, i * 2 + hid_base["f1"] + c - 1)
                    freed(act.activation(hg[:, c, :], slot("f1", "g", c)[:, :], ACT.Silu), "f1", "g", c)
                    hidden_hi("f1", c, i)
            act.wait_ge(hid_lo, hid_base["f1"] + FC)
            begin_stage(stages["ffn1"])
            run_stage(stages["ffn1"])
            copy_out(aL[:, :], slot("ga")[0:16, :], ("ga",))
            copy_out(sk[:, :], slot("sk")[:, :], ("sk",))
            copy_out(sv[:, :, :], slot("sv")[:, :].rearrange("p (t c) -> p t c", c=P), ("sv",))
            for c in range(4):
                copy_out((gq, gq, gk, gk)[c][:, c % 2, :], slot("gqk", c)[:, :], ("gqk", c), scale=0.125 if c < 2 else 1.0)
            act.wait_ge(g_abs, 1)
            own(act.activation(gt[:, :, :], gt[:, :, :], ACT.Exp, scale=-1.0))
            act.activation(gt[:, :, :], gt[:, :, :], ACT.Ln, bias=1.0).then_inc(g_ln, 1)
            act.wait_ge(g_cum, 1)
            act.activation(gx[:, :, :], gt[:, :, :], ACT.Exp, scale=1.0 / 16).then_inc(g_e1, 1)
            act.wait_ge(g_d, 1)
            act.activation(gx[:, :, :], gx[:, :, :], ACT.Exp, scale=1.0 / 16).then_inc(g_e2, 1)
            act.wait_ge(k_end, 1)
            act.activation(decay[:, :, :], gt[:, :, 63::64], ACT.Exp, scale=1.0 / 16).then_inc(g_e3, 1)
            act.activation(gx[:, :, :], gt[:, :, :], ACT.Exp, scale=-1.0 / 16).then_inc(g_e3, 1)
            for c in range(4):
                copy_out(sq[:, c, :], slot("sq", c)[:, :], ("sq", c), scale=0.125)
            for c in range(4):
                wait_full(act, "r", c)
                freed(act.activation(rT[:, c, :], slot("r", c)[:, :], ACT.Silu), "r", c)
            act.wait_ge(q_dec, 1)
            for t in range(NT):
                copy_out(gv[:, t, :], slot("gv", t)[:, 0:HALF], ("gv", t))
            for j in range(2):
                copy_out(kendt[:, 4 * j:4 * j + 4, :], slot("kendT", j)[:, :].rearrange("p (t c) -> p t c", t=4), ("kendT", j))
            act.dma_start(sw[0:64, :], sk[64:128, :]).then_inc(keys_swapped, 16)
            act.dma_start(sw[64:128, :], sk[0:64, :]).then_inc(keys_swapped, 16)
            act.dma_start(relT[:, :], a["rel_bias_2"].rearrange("b h -> h b"), allow_slow_non_contiguous=True).then_inc(line_in, 16)
            act.wait_ge(line_ok, 1)
            act.dma_start(line_dram.rearrange("q h j -> h q j"), line[:, :].unsqueeze(1).to_broadcast([8, P, 384])).then_inc(line_in, 16)
            act.wait_ge(line_in, 32)
            act.dma_start(bias[:, :, :], bass.AP(tensor=line_dram.tensor, offset=P - 1, ap=[[8 * 384 - 1, P], [384, 8], [1, 256]])).then_inc(bias_in, 16)
            for t in range(NT):
                wait_full(act, "go", t)
                for h in range(4):
                    c = (h % 2) * HALF + (h // 2) * P
                    own(act.activation(gj[:, :], slot("go", t)[:, c:c + P], ACT.Square, accum_out=ssA[:, 4 * t + h:4 * t + h + 1]))
                act.activation(rtA[:, 4 * t:4 * t + 4], ssA[:, 4 * t:4 * t + 4], ACT.Sqrt, bias=eps[:, :], scale=1.0 / P).then_inc(g_ss, 1)
            for t in range(-1, NT):
                if t + 1 < NT:
                    n = t + 1
                    c0 = P if n == 0 else 0
                    act.wait_ge(s_max, n + 1)
                    for h in range(8):
                        act.activation(sS[:, n % 2, h, c0:256], sS[:, n % 2, h, c0:256], ACT.Exp, bias=smax[:, n % 2, h:h + 1],
                                       accum_out=lsum[:, n % 2, h:h + 1]).then_inc(s_exp, 1)
                    act.wait_ge(s_shift, n + 1)
                    act.activation(sexp[:, n % 2, :], sexp[:, n % 2, :], ACT.Exp).then_inc(s_sexp, 1)
                if t >= 0:
                    k0 = 1 if t == 0 else 0
                    if t >= 1:
                        wait_full(act, "so", t - 1)
                    for g in range(2):
                        copy_out(pTs[:, 4 * g:4 * g + 4, k0:2, :],
                                 slot("spT", t, g)[:, :].rearrange("p (h k c) -> p h k c", h=4, k=2)[:, :, k0:2, :], ("spT", t, g))
            for t in range(NT):
                act.wait_ge(mix_t, t + 1)
                wait_full(act, "mixT", t)
                act.activation(Uhi[:, 0:4, t * P:t * P + P], mixt[:, t % 2, :, :], ACT.Copy).then_inc(mix_hi, 1)
                act.activation(Uhi[:, 4:8, t * P:t * P + P], slot("mixT", t)[:, HALF:D].rearrange("p (k c) -> p k c", k=4), ACT.Copy).then_inc(mix_hi, 1)
            wait_freed(act, "mixT", NT - 1)
            begin_stage(stages["mem"])
            first_half("w_out2", y3)
            run_stage(stages["mem"])
            begin_stage(stages["mix2"])
            run_stage(stages["mix2"], ("w_out2", 1))
            for cb in range(2):
                copy_out(kC[:, 4 * cb:4 * cb + 4, :], slot("wk", cb)[:, :].rearrange("p (c n) -> p c n", c=4), ("wk", cb))
            for cb in range(2):
                copy_out(vC[:, :, cb * HALF:cb * HALF + HALF], slot("wv", cb)[:, :].rearrange("p (t n) -> p t n", t=2), ("wv", cb))
            for cb in range(2):
                for c in range(4):
                    copy_out(qC[:, 4 * cb + c, :], slot("wq", cb, c)[:, :], ("wq", cb, c), scale=0.0625)
            for u in range(-1, len(CU)):
                if u + 1 < len(CU):
                    n = u + 1
                    act.wait_ge(c_max, n + 1)
                    if n >= 2:
                        wait_full(act, "cT", n - 2)
                        act.wait_ge(c_norm, n - 1)
                    for j in range(4):
                        act.activation(pC[:, n % 2, j, :], slot("cs", n)[:, j * MEM:j * MEM + MEM], ACT.Exp, bias=nmax[:, n % 2, j:j + 1],
                                       accum_out=lsum[:, n % 2, j:j + 1]).then_inc(c_exp, 1)
                if u >= 0:
                    hf, h = CU[u]
                    if u >= 2:
                        wait_full(act, "co", u - 2)
                    copy_out(pTC[:, u % 2, :, :], slot("cT", u)[:, :].rearrange("p (k n) -> p k n", k=2), ("cT", u))
                    wait_full(act, "co", u)
                    act.activation(Uhi[:, 2 * h:2 * h + 2, hf * HALF:hf * HALF + HALF],
                                   slot("co", u)[:, :].rearrange("p (k n) -> p k n", k=2), ACT.Copy).then_inc(c_hi, 1)
            begin_stage(stages["cross"])
            first_half("w_o", y4)
            run_stage(stages["cross"], ("w_o", 1))
            with act.Fori(0, FC // 2) as i:
                for c in range(2):
                    act.wait_ge(conv_done, i * 2 + c + 1)
                    act.activation(hg[:, c, :], hg[:, c, :], ACT.Silu).then_inc(act_done, 1)
                    hidden_hi("f2", c, i)
            act.wait_ge(hid_lo, hid_base["f2"] + FC)
            begin_stage(stages["ffn2"])
            run_stage(stages["ffn2"])
            for n in range(2):
                act.wait_ge(out_stored[n], 16 * (NT // 2))

        @block.vector
        def _(dve):
            own = Chain(dve, dve_own)

            def tt(o, x, y, op):
                return dve.tensor_tensor(o, x, y, op)

            def stt(o, x, s, y, op0, op1):
                return dve.scalar_tensor_tensor(out=o, in0=x, scalar=s, in1=y, op0=op0, op1=op1)

            def lo_of(dst, src, hi, key):
                freed(tt(dst, src, hi.bitcast(f32), ALU.subtract), *key)

            def run_stage(st, mm=None):
                n, hin, xn, Y = st["n"], st["hin"], st["xn"], st["Y"]
                dve.wait_ge(gains_in, 16 * st["gains"])
                for s in range(n + 2):
                    if s < n and st["kind"] != "load":
                        b = s % 3
                        if st["kind"] == "post":
                            dve.wait_ge(post_root, st["posts"] + s + 1)
                            own(dve.reciprocal(rsp[:, s % 4:s % 4 + 1], rtp[:, s % 4:s % 4 + 1]))
                            own(stt(Y[:, s, :], Y[:, s, :], rsp[:, s % 4:s % 4 + 1], st["gpost"][:, :], ALU.mult, ALU.mult))
                            dve.wait_ge(h_loaded[b], 16 * st["load"][s])
                            tt(hin[:, b, :], hin[:, b, :], Y[:, s, :], ALU.add).then_inc(h_new, 1)
                        elif st["fused"]:
                            dve.wait_ge(h_loaded[b], 16 * st["load"][s])
                            wait_full(dve, *mm, s)
                            freed(tt(hin[:, b, HALF:D], hin[:, b, HALF:D], slot(*mm, s)[:, 0:HALF], ALU.add), *mm, s)
                            wait_freed(dve, *mm, s)
                            wait_freed(dve, mm[0], 0, s)
                            tt(hin[:, b, 0:HALF], hin[:, b, 0:HALF], Y[:, s, :], ALU.add).then_inc(h_new, 1)
                        else:
                            wait_freed(dve, "f2", "d", s, i=FC // 2 - 1)
                            dve.wait_ge(h_loaded[b], 16 * st["load"][s])
                            tt(hin[:, b, :], hin[:, b, :], Y[:, s, :], ALU.add).then_inc(h_new, 1)
                    t = s - 1
                    if 0 <= t < n:
                        b = t % 3
                        dve.wait_ge(pre_root, st["first"] + t + 1)
                        own(dve.reciprocal(rs[:, t % 4:t % 4 + 1], rt[:, t % 4:t % 4 + 1]))
                        stt(xn[:, t % 2, :], hin[:, b, :], rs[:, t % 4:t % 4 + 1], st["gpre"][:, :], ALU.mult, ALU.mult).then_inc(xn_done, 1)
                    t = s - 2
                    if t >= 0 and st["dest"] is not None:
                        hi, lo = st["dest"]
                        dve.wait_ge(tr_hi, st["turns"] + t + 1)
                        lo_of(lo[:, :, t * P:t * P + P], slot("T", st["name"], t)[:, :].rearrange("p (k c) -> p k c", k=KT),
                              hi[:, :, t * P:t * P + P], ("T", st["name"], t))

            dve.wait_ge(params_in, 16 * N_PARAMS)
            for m in range(2):
                dve.tensor_tensor_reduce(out=lamj[:, m, :], in0=lamr[:, 2 * m, :], in1=lamr[:, 2 * m + 1, :], scale=1.0, scalar=0.0,
                                         op0=ALU.mult, op1=ALU.add, accum_out=lam2[:, m:m + 1]).then_inc(lam_sum, 1)
            dve.wait_ge(pool_own, 4)
            own(dve.reciprocal(cnt[:, :], cnt[:, :]))
            run_stage(stages["x"])
            dve.wait_ge(lam_exp, 1)
            own(tt(nlam[:, :], lame[:, 1:2], lame[:, 0:1], ALU.subtract))
            own(dve.tensor_scalar(nlam[:, :], nlam[:, :], -LAMBDA_INIT, None, ALU.add))
            dve.wait_ge(cols_in, 1)
            own(dve.tensor_scalar(colA[:, 92:93], colA[:, 92:93], 1.0 - LAMBDA_INIT, None, ALU.mult))
            for g in range(4):
                w = 2 << g
                wait_freed(dve, "p", g)
                src = pT
                for j in range(g + 1):
                    sh = 1 << j
                    dst = pS if j % 2 == 0 else pX
                    s_ap = pT[:, g, :] if j == 0 else (pS[:, g, :] if j % 2 == 1 else pX[:, :])
                    d_ap = pS[:, g, :] if j % 2 == 0 else pX[:, :]
                    own(dve.tensor_copy(d_ap[:, 0:sh], s_ap[:, 0:sh]))
                    own(tt(d_ap[:, sh:SEQ], s_ap[:, sh:SEQ], s_ap[:, 0:SEQ - sh], ALU.add))
                last = pS[:, g, :] if g % 2 == 0 else pX[:, :]
                own(tt(last[:, 0:w - 1], last[:, 0:w - 1], cnt[:, 0:w - 1], ALU.mult))
                own(dve.tensor_scalar(last[:, w - 1:SEQ], last[:, w - 1:SEQ], 1.0 / w, None, ALU.mult))
                tt(pS[:, g, :], last, pT[:, g, :], ALU.subtract).then_inc(pool_ready, 1)
                dve.wait_ge(pool_ready, g + 1)
            for g in range(4):
                dve.wait_ge(pool_hi, g + 1)
                freed(stt(poollo[:, g, :], slot("pool", g)[:, :], colA[:, 88 + g:89 + g], poolhi[:, g, :].bitcast(f32),
                          ALU.mult, ALU.subtract), "pool", g)
            with dve.Fori(0, 4) as i:
                for d in range(2):
                    wait_freed(dve, "gate", "a", d, i=i)
                    wait_full(dve, "y", "a", d, i=i)
                    dve.wait_ge(m_stored[d], i * 16 + 16)
                    freed(tt(mst[:, d, :], sgA[:, d, :], slot("y", "a", d)[:, :], ALU.mult), "y", "a", d)
            for d in range(2):
                dve.wait_ge(m_stored[d], 16 * 5)
            dve.wait_ge(dist_made, 1)

            def scores(u):
                h, i = UNITS[u]
                w = P * (i + 1)
                c0 = SEQ - w
                for m in range(2):
                    wait_full(dve, "sc", u, m)
                    if u >= 2:
                        wait_full(dve, "aT", u - 2)
                    freed(stt(pp[:, u % 2, m, 0:w], dist[:, c0:SEQ], 2.0 ** (-2 * (h + 1)), slot("sc", u, m)[:, 0:w], ALU.mult, ALU.add),
                          "sc", u, m)
                    wait_freed(dve, "sc", u, m)
                    dve.tensor_reduce(nmax[:, u % 2, m:m + 1], pp[:, u % 2, m, 0:w], axis=AX.X, op=ALU.max, negate=True).then_inc(neg_max, 1)

            scores(0)
            for u in range(len(UNITS)):
                if u + 1 < len(UNITS):
                    scores(u + 1)
                w = P * (UNITS[u][1] + 1)
                b = u % 2
                dve.wait_ge(p_exp, 2 * u + 2)
                own(dve.reciprocal(rsum[:, b, 0:2], lsum[:, b, 0:2]))
                own(tt(c2[:, b, 0:1], rsum[:, b, 1:2], nlam[:, :], ALU.mult))
                own(dve.tensor_scalar(pp[:, b, 1, 0:w], pp[:, b, 1, 0:w], c2[:, b, 0:1], None, ALU.mult))
                stt(pp[:, b, 0, 0:w], pp[:, b, 0, 0:w], rsum[:, b, 0:1], pp[:, b, 1, 0:w], ALU.mult, ALU.add).then_inc(a_done, 1)
            dve.wait_ge(o_root, 1)
            own(dve.reciprocal(rsA[:, :], rtA[:, :]))
            for h in range(4):
                v = qT[:, h, :].rearrange("p (i c) -> p i c", i=NT)
                tt(v, v, rsA[:, 8 * h:8 * h + 8].unsqueeze(2).to_broadcast([P, NT, P]), ALU.mult).then_inc(o_scaled, 1)
            for h in range(4):
                dve.wait_ge(o_hi, h + 1)
                freed(stt(oTlo[:, h, :], slot("oT", h)[:, :], colA[:, 92:93], oThi[:, h, :].bitcast(f32), ALU.mult, ALU.subtract), "oT", h)
            dve.wait_ge(m_loaded, 16)
            with dve.Fori(0, 4) as i:
                own.loop(i, 2)
                for d in range(2):
                    wait_freed(dve, "gate", "b", d, i=i)
                    wait_full(dve, "y", "b", d, i=i)
                    freed(tt(prB[:, d, :], sgB[:, d, :], slot("y", "b", d)[:, :], ALU.mult), "y", "b", d)
                    wait_freed(dve, "y", "b", d, i=i)
                    m = M[:, bass.ds(i * 2 + d, 1), :].rearrange("p o n -> p (o n)")
                    own(tt(m, m, prB[:, d, :], ALU.add))
            own.end(4)
            dve.sem_inc(m_final, 1)
            for k in range(KT):
                dve.wait_ge(m_hi, k + 1)
                tt(Ulo[:, k, :], M[:, k, :], Uhi[:, k, :].bitcast(f32), ALU.subtract).then_inc(m_lo, 1)
            run_stage(stages["mix1"], ("w_out", 1))

            def hidden_lo(name, c, i):
                dve.wait_ge(hid_hi, i * 2 + hi_base[name] + c + 1)
                tt(Hlo[:, c, :], hg[:, c, :], Hhi[:, c, :].bitcast(f32), ALU.subtract).then_inc(hid_lo, 1)

            def add_down(name, i):
                for t in range(NT):
                    wait_full(dve, name, "d", t, i=i)
                    freed(tt(acc[:, t, :], acc[:, t, :], slot(name, "d", t)[:, :], ALU.add), name, "d", t)

            def clear_acc(st, others=()):
                for t in range(NT - 2, NT):
                    wait_full(dve, "T", st["name"], t)
                for t in range(NT - 3, NT):
                    dve.wait_ge(h_stored[t % 3], 16 * st["store"][t])
                own(dve.memset(acc[:, :, :], 0.0))

            clear_acc(stages["mix1"])
            with dve.Fori(0, FC // 2) as i:
                for c in range(2):
                    wait_freed(dve, "f1", "g", c, i=i)
                    wait_full(dve, "f1", "u", c, i=i)
                    freed(tt(hg[:, c, :], hg[:, c, :], slot("f1", "u", c)[:, :], ALU.mult), "f1", "u", c)
                    hidden_lo("f1", c, i)
                add_down("f1", i)
            run_stage(stages["ffn1"])
            for hp in range(2):
                wait_full(dve, "alpha", hp)
                freed(dve.tensor_scalar(gx[:, hp, :], slot("alpha", hp)[:, :], colA[:, 94 + hp:95 + hp], None, ALU.add), "alpha", hp)
            wait_freed(dve, "alpha", 0)
            wait_freed(dve, "alpha", 1)
            stt(gt[:, :, :], gx[:, :, :], -1.0, gx[:, :, :], ALU.mult, ALU.max).then_inc(g_abs, 1)
            own(dve.memset(reset[:, :], 1.0))
            own(dve.memset(reset[:, 0::64], 0.0))
            dve.wait_ge(g_ln, 1)
            own(stt(gx[:, :, :], gx[:, :, :], 0.0, gt[:, :, :], ALU.min, ALU.subtract))
            own(dve.tensor_tensor_scan(gt[:, 0, :], reset[:, :], gx[:, 0, :], 0.0, ALU.mult, ALU.add))
            own(dve.tensor_tensor_scan(gt[:, 1, :], reset[:, :], gx[:, 1, :], 0.0, ALU.mult, ALU.add))
            dve.sem_inc(g_cum, 1)
            for c in range(4):
                wait_freed(dve, "gqk", c)
            dve.wait_ge(g_e1, 1)
            own(tt(gq[:, :, :], gq[:, :, :], gx[:, :, :], ALU.mult))
            for hp in range(2):
                last = gt[:, hp, 63::64].unsqueeze(2).to_broadcast([P, 16, 64])
                own(tt(gx[:, hp, :].rearrange("p (n c) -> p n c", c=64), last, gt[:, hp, :].rearrange("p (n c) -> p n c", c=64), ALU.subtract))
            dve.sem_inc(g_d, 1)
            dve.wait_ge(g_e2, 1)
            tt(kend[:, :, :], gk[:, :, :], gx[:, :, :], ALU.mult).then_inc(k_end, 1)
            dve.wait_ge(g_e3, 2)
            dve.wait_ge(k_end, 1)
            tt(gk[:, :, :], gk[:, :, :], gx[:, :, :], ALU.mult).then_inc(q_dec, 1)
            def kv_ap(n, hp):
                t, par = n // 2, n % 2
                return slot("kv", t // 2)[:, par * HALF + (t % 2) * 256 + hp * P:par * HALF + (t % 2) * 256 + hp * P + P]

            wait_full(dve, "kv", 0)
            own(dve.memset(line[:, :], NEG))
            dve.wait_ge(line_in, 16)
            ranges = t5_ranges(P)
            for n, (bk, d0, d1) in enumerate(ranges):
                own(dve.tensor_copy(line[:, 256 - d1:256 - d0], relT[:, bk:bk + 1].to_broadcast([8, d1 - d0])))
            dve.sem_inc(line_ok, 1)
            for n in range(15):
                if n % 4 == 0:
                    wait_full(dve, "kv", n // 4)
                if n == 0:
                    o = slot("kv", 0)[:, 0:256].rearrange("p (h c) -> p h c", h=2)
                    dve.tensor_copy(S[:, 1, :, :], o).then_inc(states, 1)
                else:
                    dve.wait_ge(states, n)
                    own(stt(S[:, n + 1, 0, :], S[:, n, 0, :], decay[:, 0, n:n + 1], kv_ap(n, 0), ALU.mult, ALU.add))
                    stt(S[:, n + 1, 1, :], S[:, n, 1, :], decay[:, 1, n:n + 1], kv_ap(n, 1), ALU.mult, ALU.add).then_inc(states, 1)
                if n % 4 == 3 or n == 14:
                    dve.wait_ge(states, n + 1)
                    dve.sem_inc(free[plan.slot(("kv", n // 4))], 1)
            for b in range(2):
                dve.memset(attS[:, b, :, :], 0.0).then_inc(att_ok, 1)
            dve.wait_ge(att_ok, 2)
            mask = causal[:, :].bitcast(u32).unsqueeze(1).to_broadcast([P, 2, P])

            def masked(t):
                wait_full(dve, "att", t)
                if t >= 2:
                    wait_full(dve, "go", t - 2)
                for hh in range(2):
                    src = slot("att", t)[:, hh * HALF:hh * HALF + 256].rearrange("p (h c) -> p h c", h=2)
                    ins = dve.copy_predicated(attS[:, t % 2, hh::2, :], mask, src)
                    if hh == 0:
                        own(ins)
                    else:
                        ins.then_inc(att_ok, 1)
                dve.wait_ge(att_ok, 2 + t + 1)
                dve.sem_inc(free[plan.slot(("att", t))], 1)

            masked(0)
            for t in range(NT):
                if t + 1 < NT:
                    masked(t + 1)
                dve.wait_ge(g_ss, t + 1)
                own(dve.reciprocal(rsA[:, 4 * t:4 * t + 4], rtA[:, 4 * t:4 * t + 4]))
                for hh in range(2):
                    src = slot("go", t)[:, hh * HALF:hh * HALF + 256].rearrange("p (h c) -> p h c", h=2)
                    dst = gv[:, t, :].rearrange("p (h c) -> p h c", h=4)[:, hh::2, :]
                    ins = tt(dst, src, rsA[:, 4 * t + hh:4 * t + 4:2].unsqueeze(2).to_broadcast([P, 2, P]), ALU.mult)
                    if hh == 0:
                        own(ins)
                    else:
                        ins.then_inc(g_out, 1)
                dve.wait_ge(g_out, t + 1)
                dve.sem_inc(free[plan.slot(("go", t))], 1)
            dve.wait_ge(bias_in, 16)

            def windowed(n):
                b, c0 = n % 2, P if n == 0 else 0
                for g in range(2):
                    wait_full(dve, "ssc", n, g)
                    if n >= 2:
                        wait_full(dve, "spT", n - 2, g)
                    src = slot("ssc", n, g)[:, :].rearrange("p (h c k) -> p h c k", h=2, c=2)[:, :, :, c0:256]
                    dst, bs = (x.rearrange("p (c h) k -> p h c k", h=2)[:, :, :, c0:256] for x in (sS[:, b, 4 * g:4 * g + 4, :], bias[:, 4 * g:4 * g + 4, :]))
                    freed(tt(dst, src, bs, ALU.add), "ssc", n, g)
                wait_freed(dve, "ssc", n, 0)
                wait_freed(dve, "ssc", n, 1)
                own(dve.tensor_reduce(smax[:, b, :], sS[:, b, :, c0:256], axis=AX.X, op=ALU.max))
                own(tt(smax[:, b, :], smax[:, b, :], sink[:, :], ALU.max))
                tt(sexp[:, b, :], sink[:, :], smax[:, b, :], ALU.subtract).then_inc(s_shift, 1)
                dve.wait_ge(s_shift, n + 1)
                dve.tensor_scalar(smax[:, b, :], smax[:, b, :], -1.0, None, ALU.mult).then_inc(s_max, 1)

            windowed(0)
            for t in range(NT):
                if t + 1 < NT:
                    windowed(t + 1)
                b = t % 2
                dve.wait_ge(s_exp, 8 * (t + 1))
                dve.wait_ge(s_sexp, t + 1)
                own(tt(lsum[:, b, :], lsum[:, b, :], sexp[:, b, :], ALU.add))
                own(dve.reciprocal(rsum[:, b, :], lsum[:, b, :]))
                wait_full(dve, "so", t)
                freed(tt(Os[:, t, :].rearrange("p (h c) -> p h c", h=8), slot("so", t)[:, 0:HALF].rearrange("p (h c) -> p h c", h=8),
                         rsum[:, b, :].unsqueeze(2).to_broadcast([P, 8, 64]), ALU.mult), "so", t)
            for t in range(NT):
                wait_full(dve, "mixT", t)
                if t >= 2:
                    dve.wait_ge(mix_hi, 2 * t - 2)
                ts = slice(t * P, t * P + P)
                stt(mixt[:, t % 2, :, :], slot("mixT", t)[:, 0:HALF].rearrange("p (k c) -> p k c", k=4), colA[:, 93:94],
                    rT[:, :, ts], ALU.mult, ALU.mult).then_inc(mix_t, 1)
                dve.wait_ge(mix_t, t + 1)
                dve.wait_ge(mix_hi, 2 * t + 1)
                own(tt(Ulo[:, 0:4, ts], mixt[:, t % 2, :, :], Uhi[:, 0:4, ts].bitcast(f32), ALU.subtract))
                dve.wait_ge(mix_hi, 2 * t + 2)
                lo_of(Ulo[:, 4:8, ts], slot("mixT", t)[:, HALF:D].rearrange("p (k c) -> p k c", k=4), Uhi[:, 4:8, ts], ("mixT", t))
            run_stage(stages["mem"])
            run_stage(stages["mix2"], ("w_out2", 1))

            def cross_max(n):
                wait_full(dve, "cs", n)
                dve.tensor_reduce(nmax[:, n % 2, 0:4], slot("cs", n)[:, :].rearrange("p (j c) -> p j c", j=4), axis=AX.X, op=ALU.max,
                                  negate=True).then_inc(c_max, 1)

            cross_max(0)
            for u in range(len(CU)):
                hf, h = CU[u]
                b = u % 2
                dve.wait_ge(c_exp, 4 * (u + 1))
                dve.sem_inc(free[plan.slot(("cs", u))], 1)
                if u + 1 < len(CU):
                    cross_max(u + 1)
                own(dve.reciprocal(rsum[:, b, 0:4], lsum[:, b, 0:4]))
                tt(pC[:, b, :, :], pC[:, b, :, :], rsum[:, b, 0:4].unsqueeze(2).to_broadcast([P, 4, MEM]), ALU.mult).then_inc(c_norm, 1)
                dve.wait_ge(c_hi, u + 1)
                lo_of(Ulo[:, 2 * h:2 * h + 2, hf * HALF:hf * HALF + HALF], slot("co", u)[:, :].rearrange("p (k n) -> p k n", k=2),
                      Uhi[:, 2 * h:2 * h + 2, hf * HALF:hf * HALF + HALF], ("co", u))
            run_stage(stages["cross"], ("w_o", 1))
            clear_acc(stages["cross"])

            with dve.Fori(0, FC // 2) as i:
                own.loop(i, 10)
                for c in range(2):
                    for part, dst, j0 in (("g", hg, 0), ("u", hv, FC)):
                        o = slot("f2", part, c)
                        col = i * 2 + (j0 + c)
                        wait_full(dve, "f2", part, c, i=i)
                        if part == "g":
                            dve.wait_ge(hid_lo, i * 2 + hid_base["f2"] + c - 1)
                        own(dve.tensor_scalar(dst[:, c, :], o[:, :], colB[:, bass.ds(col, 1)], colB[:, bass.ds(col + 44, 1)], ALU.mult, ALU.add))
                        own(stt(dst[:, c, 1:SEQ], o[:, 0:SEQ - 1], colA[:, bass.ds(col + 44, 1)], dst[:, c, 1:SEQ], ALU.mult, ALU.add))
                        freed(stt(dst[:, c, 2:SEQ], o[:, 0:SEQ - 2], colA[:, bass.ds(col, 1)], dst[:, c, 2:SEQ], ALU.mult, ALU.add), "f2", part, c)
                        wait_freed(dve, "f2", part, c, i=i)
                        if part == "g":
                            dve.sem_inc(conv_done, 1)
                    dve.wait_ge(act_done, i * 2 + c + 1)
                    own(tt(hg[:, c, :], hg[:, c, :], hv[:, c, :], ALU.mult))
                    dve.sem_inc(hid_prod, 1)
                    hidden_lo("f2", c, i)
                add_down("f2", i)
            own.end(FC // 2)
            run_stage(stages["ffn2"])


_INS = ['x', 'w_in', 'pool_mix', 'pool_scale', 'w_branch_a', 'lam_q1', 'lam_k1', 'lam_q2', 'lam_k2', 'subln_g',
        'w_branch_b', 'w_out', 'mix_pre_g', 'mix_post_g', 'ffn_pre_g', 'ffn_post_g', 'w_ffn_gate', 'w_ffn_up',
        'w_ffn_down', 'mem_2', 'norm_mix_2', 'w_in_2', 'w_alpha_2', 'b_alpha_2', 'gla_gain_2', 'rel_bias_2',
        'sinks_2', 'w_out_2', 'norm_cross_2', 'norm_mem_2', 'w_q_c_2', 'w_k_c_2', 'w_v_c_2', 'w_o_c_2', 'norm_ffn_2',
        'w_up_2', 'conv_w_2', 'conv_b_2', 'w_down_2', 'norm_final_2']


def kernel(**inputs):
    import numpy as _np
    import concourse.bacc as _bacc
    from concourse import mybir as _mybir
    from concourse.bass_utils import run_bass_kernel_spmd as _run

    nc = _bacc.Bacc("TRN2", target_bir_lowering=False, num_devices=1, dynamic_dma_scratch_size=1024)
    arrays, args = {}, {}
    for name in _INS:
        v = _np.ascontiguousarray(inputs[name])
        arrays[f"in_{name}"] = v
        args[name] = nc.dram_tensor(f"in_{name}", v.shape, _mybir.dt.from_np(v.dtype), kind="ExternalInput").ap()
    out = nc.dram_tensor("out_0", (1, SEQ, D), _mybir.dt.float32, kind="ExternalOutput").ap()
    build(nc, args, out)
    r = _run(nc, [arrays], core_ids=[0])
    return r.results[0]["out_0"]
```

```python
import math
from contextlib import ExitStack

import numpy as np
import concourse.bass as bass
from concourse import mybir

P = 128
SEQ = 1024
D = 1024
KT = D // P
NT = SEQ // P
HALF = 512
F = 2816
FC = F // P
EPS = 1e-6
MEM = 256
KB = 1024
BASE = 1152
RING = 144 * KB
CONST = RING + 72 * KB
NEG = -3.0e38
N_PARAMS = 15
LAMBDA_INIT = 0.8 - 0.6 * math.exp(-0.3 * 0)


class Plan:

    def __init__(self):
        self.groups, self.n, self.per, self.start = {}, 0, 0, 0
        self.blocks, self.b, self.pieces, self.bper, self.pper = {}, 0, 0, 0, 0
        self.stream, self.order, self.last, self.trip_of = [], [], {}, {}
        self.body = self.stream

    def group(self, *key):
        self.groups[key] = (self.n, self.per)
        self.n += 1

    def block(self, key, pieces):
        self.blocks[key] = (self.b, self.pieces, len(pieces), self.bper, self.pper)
        self.order.append((key, self.b))
        self.body.append((key, pieces))
        self.trip_of[key] = self.trips if self.bper else 1
        self.b += 1
        self.pieces += len(pieces)

    def loop(self, trips, groups, blocks, pieces):
        assert groups % 4 == 0 and blocks % 2 == 0 and pieces % 2 == 0
        self.per, self.bper, self.pper, self.trips = groups, blocks, pieces, trips
        self.marks = (self.n, self.b, self.pieces)
        self.body = []
        self.stream.append((trips, self.body))

    def end(self):
        n, b, p = self.marks
        assert (self.n - n, self.b - b, self.pieces - p) == (self.per, self.bper, self.pper)
        more = self.trips - 1
        self.n, self.b, self.pieces = self.n + more * self.per, self.b + more * self.bper, self.pieces + more * self.pper
        self.per = self.bper = self.pper = 0
        self.body = self.stream

    def reader(self, key):
        b, bper = self.blocks[key][0], self.blocks[key][3]
        if bper:
            return self.last[key], None
        for k, n in self.order:
            per = self.blocks[k][3]
            if (n == b - 2) or (per and b - 2 >= n and (b - 2 - n) % per == 0 and (b - 2 - n) // per < self.trip_of[k]):
                return self.last[k], (b - 2 - n) // per if per else 0
        return None

    def slot(self, key):
        return self.groups[key][0] % 4

    def uses(self, key, i=0):
        n, per = self.groups[key]
        return n // 4 + i * (per // 4) if per else n // 4


class Chain:

    def __init__(self, eng, sem):
        self.eng, self.sem, self.n, self.more = eng, sem, 0, 0

    def __call__(self, ins):
        self.n += 1
        ins.then_inc(self.sem, 1)
        self.eng.wait_ge(self.sem, self.more + self.n)

    def loop(self, i, per):
        self.start, self.per, self.more = self.n, per, i * per

    def end(self, trips):
        assert self.n - self.start == self.per, (self.n - self.start, self.per)
        self.n, self.more = self.start + trips * self.per, 0


def t5_ranges(window):
    out = []
    for dist in range(window):
        b = dist if dist < 16 else min(31, 16 + int(math.log(dist / 16) / math.log(128 / 16) * 16))
        if out and out[-1][0] == b:
            out[-1][2] = dist + 1
        else:
            out.append([b, dist, dist + 1])
    return out


def build(nc, a, out):
    f32, f32r, u32 = mybir.dt.float32, mybir.dt.float32r, mybir.dt.uint32
    ALU, ACT, AX = mybir.AluOpType, mybir.ActivationFunctionType, mybir.AxisListType
    ctx = ExitStack()

    def at(name, kb, shape, dt=f32):
        return nc.alloc_sbuf_tensor_at(name, shape, dt, offset=BASE + int(kb * KB))

    used = [CONST]

    def const(name, shape, dt=f32):
        t = nc.alloc_sbuf_tensor_at(name, shape, dt, offset=BASE + used[0])
        used[0] += (int(np.prod(shape[1:])) * 4 + 31) // 32 * 32
        assert BASE + used[0] <= 229344, used
        return t

    with ctx:
        def sem(name):
            return ctx.enter_context(nc.semaphore(name))

        Uhi, Ulo = at("Uhi", 0, [P, KT, SEQ], f32r), at("Ulo", 32, [P, KT, SEQ], f32r)
        Whi = nc.alloc_sbuf_tensor_at("Whi", [P, 2, 4096], f32r, offset=BASE + RING)
        Wlo = nc.alloc_sbuf_tensor_at("Wlo", [P, 2, 4096], f32r, offset=BASE + RING + 32 * KB)
        raw = nc.alloc_sbuf_tensor_at("raw", [P, 2, 1024], f32, offset=BASE + RING + 64 * KB)
        ident = const("ident", [P, P])
        colA, colB = const("colA", [P, 96]), const("colB", [P, 88])
        mixw = const("mixw", [P, 4, P])
        relT = nc.alloc_sbuf_tensor_at("relT", [8, 32], f32, offset=BASE + used[0] - 2048)
        line = nc.alloc_sbuf_tensor_at("line", [8, 384], f32, offset=BASE + used[0] - 1536)
        walpha = const("walpha", [16, 2, P])
        causal = const("causal", [P, P])
        eps = const("eps", [P, 1])
        tiny = const("tiny", [P, 2])
        cnt = const("cnt", [P, 16])
        lam2, nlam, lame = const("lam2", [P, 2]), const("nlam", [P, 1]), const("lame", [P, 2])
        ss, rt, rs = (const(x, [P, 4]) for x in ("ss", "rt", "rs"))
        ssp, rtp, rsp = (const(x, [P, 4]) for x in ("ssp", "rtp", "rsp"))
        ssA, rtA, rsA = (const(x, [P, 32]) for x in ("ssA", "rtA", "rsA"))
        nmax, lsum, rsum, c2 = (const(x, [P, 2, 8]) for x in ("nmax", "lsum", "rsum", "c2"))
        sink, smax, sexp = const("sink", [P, 8]), const("smax", [P, 2, 8]), const("sexp", [P, 2, 8])
        decay = const("decay", [P, 2, 16])
        rowA, rowB = at("rowA", 96, [96, P]), at("rowB", 96.5, [88, P])
        lamr, lamj = at("lamr", 97, [P, 4, 64]), at("lamj", 98, [P, 2, 64])
        pT, pS, pX = at("pT", 64, [P, 4, SEQ]), at("pS", 80, [P, 4, SEQ]), at("pX", 124, [P, SEQ])
        poolhi, poollo = at("poolhi", 96, [P, 4, SEQ], f32r), at("poollo", 112, [P, 4, SEQ], f32r)
        qT = at("qT", 128, [P, 4, SEQ])
        sgA, mst = at("sgA", 64, [P, 2, SEQ]), at("mst", 72, [P, 2, SEQ])
        kTt, vt = at("kTt", 96, [P, 4, SEQ]), at("vt", 112, [P, NT, 512])
        pp, aT, dist = at("pp", 64, [P, 3, 2, SEQ]), at("aT", 88, [P, SEQ]), at("dist", 92, [P, SEQ])
        oThi, oTlo = at("oThi", 96, [P, 4, SEQ], f32r), at("oTlo", 112, [P, 4, SEQ], f32r)
        M, sgB, prB = at("M", 64, [P, KT, SEQ]), at("sgB", 128, [P, 2, SEQ]), at("prB", 136, [P, 2, SEQ])
        Hhi, Hlo = at("Hhi", 64, [P, 2, SEQ], f32r), at("Hlo", 72, [P, 2, SEQ], f32r)
        hg, hv = at("hg", 80, [P, 2, SEQ]), at("hv", 88, [P, 2, SEQ])
        acc = at("acc", 96, [P, NT, D])
        gq, gk, gv = at("gq", 64, [P, 2, SEQ]), at("gk", 72, [P, 2, SEQ]), at("gv", 80, [P, NT, 512])
        gx, gt = at("gx", 80, [P, 2, SEQ]), at("gt", 88, [P, 2, SEQ])
        rT, sq, sk = at("rT", 96, [P, 4, SEQ]), at("sq", 112, [P, 4, SEQ]), at("sk", 128, [P, SEQ])
        sv, aL, reset, kend = at("sv", 132, [P, NT, P]), at("aL", 136, [16, SEQ]), at("reset", 140, [P, SEQ]), at("kend", 136, [P, 2, SEQ])
        kendt, S, attS = at("kendt", 0, [P, NT, 256]), at("S", 8, [P, 16, 2, P]), at("attS", 24, [P, 2, 4, P])
        bias, sS, pTs = at("bias", 32, [P, 8, 256]), at("sS", 40, [P, 2, 8, 256]), at("pTs", 56, [P, 8, 2, P])
        gj = at("gj", 31, [P, P])
        sw = at("sw", 140, [P, SEQ])
        mixt = at("mixt", 136, [P, 2, 4, P])
        memhi, memlo = at("memhi", 64, [P, KT, MEM], f32r), at("memlo", 72, [P, KT, MEM], f32r)
        kC, vC, qC = at("kC", 80, [P, KT, MEM]), at("vC", 88, [P, 2, D]), at("qC", 96, [P, KT, SEQ])
        pC, pTC = at("pC", 128, [P, 2, 4, MEM]), at("pTC", 136, [P, 2, 2, HALF])

        slots = [ctx.enter_context(nc.psum_tensor(f"slot{s}", [P, SEQ], f32)) for s in range(4)]
        hd = [nc.dram_tensor(f"h{n}", (SEQ, D), f32).ap() for n in range(4)]
        m_dram = nc.dram_tensor("m_part", (D, SEQ), f32).ap()
        line_dram = nc.dram_tensor("rel_line", (P, 8, 384), f32).ap()

        loaded = [sem(f"piece_loaded{n}") for n in range(2)]
        w_hi, w_split, raw_free, dist_made = sem("weight_hi"), sem("weight_split"), sem("raw_free"), sem("dist_made")
        full = [sem(f"slot_full{s}") for s in range(4)]
        free = [sem(f"slot_free{s}") for s in range(4)]
        act_own, dve_own, pool_own = sem("act_own"), sem("dve_own"), sem("pool_own")
        consts_made, params_in, cols_in = sem("consts_made"), sem("params_in"), sem("rows_turned")
        h_loaded = [sem(f"h_loaded{n}") for n in range(3)]
        h_stored = [sem(f"h_stored{n}") for n in range(3)]
        gains_in, post_root, h_new, pre_root, xn_done, tr_hi = (sem(x) for x in (
            "gains_in", "post_root", "h_new", "pre_root", "xn_done", "turned_hi"))
        out_stored = [sem(f"out_stored{n}") for n in range(2)]
        lam_sum, lam_exp, pool_ready, pool_hi = (sem(x) for x in ("lam_sum", "lam_exp", "pool_ready", "pool_hi"))
        m_stored, m_loaded, m_final, m_hi, m_lo = [sem("m_stored0"), sem("m_stored1")], sem("m_loaded"), sem("m_final"), sem("m_hi"), sem("m_lo")
        neg_max, p_exp, a_done, o_root, o_scaled, o_hi = (sem(x) for x in (
            "neg_max", "p_exp", "a_done", "o_root", "o_scaled", "o_hi"))
        conv_done, act_done, hid_prod, hid_hi, hid_lo = (sem(x) for x in ("conv_done", "gate_act", "hidden_prod", "hidden_hi", "hidden_lo"))
        g_abs, g_ln, g_cum, g_e1, g_d, g_e2, g_k, g_e3, k_end, q_dec = (sem(x) for x in (
            "gla_abs", "gla_ln", "gla_cumsum", "gla_exp_q", "gla_to_end", "gla_exp_end", "gla_k_end_done", "gla_exp_k",
            "k_end_done", "q_k_decayed"))
        att_ok, g_ss, g_out, states = sem("att_masked"), sem("gla_root"), sem("gla_out"), sem("states_done")
        line_ok, line_in, bias_in, s_max, s_exp, s_sexp, s_out = (sem(x) for x in (
            "line_made", "line_stored", "bias_in", "swa_max", "swa_exp", "swa_sink_exp", "swa_out"))
        s_shift, keys_swapped = sem("swa_shift"), sem("keys_swapped")
        mix_t, mix_hi = sem("mix_gated"), sem("mix_hi")
        c_max, c_exp, c_norm, c_hi = (sem(x) for x in ("cross_max", "cross_exp", "cross_normed", "cross_hi"))

        plan = Plan()

        def view(x):
            return x.rearrange("(k p) n -> p k n", p=P)

        def cols(w, k0, k1, c0, step, width):
            v = view(w)
            if step:
                return (lambda i, eng: v[:, k0:k1, bass.ds(eng.snap(i * step + c0), width)]), k1 - k0, width
            return (lambda i, eng: v[:, k0:k1, c0:c0 + width]), k1 - k0, width

        def wide(w, c0):
            return [cols(w, 2 * j, 2 * j + 2, c0, 0, HALF) for j in range(4)]

        w_in, w_in2 = a["w_in"][0], a["w_in_2"][0]
        stages = {}
        loads, stores, tiles = [0, 0, 0], [0, 0, 0], 0

        def stage(name, n, kind, hin, xn, gpre, gpost=None, src=None, dst=None, Y=None, gnames=(), dest=None, fused=None):
            nonlocal tiles
            st = dict(name=name, n=n, kind=kind, src=src, dst=dst, Y=Y, gnames=gnames, dest=dest, fused=fused, first=tiles,
                      hin=at(f"hin_{name}", hin, [P, 3 if n > 2 else 2, D]), xn=at(f"xn_{name}", xn, [P, 2, D]),
                      gpre=at(f"gpre_{name}", gpre, [P, D]),
                      gpost=None if gpost is None else at(f"gpost_{name}", gpost, [P, D]), load={}, store={})
            for t in range(n):
                loads[t % 3] += 1
                st["load"][t] = loads[t % 3]
                if dst is not None:
                    stores[t % 3] += 1
                    st["store"][t] = stores[t % 3]
            st["gains"] = sum(len(s["gnames"]) for s in stages.values()) + len(gnames)
            st["posts"] = sum(s["n"] for s in stages.values() if s["kind"] == "post")
            st["news"] = sum(s["n"] for s in stages.values() if s["kind"] != "load")
            st["turns"] = sum(s["n"] for s in stages.values() if s["dest"] is not None)
            stages[name] = st
            tiles += n

        def plan_stage(st, mm=None, early=()):
            for s in range(st["n"] + 2):
                if mm and s < st["n"]:
                    plan.group(*mm, s)
                if s == st["n"]:
                    for key in early:
                        plan.group(*key)
                if s >= 2 and st["dest"] is not None:
                    plan.group("T", st["name"], s - 2)

        U = (Uhi, Ulo)
        x_t = a["x"][0].rearrange("(t p) d -> t p d", p=P)
        hd_t = [h.rearrange("(t p) d -> t p d", p=P) for h in hd]
        mem_t = a["mem_2"][0].rearrange("(t p) d -> t p d", p=P)
        out_t = out[0].rearrange("(t p) d -> t p d", p=P)
        yM = at("yM", 64, [P, NT, D])
        y3, y4 = at("y3", 80, [P, NT, HALF]), at("y4", 64, [P, NT, HALF])
        stage("x", 8, "load", 64, 76, 84, src=x_t, gnames=("mix_pre_g",), dest=U)
        stage("mix1", 8, "post", 96, 108, 116, 120, src=x_t, dst=hd_t[0], Y=yM, gnames=("ffn_pre_g", "mix_post_g"), dest=U, fused="copy")
        stage("ffn1", 8, "post", 128, 80, 140, 88, src=hd_t[0], dst=hd_t[1], Y=acc, gnames=("norm_mix_2", "ffn_post_g"), dest=U, fused="down")
        stage("mem", 2, "load", 132, 104, 100, src=mem_t, gnames=("norm_mem_2",), dest=(memhi, memlo))
        stage("mix2", 8, "add", 112, 124, 96, src=hd_t[1], dst=hd_t[2], Y=y3, gnames=("norm_cross_2",), dest=U, fused="add")
        stage("cross", 8, "add", 112, 104, 96, src=hd_t[2], dst=hd_t[3], Y=y4, gnames=("norm_ffn_2",), dest=U, fused="add")
        stage("ffn2", 8, "add", 128, 88, 140, src=hd_t[3], Y=acc, gnames=("norm_final_2",), fused="down")

        UNITS = [(h, i) for h in range(4) for i in range(NT)]

        def stat(u, m):
            return slice(2 * (u % 4) + m, 2 * (u % 4) + m + 1)

        CU = [(hf, h) for hf in range(2) for h in range(4)]

        plan.group("cols")
        plan_stage(stages["x"], early=(("p", 0), ("p", 1)))
        plan.block("p", wide(w_in, 0))
        for c in range(2, 4):
            plan.group("p", c)
        plan.block("q", wide(w_in, 512))
        for c in range(4):
            plan.group("q", c)
        plan.last.update({k: (k, 3) for k in ("p", "q", "k", "gqk", "sq", "r")})
        plan.last.update({"v": ("v", 7), "gv": ("gv", 7), "misc": ("sv",)})
        plan.last.update({("gate", half, d): ("y", half, d) for half in "ab" for d in range(2)})
        plan.last.update({(n, cb): (n, cb, 7) for n in ("w_out", "w_out2", "w_o") for cb in range(2)})
        plan.last.update({(n, cb): (n, cb) for n in ("wk", "wv") for cb in range(2)})
        plan.last.update({("wq", cb): ("wq", cb, 3) for cb in range(2)})
        for n in ("f1", "f2"):
            plan.last.update({(n, "first up"): (n, "first u", 1), (n, "up"): (n, "d", 1), (n, "down"): (n, "d", 7), (n, "last down"): (n, "last d", 7)})
        hid_base = {"f1": 0, "f2": FC}
        for g in range(4):
            plan.group("pool", g)
        for half, gcol, branch in (("a", 2048, a["w_branch_a"][0]), ("b", 3072, a["w_branch_b"][0])):
            plan.loop(4, 4, 2, 4)
            for d in range(2):
                plan.block(("gate", half, d), [cols(w_in, 0, KT, gcol + P * d, 256, P), cols(branch, 0, 4, P * d, 256, P)])
                plan.group("gate", half, d)
                plan.group("y", half, d)
            plan.end()
            if half == "a":
                plan.block("k", wide(w_in, 1024))
                for c in range(4):
                    plan.group("k", c)
                plan.block("v", wide(w_in, 1536))
                for t in range(NT):
                    plan.group("v", t)
                for u in range(-2, len(UNITS)):
                    if u >= 0:
                        plan.group("aT", u)
                    if u + 2 < len(UNITS):
                        plan.group("sc", u + 2, 0)
                        plan.group("sc", u + 2, 1)
                    if u >= 0:
                        plan.group("pv", u)
                for h in range(4):
                    plan.group("oT", h)

        def first_ffn(name):
            return ((name, "first g", 0), (name, "first u", 0))

        for cb in range(2):
            plan.block(("w_out", cb), wide(a["w_out"][0], cb * HALF))
        for t in range(NT):
            plan.group("w_out", 0, t)
        plan_stage(stages["mix1"], ("w_out", 1), first_ffn("f1"))

        PAIRS = FC // 2

        def plan_ffn(name, up_src, down, st, early):
            plan.block((name, "first up"), [cols(w, 4 * j, 4 * j + 4, c0, 0, 256) for w, c0 in up_src for j in range(2)])
            plan.group(name, "first g", 1)
            plan.group(name, "first u", 1)
            plan.loop(PAIRS - 1, 12, 2, 6)
            plan.block((name, "up"), [cols(w, 4 * j, 4 * j + 4, c0 + 256, 256, 256) for w, c0 in up_src for j in range(2)])
            for c in range(2):
                plan.group(name, "g", c)
                plan.group(name, "u", c)
            dv = down.rearrange("(c p) n -> p c n", p=P)
            plan.block((name, "down"), [((lambda i, eng, j=j: dv[:, bass.ds(eng.snap(i * 2 + j), 1), :]), 1, D) for j in range(2)])
            for t in range(NT):
                plan.group(name, "d", t)
            plan.end()
            plan.block((name, "last down"), [((lambda i, eng, j=j: dv[:, FC - 2 + j:FC - 1 + j, :]), 1, D) for j in range(2)])
            plan_stage(st, (name, "last d"), early)

        plan_ffn("f1", ((a["w_ffn_gate"][0], 0), (a["w_ffn_up"][0], 0)), a["w_ffn_down"][0], stages["ffn1"], (("ga",), ("sk",)))
        plan.block("misc", [cols(w_in2, 0, KT, 1536, 0, P), cols(w_in2, 0, 4, 2064, 0, 256), cols(w_in2, 4, KT, 2064, 0, 256)])
        plan.block("gqk", wide(w_in2, 0))
        plan.group("sv")
        for c in range(4):
            plan.group("gqk", c)
        plan.group("alpha", 0)
        plan.group("alpha", 1)
        plan.block("sq", wide(w_in2, 1552))
        plan.block("r", wide(w_in2, 1024))
        plan.block("gv", wide(w_in2, 512))
        for key in ("sq", "r"):
            for c in range(4):
                plan.group(key, c)
        for t in range(NT):
            plan.group("gv", t)
        for j in range(2):
            plan.group("kendT", j)
        for t in range(-1, NT):
            if t + 1 < NT:
                plan.group("att", t + 1)
                plan.group("ssc", t + 1, 0)
                plan.group("ssc", t + 1, 1)
                if t % 2:
                    plan.group("kv", (t + 1) // 2)
            if t >= 0:
                plan.group("spT", t, 0)
                plan.group("spT", t, 1)
                plan.group("go", t)
                plan.group("so", t)
        for cb in range(2):
            plan.block(("w_out2", cb), wide(a["w_out_2"][0], cb * HALF))
        for t in range(-2, NT):
            if t + 2 < NT:
                plan.group("mixT", t + 2)
            if t >= 0:
                plan.group("w_out2", 0, t)
        plan_stage(stages["mem"])
        plan_stage(stages["mix2"], ("w_out2", 1), (("wk", 0), ("wk", 1)))
        for key, w in (("wk", a["w_k_c_2"][0]), ("wv", a["w_v_c_2"][0]), ("wq", a["w_q_c_2"][0])):
            for cb in range(2):
                plan.block((key, cb), wide(w, cb * HALF))
                if key == "wv":
                    plan.group(key, cb)
                elif key == "wq":
                    for c in range(4):
                        plan.group(key, cb, c)
        for cb in range(2):
            plan.block(("w_o", cb), wide(a["w_o_c_2"][0], cb * HALF))
        for u in range(-2, len(CU)):
            if u >= 0:
                plan.group("cT", u)
            if u + 2 < len(CU):
                plan.group("cs", u + 2)
            if u >= 0:
                plan.group("co", u)
            if u >= 4:
                plan.group("w_o", 0, u - 4)
        for t in range(4, NT):
            plan.group("w_o", 0, t)
        plan_stage(stages["cross"], ("w_o", 1), first_ffn("f2"))
        plan_ffn("f2", ((a["w_up_2"][0], 0), (a["w_up_2"][0], F)), a["w_down_2"][0], stages["ffn2"], ())

        def slot(*key):
            return slots[plan.slot(key)]

        def wait_full(eng, *key, i=0):
            eng.wait_ge(full[plan.slot(key)], plan.uses(key, i) + 1)

        def wait_freed(eng, *key, i=0):
            eng.wait_ge(free[plan.slot(key)], plan.uses(key, i) + 1)

        def freed(ins, *key):
            ins.then_inc(free[plan.slot(key)], 1)

        block = ctx.enter_context(nc.Block())

        @block.sync
        def _(sp):
            def load(src, n, w, p, i, per):
                s = p % 2
                src = src(i, sp)
                if p >= 2 or per:
                    sp.wait_ge(w_split, i * per + p - 1)
                    sp.sem_inc(raw_free, 1)
                sp.dma_start(raw[:, s, 0:n * w].rearrange("p (k c) -> p k c", k=n), src).then_inc(loaded[s], 16)

            p = 0
            for entry in plan.stream:
                if isinstance(entry[0], int):
                    trips, body = entry
                    per = sum(len(pieces) for _, pieces in body)
                    with sp.Fori(0, trips) as i:
                        q = p
                        for _, pieces in body:
                            for src, n, w in pieces:
                                load(src, n, w, q, i, per)
                                q += 1
                    p += trips * per
                else:
                    for src, n, w in entry[1]:
                        load(src, n, w, p, 0, 0)
                        p += 1

        @block.gpsimd
        def _(pool):
            own = Chain(pool, pool_own)
            own(pool.memset(ident[:, :], 0.0))
            pool.affine_select(out=ident[:, :], in_=ident[:, :], compare_op=ALU.not_equal, fill=1.0, base=0,
                               pattern=[[-1, P]], channel_multiplier=1).then_inc(consts_made, 1)
            pool.memset(eps[:, :], EPS).then_inc(consts_made, 1)
            own(pool.memset(causal[:, :], 1.0))
            own(pool.affine_select(out=causal[:, :], in_=causal[:, :], compare_op=ALU.is_ge, fill=0.0, base=0,
                                   pattern=[[1, P]], channel_multiplier=-1))
            pool.memset(causal[0:64, 64:128], 0.0).then_inc(consts_made, 1)
            own(pool.iota(cnt[:, :], pattern=[[1, 16]], base=1, channel_multiplier=0, allow_small_or_imprecise_dtypes=True))
            own(pool.memset(tiny[:, :], 1.0))

            def split(key, dst, first, n, p, b, i, per):
                s = p % 2
                if first and plan.reader(key):
                    group, trip = plan.reader(key)
                    count = plan.uses(group, i) + 1 - plan.groups[group][1] // 4 if trip is None else plan.uses(group, trip) + 1
                    pool.wait_ge(full[plan.slot(group)], count)
                pool.wait_ge(loaded[s], i * (per * 8) + 16 * (p // 2 + 1))
                pool.tensor_tensor(tiny[:, 1:2], tiny[:, 0:1], tiny[:, 0:1], ALU.mult)
                hi, lo = Whi[:, b % 2, dst:dst + n], Wlo[:, b % 2, dst:dst + n]
                pool.tensor_scalar(hi, raw[:, s, 0:n], 1.0, 1.0, ALU.mult, ALU.mult).then_inc(w_hi, 1)
                pool.wait_ge(w_hi, i * per + p + 1)
                pool.tensor_tensor(lo, raw[:, s, 0:n], hi.bitcast(f32), ALU.subtract).then_inc(w_split, 1)

            def make_dist():
                wait_full(pool, "pool", 3)
                own(pool.iota(dist[:, :], pattern=[[1, SEQ]], base=-(SEQ - P), channel_multiplier=-1, allow_small_or_imprecise_dtypes=True))
                pool.affine_select(out=dist[:, :], in_=dist[:, :], compare_op=ALU.is_ge, fill=NEG, base=SEQ - P,
                                   pattern=[[-1, SEQ]], channel_multiplier=1).then_inc(dist_made, 1)

            def run(blocks, p, b, i, per):
                for key, pieces in blocks:
                    if key == "k":
                        make_dist()
                    dst = 0
                    for j, (_, n, w) in enumerate(pieces):
                        split(key, dst, j == 0, n * w, p, b, i, per)
                        dst += n * w
                        p += 1
                    b += 1
                return p, b

            p = b = 0
            for entry in plan.stream:
                if isinstance(entry[0], int):
                    trips, body = entry
                    per = sum(len(pieces) for _, pieces in body)
                    with pool.Fori(0, trips) as i:
                        run(body, p, b, i, per)
                    p, b = p + trips * per, b + trips * len(body)
                else:
                    p, b = run([entry], p, b, 0, 0)

        @block.tensor
        def _(pe):
            def begin(*key, i=0):
                if plan.groups[key][0] >= 4 or plan.groups[key][1]:
                    pe.wait_ge(free[plan.slot(key)], plan.uses(key, i))
                return slots[plan.slot(key)]

            def done(ins, *key):
                ins.then_inc(full[plan.slot(key)], 1)

            def weights(key, i=0):
                b, p, n, bper, pper = plan.blocks[key]
                pe.wait_ge(w_split, i * pper + p + n if pper else p + n)
                return Whi[:, b % 2, :], Wlo[:, b % 2, :]

            def mm3(o, l, r, start, stop):
                for j, (x, y) in enumerate(((0, 0), (0, 1), (1, 0))):
                    ins = pe.matmul(o, lhsT=l[x], rhs=r[y], start=start and j == 0, stop=stop and j == 2)
                return ins

            def pair(t, *idx):
                return tuple(x[idx] for x in t)

            def turn(o, src):
                return pe.transpose(o, src, ident[:, :])

            def half(w, off, width, c, src, o, hf, n=KT):
                wv = tuple(x[:, off:off + n * width].rearrange("p (k c) -> p k c", k=n) for x in w)
                ts = slice(hf * HALF, hf * HALF + HALF)
                for k in range(n):
                    ins = mm3(o[:, ts], pair(wv, slice(None), k, slice(c, c + P)), pair(src, slice(None), k, ts), k == 0, k == n - 1)
                return ins

            def features(w, off, width, c, src, key, i=0, n=KT):
                o = begin(*key, i=i)
                half(w, off, width, c, src, o, 0, n)
                return half(w, off, width, c, src, o, 1, n)

            def early_halves(name, block_key, parts):
                def start(j):
                    def f(o):
                        if j == 0:
                            for t in range(NT // 2):
                                wait_freed(pe, "T", name, t)
                        half(weights(block_key), *parts[j][1:], U, o, 0)
                    return parts[j][0], f

                def finish():
                    u_ready(name)
                    for key, *where in parts:
                        done(half(weights(block_key), *where, U, slot(*key), 1), *key)

                return [start(0), start(1)], finish

            def tokens(w, t, src, o, made=None):
                wv = tuple(x.rearrange("p (k c) -> p k c", k=KT) for x in w)
                for k in range(KT):
                    if made:
                        pe.wait_ge(made, k + 1)
                    ins = mm3(o, pair(src, slice(None), k, slice(t * P, t * P + P)), pair(wv, slice(None), k), k == 0, k == KT - 1)
                return ins

            def wide_features(key, src, block_key=None, first=0):
                w = weights(block_key or key[0])
                for c in range(first, 4):
                    k = (*key, c)
                    done(features(w, 0, HALF, c * P, src, k), *k)

            def run_stage(st, mm=None, product=None, early=()):
                n = st["n"]
                for s in range(n + 2):
                    if mm and s < n:
                        key = (*mm, s)
                        done(product(s, begin(*key)), *key)
                    if s == n:
                        for key, start in early:
                            start(begin(*key))
                    t = s - 2
                    if t >= 0 and st["dest"] is not None:
                        pe.wait_ge(xn_done, st["first"] + t + 1)
                        o = begin("T", st["name"], t)
                        for k in range(KT):
                            ins = turn(o[:, k * P:k * P + P], st["xn"][:, t % 2, k * P:k * P + P])
                        done(ins, "T", st["name"], t)

            def u_ready(name, n=NT):
                for t in range(n):
                    wait_freed(pe, "T", name, t)

            def first_up(name, st):
                return early_halves(st, (name, "first up"), [((name, "first g", 0), 0, 256, 0), ((name, "first u", 0), 2048, 256, 0)])

            def ffn(name, st, early):
                def up(w, gate, value, i=0, first=0):
                    for c in range(first, 2):
                        for j, part in enumerate((gate, value)):
                            done(features(w, 2048 * j, 256, c * P, U, (name, part, c), i), name, part, c)

                def down_weights(part, i=0):
                    return tuple(x[:, 0:2 * D].rearrange("p (c n) -> p c n", c=2) for x in weights((name, part), i))

                def down(w, t, o):
                    for half in range(2):
                        cs = slice(half * HALF, half * HALF + HALF)
                        for c in range(2):
                            ins = mm3(o[:, cs], (Hhi[:, c, t * P:t * P + P], Hlo[:, c, t * P:t * P + P]),
                                      pair(w, slice(None), c, cs), c == 0, c == 1)
                    return ins

                base = hid_base[name]
                up(weights((name, "first up")), "first g", "first u", first=1)
                with pe.Fori(0, PAIRS - 1) as i:
                    up(weights((name, "up"), i), "g", "u", i)
                    w = down_weights("down", i)
                    pe.wait_ge(hid_lo, i * 2 + base + 2)
                    for t in range(NT):
                        done(down(w, t, begin(name, "d", t, i=i)), name, "d", t)
                w = down_weights("last down")
                pe.wait_ge(hid_lo, base + FC)
                run_stage(st, (name, "last d"), lambda t, o: down(w, t, o), early)

            pe.wait_ge(consts_made, 3)
            pe.wait_ge(params_in, 16 * N_PARAMS)
            o = begin("cols")
            pe.transpose(o[:, 0:96], rowA[:, :], ident[0:96, 0:96])
            done(pe.transpose(o[:, HALF:HALF + 88], rowB[:, :], ident[0:88, 0:88]), "cols")
            early, finish = early_halves("x", "p", [(("p", c), 0, HALF, c * P) for c in range(2)])
            run_stage(stages["x"], early=early)
            finish()
            wide_features(("p",), U, first=2)
            wide_features(("q",), U)
            for g in range(4):
                pe.wait_ge(pool_ready, g + 1)
                o = begin("pool", g)
                for hf in range(2):
                    ins = pe.matmul(o[:, hf * HALF:hf * HALF + HALF], lhsT=mixw[:, g, :],
                                    rhs=pS[:, g, hf * HALF:hf * HALF + HALF], start=True, stop=True)
                done(ins, "pool", g)

            def gates(half, src):
                with pe.Fori(0, 4) as i:
                    for d in range(2):
                        w = weights(("gate", half, d), i)
                        done(features(w, 0, P, 0, U, ("gate", half, d), i), "gate", half, d)
                        done(features(w, D, P, 0, src, ("y", half, d), i, n=4), "y", half, d)

            for g in range(4):
                wait_freed(pe, "pool", g)
            gates("a", (poolhi, poollo))
            wide_features(("k",), U)
            w = weights("v")
            for t in range(NT):
                done(tokens(w, t, U, begin("v", t)[:, 0:HALF]), "v", t)
            for c in range(4):
                wait_freed(pe, "k", c)
            for t in range(NT):
                wait_freed(pe, "v", t)
            for u in range(-2, len(UNITS)):
                if u >= 0:
                    h, i = UNITS[u]
                    pe.wait_ge(a_done, u + 1)
                    o = begin("aT", u)
                    for j in range(i + 1):
                        ins = turn(o[:, j * P:j * P + P], pp[:, u % 3, 0, j * P:j * P + P])
                    done(ins, "aT", u)
                if u + 2 < len(UNITS):
                    h, i = UNITS[u + 2]
                    for m in range(2):
                        o = begin("sc", u + 2, m)
                        r = slice(64 * m, 64 * m + 64)
                        for c0 in range(0, P * (i + 1), HALF):
                            c1 = min(c0 + HALF, P * (i + 1))
                            ins = pe.matmul(o[:, c0:c1], lhsT=qT[r, h, i * P:i * P + P], rhs=kTt[r, h, c0:c1], start=True, stop=True)
                        done(ins, "sc", u + 2, m)
                if u >= 0:
                    h, i = UNITS[u]
                    wait_freed(pe, "aT", u)
                    o = begin("pv", u)
                    for j in range(i + 1):
                        ins = pe.matmul(o[:, 0:P], lhsT=aT[:, j * P:j * P + P], rhs=vt[:, j, h * P:h * P + P],
                                        start=j == 0, stop=j == i)
                    done(ins, "pv", u)
            for h in range(4):
                pe.wait_ge(o_scaled, h + 1)
                o = begin("oT", h)
                for i in range(NT):
                    ins = turn(o[:, i * P:i * P + P], qT[:, h, i * P:i * P + P])
                done(ins, "oT", h)
            for h in range(4):
                wait_freed(pe, "oT", h)
            gates("b", (oThi, oTlo))
            w = weights(("w_out", 0))
            for t in range(NT):
                done(tokens(w, t, U, begin("w_out", 0, t)[:, 0:HALF], m_lo if t == 0 else None), "w_out", 0, t)
            w = weights(("w_out", 1))
            early, finish = first_up("f1", "mix1")
            run_stage(stages["mix1"], ("w_out", 1), lambda t, o: tokens(w, t, U, o[:, 0:HALF]), early)
            finish()
            early, finish = early_halves("ffn1", "misc", [(("ga",), 0, P, 0), (("sk",), D, 256, 0)])
            ffn("f1", stages["ffn1"], early)
            finish()
            w = weights("misc")
            o = begin("sv")
            wv = tuple(x[:, D:D + KT * 256].rearrange("p (k c) -> p k c", k=KT) for x in w)
            for t in range(NT):
                for k in range(KT):
                    ins = mm3(o[:, t * P:t * P + P], pair(U, slice(None), k, slice(t * P, t * P + P)),
                              pair(wv, slice(None), k, slice(P, 256)), k == 0, k == KT - 1)
            done(ins, "sv")
            wide_features(("gqk",), U)
            wait_freed(pe, "ga")
            for hp in range(2):
                o = begin("alpha", hp)
                for hf in range(2):
                    ins = pe.matmul(o[:, hf * HALF:hf * HALF + HALF], lhsT=walpha[:, hp, :],
                                    rhs=aL[:, hf * HALF:hf * HALF + HALF], start=True, stop=True)
                done(ins, "alpha", hp)
            wide_features(("sq",), U)
            wide_features(("r",), U)
            w = weights("gv")
            for t in range(NT):
                done(tokens(w, t, U, begin("gv", t)[:, 0:HALF]), "gv", t)
            pe.wait_ge(q_dec, 1)
            for j in range(2):
                o = begin("kendT", j)
                for tt in range(4):
                    for hp in range(2):
                        t = 4 * j + tt
                        c = tt * 256 + hp * P
                        ins = turn(o[:, c:c + P], kend[:, hp, t * P:t * P + P])
                done(ins, "kendT", j)
            for j in range(2):
                wait_freed(pe, "kendT", j)
            for t in range(NT):
                wait_freed(pe, "gv", t)
            pe.wait_ge(keys_swapped, 32)
            for t in range(-1, NT):
                if t + 1 < NT:
                    n = t + 1
                    o = begin("att", n)
                    for h in range(4):
                        hp, hh = h // 2, h % 2
                        r = slice(64 * hh, 64 * hh + 64)
                        c = hh * HALF + hp * P
                        ins = pe.matmul(o[:, c:c + P], lhsT=gk[r, hp, n * P:n * P + P], rhs=gq[r, hp, n * P:n * P + P], start=True, stop=True)
                    done(ins, "att", n)
                    k0 = max(n - 1, 0) * P
                    off = P if n == 0 else 0
                    for g in range(2):
                        o = begin("ssc", n, g)
                        for hh in range(2):
                            r = slice(64 * hh, 64 * hh + 64)
                            keys = sk if hh == g else sw
                            for c in range(2):
                                c1 = hh * HALF + c * 256
                                ins = pe.matmul(o[:, c1 + off:c1 + 256], lhsT=sq[r, 2 * g + c, n * P:n * P + P],
                                                rhs=keys[r, k0:n * P + P], start=True, stop=True)
                        done(ins, "ssc", n, g)
                    if n % 2 == 0:
                        o = begin("kv", n // 2)
                        for tt in range(2):
                            for par in range(2):
                                r = slice(64 * par, 64 * par + 64)
                                for h in range(4):
                                    hp, hh = h // 2, h % 2
                                    c = par * HALF + tt * 256 + hp * P
                                    ins = pe.matmul(o[64 * hh:64 * hh + 64, c:c + P], lhsT=kendt[r, n + tt, h * 64:h * 64 + 64],
                                                    rhs=gv[r, n + tt, h * P:h * P + P], start=True, stop=True)
                        done(ins, "kv", n // 2)
                if t >= 0:
                    kts = (1,) if t == 0 else (0, 1)
                    pe.wait_ge(s_exp, 8 * (t + 1))
                    for g in range(2):
                        o = begin("spT", t, g)
                        for c in range(4):
                            for kt in kts:
                                cc = c * 256 + kt * P
                                ins = turn(o[:, cc:cc + P], sS[:, t % 2, 4 * g + c, kt * P:kt * P + P])
                        done(ins, "spT", t, g)
                    pe.wait_ge(states, 2 * t + 1)
                    pe.wait_ge(att_ok, 2 + t + 1)
                    o = begin("go", t)
                    for h in range(4):
                        hp, hh = h // 2, h % 2
                        r = slice(64 * hh, 64 * hh + 64)
                        c = hh * HALF + hp * P
                        ins = pe.matmul(o[:, c:c + P], lhsT=attS[:, t % 2, h, :], rhs=gv[:, t, h * P:h * P + P], start=True, stop=False,
                                        skip_group_check=True)
                        for par in range(2):
                            n = 2 * t + par
                            if n:
                                ins = pe.matmul(o[64 * par:64 * par + 64, c:c + P], lhsT=gq[r, hp, n * 64:n * 64 + 64],
                                                rhs=S[r, n, hp, :], start=False, stop=par == 1, skip_group_check=True)
                    done(ins, "go", t)
                    o = begin("so", t)
                    for g in range(2):
                        wait_freed(pe, "spT", t, g)
                        for c in range(4):
                            h = 4 * g + c
                            for kt in kts:
                                ins = pe.matmul(o[:, h * 64:h * 64 + 64], lhsT=pTs[:, h, kt, :],
                                                rhs=sv[:, t - 1 + kt, g * 64:g * 64 + 64], start=kt == kts[0], stop=kt == 1)
                    done(ins, "so", t)
            w = weights(("w_out2", 0))
            for t in range(-2, NT):
                if t + 2 < NT:
                    n = t + 2
                    pe.wait_ge(g_out, n + 1)
                    wait_freed(pe, "so", n)
                    if n == 0:
                        wait_freed(pe, "so", NT - 1)
                    o = begin("mixT", n)
                    for k in range(4):
                        turn(o[:, k * P:k * P + P], gv[:, n, k * P:k * P + P])
                    for k in range(4):
                        ins = turn(o[:, HALF + k * P:HALF + k * P + P], sq[:, k, n * P:n * P + P])
                    done(ins, "mixT", n)
                if t >= 0:
                    wait_freed(pe, "mixT", t)
                    done(tokens(w, t, U, begin("w_out2", 0, t)[:, 0:HALF]), "w_out2", 0, t)
            run_stage(stages["mem"])
            w = weights(("w_out2", 1))


            def memory_keys(cb):
                def f(o):
                    if cb == 0:
                        u_ready("mem", 2)
                    wv = tuple(x.rearrange("p (k c) -> p k c", k=KT) for x in weights(("wk", cb)))
                    for c in range(4):
                        for k in range(KT):
                            ins = mm3(o[:, c * MEM:c * MEM + MEM], pair(wv, slice(None), k, slice(c * P, c * P + P)),
                                      (memhi[:, k, :], memlo[:, k, :]), k == 0, k == KT - 1)
                    done(ins, "wk", cb)
                return ("wk", cb), f

            run_stage(stages["mix2"], ("w_out2", 1), lambda t, o: tokens(w, t, U, o[:, 0:HALF]), [memory_keys(0), memory_keys(1)])
            for cb in range(2):
                w = weights(("wv", cb))
                o = begin("wv", cb)
                for t in range(2):
                    ins = tokens(w, t, (memhi, memlo), o[:, t * HALF:t * HALF + HALF])
                done(ins, "wv", cb)
            u_ready("mix2")
            for cb in range(2):
                wide_features(("wq", cb), U, ("wq", cb))
            for cb in range(2):
                wait_freed(pe, "wk", cb)
                wait_freed(pe, "wv", cb)
                for c in range(4):
                    wait_freed(pe, "wq", cb, c)
            for u in range(-2, len(CU)):
                if u >= 0:
                    pe.wait_ge(c_norm, u + 1)
                    o = begin("cT", u)
                    for kt in range(2):
                        for j in range(4):
                            c = kt * HALF + j * P
                            ins = turn(o[:, c:c + P], pC[:, u % 2, j, kt * P:kt * P + P])
                    done(ins, "cT", u)
                if u + 2 < len(CU):
                    hf, h = CU[u + 2]
                    o = begin("cs", u + 2)
                    for j in range(4):
                        t = 4 * hf + j
                        for k in range(2):
                            ins = pe.matmul(o[:, j * MEM:j * MEM + MEM], lhsT=qC[:, 2 * h + k, t * P:t * P + P],
                                            rhs=kC[:, 2 * h + k, :], start=k == 0, stop=k == 1)
                    done(ins, "cs", u + 2)
                if u >= 0:
                    hf, h = CU[u]
                    wait_freed(pe, "cT", u)
                    o = begin("co", u)
                    for dt in range(2):
                        for kt in range(2):
                            f0 = h * 256 + dt * P
                            ins = pe.matmul(o[:, dt * HALF:dt * HALF + HALF], lhsT=vC[:, kt, f0:f0 + P],
                                            rhs=pTC[:, u % 2, kt, :], start=kt == 0, stop=kt == 1)
                    done(ins, "co", u)
                if u >= 4:
                    if u == 4:
                        for v in range(4):
                            wait_freed(pe, "co", v)
                    done(tokens(weights(("w_o", 0)), u - 4, U, begin("w_o", 0, u - 4)[:, 0:HALF]), "w_o", 0, u - 4)
            for u in range(4, len(CU)):
                wait_freed(pe, "co", u)
            w = weights(("w_o", 0))
            for t in range(4, NT):
                done(tokens(w, t, U, begin("w_o", 0, t)[:, 0:HALF]), "w_o", 0, t)
            w = weights(("w_o", 1))
            early, finish = first_up("f2", "cross")
            run_stage(stages["cross"], ("w_o", 1), lambda t, o: tokens(w, t, U, o[:, 0:HALF]), early)
            finish()
            ffn("f2", stages["ffn2"], ())

        @block.scalar
        def _(act):
            own = Chain(act, act_own)

            def load_h(st, t):
                b = t % 3
                if t >= 3:
                    act.wait_ge(xn_done, st["first"] + t - 2)
                    if st["dst"] is not None:
                        act.wait_ge(h_stored[b], 16 * st["store"][t - 3])
                act.dma_start(st["hin"][:, b, :], st["src"][t]).then_inc(h_loaded[b], 16)

            def begin_stage(st):
                gains = (st["gpre"], st["gpost"])
                for g, name in zip(gains, st["gnames"]):
                    v = a[name] if name == "norm_final_2" else a[name][0]
                    act.dma_start(g[:, :], v.partition_broadcast(P)).then_inc(gains_in, 16)
                load_h(st, 0)

            def run_stage(st, mm=None):
                n, hin, xn, Y = st["n"], st["hin"], st["xn"], st["Y"]
                for s in range(n + 2):
                    if s < n and st["kind"] == "post":
                        if st["fused"] == "copy":
                            wait_full(act, *mm, s)
                            wait_freed(act, mm[0], 0, s)
                            freed(act.activation(Y[:, s, HALF:D], slot(*mm, s)[:, 0:HALF], ACT.Copy), *mm, s)
                            wait_freed(act, *mm, s)
                        else:
                            wait_freed(act, *mm, s)
                        if s >= 2:
                            act.wait_ge(xn_done, st["first"] + s - 1)
                            wait_full(act, "T", st["name"], s - 2)
                        own(act.activation(xn[:, s % 2, :], Y[:, s, :], ACT.Square, accum_out=ssp[:, s % 4:s % 4 + 1]))
                        if s >= 4:
                            act.wait_ge(h_new, st["news"] + s - 3)
                        act.activation(rtp[:, s % 4:s % 4 + 1], ssp[:, s % 4:s % 4 + 1], ACT.Sqrt, bias=eps[:, :], scale=1.0 / D).then_inc(post_root, 1)
                    t = s - 1
                    if 0 <= t < n:
                        b = t % 3
                        if st["kind"] == "load":
                            act.wait_ge(h_loaded[b], 16 * st["load"][t])
                        else:
                            act.wait_ge(h_new, st["news"] + t + 1)
                            if st["dst"] is not None:
                                act.dma_start(st["dst"][t], hin[:, b, :]).then_inc(h_stored[b], 16)
                        if t >= 2:
                            if st["dest"] is not None:
                                wait_full(act, "T", st["name"], t - 2)
                            else:
                                act.wait_ge(out_stored[t % 2], 16 * (t // 2))
                        own(act.activation(xn[:, t % 2, :], hin[:, b, :], ACT.Square, accum_out=ss[:, t % 4:t % 4 + 1]))
                        if t >= 4:
                            act.wait_ge(xn_done, st["first"] + t - 3)
                        act.activation(rt[:, t % 4:t % 4 + 1], ss[:, t % 4:t % 4 + 1], ACT.Sqrt, bias=eps[:, :], scale=1.0 / D).then_inc(pre_root, 1)
                    t = s - 2
                    if t >= 0:
                        if st["dest"] is not None:
                            wait_full(act, "T", st["name"], t)
                            act.activation(st["dest"][0][:, :, t * P:t * P + P],
                                           slot("T", st["name"], t)[:, :].rearrange("p (k c) -> p k c", k=KT), ACT.Copy).then_inc(tr_hi, 1)
                        else:
                            act.wait_ge(xn_done, st["first"] + t + 1)
                            act.dma_start(out_t[t], xn[:, t % 2, :]).then_inc(out_stored[t % 2], 16)
                    if s + 1 < n:
                        load_h(st, s + 1)
                if st["dst"] is not None:
                    for t in range(n - 3, n):
                        act.wait_ge(h_stored[t % 3], 16 * st["store"][t])

            def copy_out(dst, src, key, scale=1.0):
                wait_full(act, *key)
                freed(act.activation(dst, src, ACT.Copy, scale=scale), *key)

            def first_half(name, Y, start=0, end=NT):
                for t in range(start, end):
                    copy_out(Y[:, t, 0:HALF], slot(name, 0, t)[:, 0:HALF], (name, 0, t))

            cw, cb = a["conv_w_2"][0], a["conv_b_2"][0]
            params = [(rowA[0:44, :], cw[0].rearrange("(r c) -> r c", c=P)), (rowA[44:88, :], cw[1].rearrange("(r c) -> r c", c=P)),
                      (rowA[88:92, :], a["pool_scale"][0].rearrange("(r c) -> r c", c=P)), (rowA[92:93, :], a["subln_g"]),
                      (rowA[93:94, :], a["gla_gain_2"]), (rowA[94:96, :], a["b_alpha_2"][0].rearrange("(r c) -> r c", c=P)),
                      (rowB[0:44, :], cw[2].rearrange("(r c) -> r c", c=P)), (rowB[44:88, :], cb.rearrange("(r c) -> r c", c=P)),
                      (mixw[:, :, :], a["pool_mix"][0].rearrange("g c d -> c g d")),
                      (walpha[:, :, :], a["w_alpha_2"][0].rearrange("r (h c) -> r h c", c=P)),
                      (sink[:, :], a["sinks_2"][0].partition_broadcast(P))]
            params += [(lamr[:, n, :], a[x][0].partition_broadcast(P)) for n, x in enumerate(("lam_q1", "lam_k1", "lam_q2", "lam_k2"))]
            assert len(params) == N_PARAMS
            begin_stage(stages["x"])
            for dst, src in params:
                act.dma_start(dst, src).then_inc(params_in, 16)
            for s in m_stored:
                act.sem_inc(s, 16)
            act.wait_ge(consts_made, 3)
            wait_full(act, "cols")
            act.activation(colA[:, :], slot("cols")[:, 0:96], ACT.Copy).then_inc(cols_in, 1)
            freed(act.activation(colB[:, :], slot("cols")[:, HALF:HALF + 88], ACT.Copy), "cols")
            run_stage(stages["x"])
            act.wait_ge(lam_sum, 2)
            act.activation(lame[:, :], lam2[:, :], ACT.Exp).then_inc(lam_exp, 1)
            for c in range(4):
                copy_out(pT[:, c, :], slot("p", c)[:, :], ("p", c))
            for c in range(4):
                copy_out(qT[:, c, :], slot("q", c)[:, :], ("q", c), scale=0.125)
            act.wait_ge(cols_in, 1)
            for g in range(4):
                wait_full(act, "pool", g)
                act.activation(poolhi[:, g, :], slot("pool", g)[:, :], ACT.Copy, scale=colA[:, 88 + g:89 + g]).then_inc(pool_hi, 1)

            with act.Fori(0, 4) as i:
                for d in range(2):
                    wait_full(act, "gate", "a", d, i=i)
                    act.wait_ge(free[plan.slot(("y", "a", d))], plan.uses(("y", "a", d), i))
                    freed(act.activation(sgA[:, d, :], slot("gate", "a", d)[:, :], ACT.Sigmoid), "gate", "a", d)
                    wait_freed(act, "y", "a", d, i=i)
                    act.dma_start(m_dram[bass.ds(i * 256 + d * P, P), :], mst[:, d, :]).then_inc(m_stored[d], 16)
            for c in range(4):
                copy_out(kTt[:, c, :], slot("k", c)[:, :], ("k", c))
            for t in range(NT):
                copy_out(vt[:, t, :], slot("v", t)[:, 0:HALF], ("v", t))
            for d in range(2):
                act.wait_ge(m_stored[d], 16 * 5)
            for u in range(-2, len(UNITS)):
                if u >= 0:
                    h, i = UNITS[u]
                    w = P * (i + 1)
                    if u >= 1:
                        wait_full(act, "pv", u - 1)
                    copy_out(aT[:, 0:w], slot("aT", u)[:, 0:w], ("aT", u))
                if u + 2 < len(UNITS):
                    n = u + 2
                    w = P * (UNITS[n][1] + 1)
                    for m in range(2):
                        act.wait_ge(neg_max, 2 * n + m + 1)
                        act.activation(pp[:, n % 3, m, 0:w], pp[:, n % 3, m, 0:w], ACT.Exp, bias=nmax[:, 0, stat(n, m)],
                                       accum_out=lsum[:, 0, stat(n, m)]).then_inc(p_exp, 1)
                if u >= 0:
                    wait_full(act, "pv", u)
                    own(act.activation(slot("pv", u)[:, P:2 * P], slot("pv", u)[:, 0:P], ACT.Square, scale=rsum[:, 0, stat(u, 0)],
                                       accum_out=ssA[:, u:u + 1]))
                    freed(act.activation(qT[:, h, i * P:i * P + P], slot("pv", u)[:, 0:P], ACT.Copy, scale=rsum[:, 0, stat(u, 0)]), "pv", u)
            act.dma_start(M[:, :, :], m_dram.rearrange("(k p) n -> p k n", p=P)).then_inc(m_loaded, 16)
            act.activation(rtA[:, :], ssA[:, :], ACT.Sqrt, bias=eps[:, :], scale=1.0 / P).then_inc(o_root, 1)
            for h in range(4):
                wait_full(act, "oT", h)
                act.activation(oThi[:, h, :], slot("oT", h)[:, :], ACT.Copy, scale=colA[:, 92:93]).then_inc(o_hi, 1)
            with act.Fori(0, 4) as i:
                for d in range(2):
                    wait_full(act, "gate", "b", d, i=i)
                    act.wait_ge(free[plan.slot(("y", "b", d))], plan.uses(("y", "b", d), i))
                    freed(act.activation(sgB[:, d, :], slot("gate", "b", d)[:, :], ACT.Sigmoid), "gate", "b", d)
            act.wait_ge(m_final, 1)
            begin_stage(stages["mix1"])
            for k in range(KT):
                act.activation(Uhi[:, k, :], M[:, k, :], ACT.Copy).then_inc(m_hi, 1)
            act.wait_ge(m_lo, KT)
            first_half("w_out", yM)
            run_stage(stages["mix1"], ("w_out", 1))

            def hidden(name, parts, i):
                k, j = (0, 0) if i is None else (i, i * 2 + 2)
                base = hid_base[name]
                for c in range(2):
                    if name == "f1":
                        wait_full(act, name, parts[0], c, i=k)
                        if i is not None:
                            act.wait_ge(hid_lo, i * 2 + base + c + 1)
                        freed(act.activation(hg[:, c, :], slot(name, parts[0], c)[:, :], ACT.Silu), name, parts[0], c)
                    else:
                        act.wait_ge(conv_done, j + c + 1)
                        act.activation(hg[:, c, :], hg[:, c, :], ACT.Silu).then_inc(act_done, 1)
                for c in range(2):
                    if name == "f1":
                        wait_freed(act, name, parts[1], c, i=k)
                    else:
                        act.wait_ge(hid_prod, j + c + 1)
                    if i is not None:
                        wait_full(act, name, "d", 7, i=i)
                    act.activation(Hhi[:, c, :], hg[:, c, :], ACT.Copy).then_inc(hid_hi, 1)

            def ffn(name, st):
                hidden(name, ("first g", "first u"), None)
                begin_stage(st)
                if name == "f1":
                    act.dma_start(relT[:, :], a["rel_bias_2"].rearrange("b h -> h b"), allow_slow_non_contiguous=True).then_inc(line_in, 16)
                with act.Fori(0, PAIRS - 1) as i:
                    hidden(name, ("g", "u"), i)
                if name == "f1":
                    act.wait_ge(line_ok, 1)
                    act.dma_start(line_dram.rearrange("q h j -> h q j"), line[:, :].unsqueeze(1).to_broadcast([8, P, 384])).then_inc(line_in, 16)
                act.wait_ge(hid_lo, hid_base[name] + FC)
                run_stage(st, (name, "last d"))

            ffn("f1", stages["ffn1"])
            copy_out(aL[:, :], slot("ga")[0:16, :], ("ga",))
            copy_out(sk[:, :], slot("sk")[:, :], ("sk",))
            copy_out(sv[:, :, :], slot("sv")[:, :].rearrange("p (t c) -> p t c", c=P), ("sv",))
            for c in range(4):
                copy_out((gq, gq, gk, gk)[c][:, c % 2, :], slot("gqk", c)[:, :], ("gqk", c), scale=0.125 if c < 2 else 1.0)
            act.wait_ge(g_abs, 1)
            own(act.activation(gt[:, :, :], gt[:, :, :], ACT.Exp, scale=-1.0))
            act.activation(gt[:, :, :], gt[:, :, :], ACT.Ln, bias=1.0).then_inc(g_ln, 1)
            act.wait_ge(g_cum, 1)
            act.activation(gx[:, :, :], gt[:, :, :], ACT.Exp, scale=1.0 / 16).then_inc(g_e1, 1)
            act.wait_ge(g_d, 1)
            act.activation(gx[:, :, :], gx[:, :, :], ACT.Exp, scale=1.0 / 16).then_inc(g_e2, 1)
            act.wait_ge(k_end, 1)
            act.activation(decay[:, :, :], gt[:, :, 63::64], ACT.Exp, scale=1.0 / 16).then_inc(g_e3, 1)
            act.activation(gx[:, :, :], gt[:, :, :], ACT.Exp, scale=-1.0 / 16).then_inc(g_e3, 1)
            for c in range(4):
                copy_out(sq[:, c, :], slot("sq", c)[:, :], ("sq", c), scale=0.125)
            for c in range(4):
                wait_full(act, "r", c)
                freed(act.activation(rT[:, c, :], slot("r", c)[:, :], ACT.Silu), "r", c)
            act.wait_ge(q_dec, 1)
            for t in range(NT):
                copy_out(gv[:, t, :], slot("gv", t)[:, 0:HALF], ("gv", t))
            for j in range(2):
                copy_out(kendt[:, 4 * j:4 * j + 4, :], slot("kendT", j)[:, :].rearrange("p (t c) -> p t c", t=4), ("kendT", j))
            act.dma_start(sw[0:64, :], sk[64:128, :]).then_inc(keys_swapped, 16)
            act.dma_start(sw[64:128, :], sk[0:64, :]).then_inc(keys_swapped, 16)
            act.wait_ge(line_in, 32)
            act.dma_start(bias[:, :, :], bass.AP(tensor=line_dram.tensor, offset=P - 1, ap=[[8 * 384 - 1, P], [384, 8], [1, 256]])).then_inc(bias_in, 16)
            for t in range(-1, NT):
                if t >= 0:
                    k0 = 1 if t == 0 else 0
                    if t >= 1:
                        wait_full(act, "so", t - 1)
                    for g in range(2):
                        copy_out(pTs[:, 4 * g:4 * g + 4, k0:2, :],
                                 slot("spT", t, g)[:, :].rearrange("p (h k c) -> p h k c", h=4, k=2)[:, :, k0:2, :], ("spT", t, g))
                if t + 1 < NT:
                    n = t + 1
                    c0 = P if n == 0 else 0
                    act.wait_ge(s_max, n + 1)
                    for h in range(8):
                        act.activation(sS[:, n % 2, h, c0:256], sS[:, n % 2, h, c0:256], ACT.Exp, bias=smax[:, n % 2, h:h + 1],
                                       accum_out=lsum[:, n % 2, h:h + 1]).then_inc(s_exp, 1)
                    act.wait_ge(s_shift, n + 1)
                    act.activation(sexp[:, n % 2, :], sexp[:, n % 2, :], ACT.Exp).then_inc(s_sexp, 1)
                if t >= 0:
                    wait_full(act, "go", t)
                    for h in range(4):
                        c = (h % 2) * HALF + (h // 2) * P
                        own(act.activation(gj[:, :], slot("go", t)[:, c:c + P], ACT.Square, accum_out=ssA[:, 4 * t + h:4 * t + h + 1]))
                    act.activation(rtA[:, 4 * t:4 * t + 4], ssA[:, 4 * t:4 * t + 4], ACT.Sqrt, bias=eps[:, :], scale=1.0 / P).then_inc(g_ss, 1)
            for t in range(NT):
                act.wait_ge(mix_t, t + 1)
                wait_full(act, "mixT", t)
                act.activation(Uhi[:, 0:4, t * P:t * P + P], mixt[:, t % 2, :, :], ACT.Copy).then_inc(mix_hi, 1)
                act.activation(Uhi[:, 4:8, t * P:t * P + P], slot("mixT", t)[:, HALF:D].rearrange("p (k c) -> p k c", k=4), ACT.Copy).then_inc(mix_hi, 1)
                if t >= 2:
                    first_half("w_out2", y3, t - 2, t - 1)
            first_half("w_out2", y3, NT - 2)
            begin_stage(stages["mem"])
            run_stage(stages["mem"])
            begin_stage(stages["mix2"])
            run_stage(stages["mix2"], ("w_out2", 1))
            for cb in range(2):
                copy_out(kC[:, 4 * cb:4 * cb + 4, :], slot("wk", cb)[:, :].rearrange("p (c n) -> p c n", c=4), ("wk", cb))
            for cb in range(2):
                copy_out(vC[:, :, cb * HALF:cb * HALF + HALF], slot("wv", cb)[:, :].rearrange("p (t n) -> p t n", t=2), ("wv", cb))
            for cb in range(2):
                for c in range(4):
                    copy_out(qC[:, 4 * cb + c, :], slot("wq", cb, c)[:, :], ("wq", cb, c), scale=0.0625)
            for u in range(-2, len(CU)):
                if u >= 0:
                    if u >= 2:
                        wait_full(act, "co", u - 2)
                    copy_out(pTC[:, u % 2, :, :], slot("cT", u)[:, :].rearrange("p (k n) -> p k n", k=2), ("cT", u))
                if u + 2 < len(CU):
                    n = u + 2
                    act.wait_ge(c_max, n + 1)
                    if n >= 2:
                        wait_full(act, "cT", n - 2)
                        act.wait_ge(c_norm, n - 1)
                    for j in range(4):
                        act.activation(pC[:, n % 2, j, :], slot("cs", n)[:, j * MEM:j * MEM + MEM], ACT.Exp, bias=nmax[:, n % 2, j:j + 1],
                                       accum_out=lsum[:, n % 2, j:j + 1]).then_inc(c_exp, 1)
                if u >= 0:
                    hf, h = CU[u]
                    wait_full(act, "co", u)
                    act.activation(Uhi[:, 2 * h:2 * h + 2, hf * HALF:hf * HALF + HALF],
                                   slot("co", u)[:, :].rearrange("p (k n) -> p k n", k=2), ACT.Copy).then_inc(c_hi, 1)
                if u >= 5:
                    first_half("w_o", y4, u - 5, u - 4)
            begin_stage(stages["cross"])
            first_half("w_o", y4, 3)
            run_stage(stages["cross"], ("w_o", 1))
            ffn("f2", stages["ffn2"])
            for n in range(2):
                act.wait_ge(out_stored[n], 16 * (NT // 2))

        @block.vector
        def _(dve):
            own = Chain(dve, dve_own)

            def tt(o, x, y, op):
                return dve.tensor_tensor(o, x, y, op)

            def stt(o, x, s, y, op0, op1):
                return dve.scalar_tensor_tensor(out=o, in0=x, scalar=s, in1=y, op0=op0, op1=op1)

            def lo_of(dst, src, hi, key):
                freed(tt(dst, src, hi.bitcast(f32), ALU.subtract), *key)

            def run_stage(st, mm=None):
                n, hin, xn, Y = st["n"], st["hin"], st["xn"], st["Y"]
                dve.wait_ge(gains_in, 16 * st["gains"])

                def add_last(t):
                    wait_full(dve, *mm, t)
                    freed(tt(Y[:, t, :], Y[:, t, :], slot(*mm, t)[:, :], ALU.add), *mm, t)

                down = st["fused"] == "down" and st["kind"] == "post"
                if down:
                    add_last(0)
                for s in range(n + 2):
                    if down and s + 1 < n:
                        add_last(s + 1)
                    if s < n and st["kind"] != "load":
                        b = s % 3
                        if st["kind"] == "post":
                            dve.wait_ge(post_root, st["posts"] + s + 1)
                            own(dve.reciprocal(rsp[:, s % 4:s % 4 + 1], rtp[:, s % 4:s % 4 + 1]))
                            own(stt(Y[:, s, :], Y[:, s, :], rsp[:, s % 4:s % 4 + 1], st["gpost"][:, :], ALU.mult, ALU.mult))
                            dve.wait_ge(h_loaded[b], 16 * st["load"][s])
                            tt(hin[:, b, :], hin[:, b, :], Y[:, s, :], ALU.add).then_inc(h_new, 1)
                        elif st["fused"] == "add":
                            dve.wait_ge(h_loaded[b], 16 * st["load"][s])
                            wait_full(dve, *mm, s)
                            freed(tt(hin[:, b, HALF:D], hin[:, b, HALF:D], slot(*mm, s)[:, 0:HALF], ALU.add), *mm, s)
                            wait_freed(dve, *mm, s)
                            wait_freed(dve, mm[0], 0, s)
                            tt(hin[:, b, 0:HALF], hin[:, b, 0:HALF], Y[:, s, :], ALU.add).then_inc(h_new, 1)
                        else:
                            dve.wait_ge(h_loaded[b], 16 * st["load"][s])
                            wait_full(dve, *mm, s)
                            freed(tt(hin[:, b, :], hin[:, b, :], slot(*mm, s)[:, :], ALU.add), *mm, s)
                            wait_freed(dve, *mm, s)
                            tt(hin[:, b, :], hin[:, b, :], Y[:, s, :], ALU.add).then_inc(h_new, 1)
                    t = s - 1
                    if 0 <= t < n:
                        b = t % 3
                        dve.wait_ge(pre_root, st["first"] + t + 1)
                        own(dve.reciprocal(rs[:, t % 4:t % 4 + 1], rt[:, t % 4:t % 4 + 1]))
                        stt(xn[:, t % 2, :], hin[:, b, :], rs[:, t % 4:t % 4 + 1], st["gpre"][:, :], ALU.mult, ALU.mult).then_inc(xn_done, 1)
                    t = s - 2
                    if t >= 0 and st["dest"] is not None:
                        hi, lo = st["dest"]
                        dve.wait_ge(tr_hi, st["turns"] + t + 1)
                        lo_of(lo[:, :, t * P:t * P + P], slot("T", st["name"], t)[:, :].rearrange("p (k c) -> p k c", k=KT),
                              hi[:, :, t * P:t * P + P], ("T", st["name"], t))

            dve.wait_ge(params_in, 16 * N_PARAMS)
            for m in range(2):
                dve.tensor_tensor_reduce(out=lamj[:, m, :], in0=lamr[:, 2 * m, :], in1=lamr[:, 2 * m + 1, :], scale=1.0, scalar=0.0,
                                         op0=ALU.mult, op1=ALU.add, accum_out=lam2[:, m:m + 1]).then_inc(lam_sum, 1)
            dve.wait_ge(pool_own, 4)
            own(dve.reciprocal(cnt[:, :], cnt[:, :]))
            run_stage(stages["x"])
            dve.wait_ge(lam_exp, 1)
            own(tt(nlam[:, :], lame[:, 1:2], lame[:, 0:1], ALU.subtract))
            own(dve.tensor_scalar(nlam[:, :], nlam[:, :], -LAMBDA_INIT, None, ALU.add))
            dve.wait_ge(cols_in, 1)
            own(dve.tensor_scalar(colA[:, 92:93], colA[:, 92:93], 1.0 - LAMBDA_INIT, None, ALU.mult))
            for g in range(4):
                w = 2 << g
                wait_freed(dve, "p", g)
                src = pT
                for j in range(g + 1):
                    sh = 1 << j
                    dst = pS if j % 2 == 0 else pX
                    s_ap = pT[:, g, :] if j == 0 else (pS[:, g, :] if j % 2 == 1 else pX[:, :])
                    d_ap = pS[:, g, :] if j % 2 == 0 else pX[:, :]
                    own(dve.tensor_copy(d_ap[:, 0:sh], s_ap[:, 0:sh]))
                    own(tt(d_ap[:, sh:SEQ], s_ap[:, sh:SEQ], s_ap[:, 0:SEQ - sh], ALU.add))
                last = pS[:, g, :] if g % 2 == 0 else pX[:, :]
                own(tt(last[:, 0:w - 1], last[:, 0:w - 1], cnt[:, 0:w - 1], ALU.mult))
                own(dve.tensor_scalar(last[:, w - 1:SEQ], last[:, w - 1:SEQ], 1.0 / w, None, ALU.mult))
                tt(pS[:, g, :], last, pT[:, g, :], ALU.subtract).then_inc(pool_ready, 1)
                dve.wait_ge(pool_ready, g + 1)
            for g in range(4):
                dve.wait_ge(pool_hi, g + 1)
                freed(stt(poollo[:, g, :], slot("pool", g)[:, :], colA[:, 88 + g:89 + g], poolhi[:, g, :].bitcast(f32),
                          ALU.mult, ALU.subtract), "pool", g)
            with dve.Fori(0, 4) as i:
                for d in range(2):
                    wait_freed(dve, "gate", "a", d, i=i)
                    wait_full(dve, "y", "a", d, i=i)
                    dve.wait_ge(m_stored[d], i * 16 + 16)
                    freed(tt(mst[:, d, :], sgA[:, d, :], slot("y", "a", d)[:, :], ALU.mult), "y", "a", d)
            for d in range(2):
                dve.wait_ge(m_stored[d], 16 * 5)
            dve.wait_ge(dist_made, 1)

            def scores(u):
                h, i = UNITS[u]
                w = P * (i + 1)
                c0 = SEQ - w
                for m in range(2):
                    wait_full(dve, "sc", u, m)
                    if u >= 3:
                        wait_full(dve, "aT", u - 3)
                    freed(stt(pp[:, u % 3, m, 0:w], dist[:, c0:SEQ], 2.0 ** (-2 * (h + 1)), slot("sc", u, m)[:, 0:w], ALU.mult, ALU.add),
                          "sc", u, m)
                    wait_freed(dve, "sc", u, m)
                    dve.tensor_reduce(nmax[:, 0, stat(u, m)], pp[:, u % 3, m, 0:w], axis=AX.X, op=ALU.max, negate=True).then_inc(neg_max, 1)

            def combine(u):
                w, k = P * (UNITS[u][1] + 1), 2 * (u % 4)
                dve.wait_ge(p_exp, 2 * u + 2)
                own(dve.reciprocal(rsum[:, 0, k:k + 2], lsum[:, 0, k:k + 2]))
                own(stt(c2[:, 0, stat(u, 0)], rsum[:, 0, stat(u, 1)], nlam[:, :], lsum[:, 0, stat(u, 0)], ALU.mult, ALU.mult))
                stt(pp[:, u % 3, 0, 0:w], pp[:, u % 3, 1, 0:w], c2[:, 0, stat(u, 0)], pp[:, u % 3, 0, 0:w], ALU.mult, ALU.add).then_inc(a_done, 1)

            scores(0)
            scores(1)
            combine(0)
            for u in range(len(UNITS)):
                if u + 1 < len(UNITS):
                    combine(u + 1)
                if u + 2 < len(UNITS):
                    scores(u + 2)
            dve.wait_ge(o_root, 1)
            own(dve.reciprocal(rsA[:, :], rtA[:, :]))
            for h in range(4):
                v = qT[:, h, :].rearrange("p (i c) -> p i c", i=NT)
                tt(v, v, rsA[:, 8 * h:8 * h + 8].unsqueeze(2).to_broadcast([P, NT, P]), ALU.mult).then_inc(o_scaled, 1)
            for h in range(4):
                dve.wait_ge(o_hi, h + 1)
                freed(stt(oTlo[:, h, :], slot("oT", h)[:, :], colA[:, 92:93], oThi[:, h, :].bitcast(f32), ALU.mult, ALU.subtract), "oT", h)
            dve.wait_ge(m_loaded, 16)
            with dve.Fori(0, 4) as i:
                own.loop(i, 2)
                for d in range(2):
                    wait_freed(dve, "gate", "b", d, i=i)
                    wait_full(dve, "y", "b", d, i=i)
                    freed(tt(prB[:, d, :], sgB[:, d, :], slot("y", "b", d)[:, :], ALU.mult), "y", "b", d)
                    wait_freed(dve, "y", "b", d, i=i)
                    m = M[:, bass.ds(i * 2 + d, 1), :].rearrange("p o n -> p (o n)")
                    own(tt(m, m, prB[:, d, :], ALU.add))
            own.end(4)
            dve.sem_inc(m_final, 1)
            for k in range(KT):
                dve.wait_ge(m_hi, k + 1)
                tt(Ulo[:, k, :], M[:, k, :], Uhi[:, k, :].bitcast(f32), ALU.subtract).then_inc(m_lo, 1)
            run_stage(stages["mix1"], ("w_out", 1))

            def hidden_lo(name, c, i):
                dve.wait_ge(hid_hi, hid_base[name] + c + 1 + (0 if i is None else i * 2 + 2))
                tt(Hlo[:, c, :], hg[:, c, :], Hhi[:, c, :].bitcast(f32), ALU.subtract).then_inc(hid_lo, 1)

            def add_down(name, i):
                for t in range(NT):
                    wait_full(dve, name, "d", t, i=i)
                    freed(tt(acc[:, t, :], acc[:, t, :], slot(name, "d", t)[:, :], ALU.add), name, "d", t)

            def clear_acc(st, others=()):
                for t in range(NT - 2, NT):
                    wait_full(dve, "T", st["name"], t)
                for t in range(NT - 3, NT):
                    dve.wait_ge(h_stored[t % 3], 16 * st["store"][t])
                own(dve.memset(acc[:, :, :], 0.0))

            clear_acc(stages["mix1"])
            def gated(gate, value, i=0):
                for c in range(2):
                    wait_freed(dve, "f1", gate, c, i=i)
                    wait_full(dve, "f1", value, c, i=i)
                    freed(tt(hg[:, c, :], hg[:, c, :], slot("f1", value, c)[:, :], ALU.mult), "f1", value, c)

            gated("first g", "first u")
            for c in range(2):
                hidden_lo("f1", c, None)
            own(dve.memset(line[:, :], NEG))
            dve.wait_ge(line_in, 16)
            for bk, d0, d1 in t5_ranges(P):
                own(dve.tensor_copy(line[:, 256 - d1:256 - d0], relT[:, bk:bk + 1].to_broadcast([8, d1 - d0])))
            dve.sem_inc(line_ok, 1)
            with dve.Fori(0, PAIRS - 1) as i:
                gated("g", "u", i)
                add_down("f1", i)
                for c in range(2):
                    hidden_lo("f1", c, i)
            run_stage(stages["ffn1"], ("f1", "last d"))
            for hp in range(2):
                wait_full(dve, "alpha", hp)
                freed(dve.tensor_scalar(gx[:, hp, :], slot("alpha", hp)[:, :], colA[:, 94 + hp:95 + hp], None, ALU.add), "alpha", hp)
            wait_freed(dve, "alpha", 0)
            wait_freed(dve, "alpha", 1)
            stt(gt[:, :, :], gx[:, :, :], -1.0, gx[:, :, :], ALU.mult, ALU.max).then_inc(g_abs, 1)
            own(dve.memset(reset[:, :], 1.0))
            own(dve.memset(reset[:, 0::64], 0.0))
            dve.wait_ge(g_ln, 1)
            own(stt(gx[:, :, :], gx[:, :, :], 0.0, gt[:, :, :], ALU.min, ALU.subtract))
            own(dve.tensor_tensor_scan(gt[:, 0, :], reset[:, :], gx[:, 0, :], 0.0, ALU.mult, ALU.add))
            own(dve.tensor_tensor_scan(gt[:, 1, :], reset[:, :], gx[:, 1, :], 0.0, ALU.mult, ALU.add))
            dve.sem_inc(g_cum, 1)
            for c in range(4):
                wait_freed(dve, "gqk", c)
            dve.wait_ge(g_e1, 1)
            own(tt(gq[:, :, :], gq[:, :, :], gx[:, :, :], ALU.mult))
            for hp in range(2):
                last = gt[:, hp, 63::64].unsqueeze(2).to_broadcast([P, 16, 64])
                own(tt(gx[:, hp, :].rearrange("p (n c) -> p n c", c=64), last, gt[:, hp, :].rearrange("p (n c) -> p n c", c=64), ALU.subtract))
            dve.sem_inc(g_d, 1)
            dve.wait_ge(g_e2, 1)
            tt(kend[:, :, :], gk[:, :, :], gx[:, :, :], ALU.mult).then_inc(k_end, 1)
            dve.wait_ge(g_e3, 2)
            dve.wait_ge(k_end, 1)
            tt(gk[:, :, :], gk[:, :, :], gx[:, :, :], ALU.mult).then_inc(q_dec, 1)
            def kv_ap(n, hp):
                t, par = n // 2, n % 2
                return slot("kv", t // 2)[:, par * HALF + (t % 2) * 256 + hp * P:par * HALF + (t % 2) * 256 + hp * P + P]

            def chunk_states(j):
                wait_full(dve, "kv", j)
                for n in range(4 * j, min(4 * j + 4, 15)):
                    if n == 0:
                        o = slot("kv", 0)[:, 0:256].rearrange("p (h c) -> p h c", h=2)
                        dve.tensor_copy(S[:, 1, :, :], o).then_inc(states, 1)
                    else:
                        dve.wait_ge(states, n)
                        own(stt(S[:, n + 1, 0, :], S[:, n, 0, :], decay[:, 0, n:n + 1], kv_ap(n, 0), ALU.mult, ALU.add))
                        stt(S[:, n + 1, 1, :], S[:, n, 1, :], decay[:, 1, n:n + 1], kv_ap(n, 1), ALU.mult, ALU.add).then_inc(states, 1)
                dve.wait_ge(states, min(4 * j + 4, 15))
                dve.sem_inc(free[plan.slot(("kv", j))], 1)

            wait_full(dve, "kendT", 1)
            for b in range(2):
                dve.memset(attS[:, b, :, :], 0.0).then_inc(att_ok, 1)
            dve.wait_ge(att_ok, 2)
            mask = causal[:, :].bitcast(u32).unsqueeze(1).to_broadcast([P, 2, P])

            def masked(t):
                wait_full(dve, "att", t)
                if t >= 2:
                    wait_full(dve, "go", t - 2)
                for hh in range(2):
                    src = slot("att", t)[:, hh * HALF:hh * HALF + 256].rearrange("p (h c) -> p h c", h=2)
                    ins = dve.copy_predicated(attS[:, t % 2, hh::2, :], mask, src)
                    if hh == 0:
                        own(ins)
                    else:
                        ins.then_inc(att_ok, 1)
                dve.wait_ge(att_ok, 2 + t + 1)
                dve.sem_inc(free[plan.slot(("att", t))], 1)

            def gla_output(t):
                dve.wait_ge(g_ss, t + 1)
                own(dve.reciprocal(rsA[:, 4 * t:4 * t + 4], rtA[:, 4 * t:4 * t + 4]))
                for hh in range(2):
                    src = slot("go", t)[:, hh * HALF:hh * HALF + 256].rearrange("p (h c) -> p h c", h=2)
                    dst = gv[:, t, :].rearrange("p (h c) -> p h c", h=4)[:, hh::2, :]
                    ins = tt(dst, src, rsA[:, 4 * t + hh:4 * t + 4:2].unsqueeze(2).to_broadcast([P, 2, P]), ALU.mult)
                    if hh == 0:
                        own(ins)
                    else:
                        ins.then_inc(g_out, 1)
                dve.wait_ge(g_out, t + 1)
                dve.sem_inc(free[plan.slot(("go", t))], 1)

            dve.wait_ge(bias_in, 16)

            def windowed(n):
                b, c0 = n % 2, P if n == 0 else 0
                for g in range(2):
                    wait_full(dve, "ssc", n, g)
                    if n >= 2:
                        wait_full(dve, "spT", n - 2, g)
                    src = slot("ssc", n, g)[:, :].rearrange("p (h c k) -> p h c k", h=2, c=2)[:, :, :, c0:256]
                    dst, bs = (x.rearrange("p (c h) k -> p h c k", h=2)[:, :, :, c0:256] for x in (sS[:, b, 4 * g:4 * g + 4, :], bias[:, 4 * g:4 * g + 4, :]))
                    freed(tt(dst, src, bs, ALU.add), "ssc", n, g)
                wait_freed(dve, "ssc", n, 0)
                wait_freed(dve, "ssc", n, 1)
                own(dve.tensor_reduce(smax[:, b, :], sS[:, b, :, c0:256], axis=AX.X, op=ALU.max))
                own(tt(smax[:, b, :], smax[:, b, :], sink[:, :], ALU.max))
                tt(sexp[:, b, :], sink[:, :], smax[:, b, :], ALU.subtract).then_inc(s_shift, 1)
                dve.wait_ge(s_shift, n + 1)
                dve.tensor_scalar(smax[:, b, :], smax[:, b, :], -1.0, None, ALU.mult).then_inc(s_max, 1)

            for t in range(-1, NT):
                if t + 1 < NT:
                    windowed(t + 1)
                    masked(t + 1)
                    if t % 2:
                        chunk_states((t + 1) // 2)
                if t >= 0:
                    b = t % 2
                    dve.wait_ge(s_exp, 8 * (t + 1))
                    dve.wait_ge(s_sexp, t + 1)
                    own(tt(lsum[:, b, :], lsum[:, b, :], sexp[:, b, :], ALU.add))
                    own(dve.reciprocal(rsum[:, b, :], lsum[:, b, :]))
                    gla_output(t)
                    wait_full(dve, "so", t)
                    for j in range(2):
                        ins = tt(sq[:, :, t * P + 64 * j:t * P + 64 * j + 64], slot("so", t)[:, 0:HALF].rearrange("p (c h d) -> p h c d", c=4, h=2)[:, j],
                                 rsum[:, b, j::2].unsqueeze(2).to_broadcast([P, 4, 64]), ALU.mult)
                        if j == 0:
                            own(ins)
                        else:
                            freed(ins, "so", t)

            def gated_mix(t):
                wait_full(dve, "mixT", t)
                if t >= 2:
                    dve.wait_ge(mix_hi, 2 * t - 2)
                stt(mixt[:, t % 2, :, :], slot("mixT", t)[:, 0:HALF].rearrange("p (k c) -> p k c", k=4), colA[:, 93:94],
                    rT[:, :, t * P:t * P + P], ALU.mult, ALU.mult).then_inc(mix_t, 1)

            gated_mix(0)
            for t in range(NT):
                ts = slice(t * P, t * P + P)
                if t + 1 < NT:
                    gated_mix(t + 1)
                dve.wait_ge(mix_t, t + 1)
                dve.wait_ge(mix_hi, 2 * t + 1)
                own(tt(Ulo[:, 0:4, ts], mixt[:, t % 2, :, :], Uhi[:, 0:4, ts].bitcast(f32), ALU.subtract))
                dve.wait_ge(mix_hi, 2 * t + 2)
                lo_of(Ulo[:, 4:8, ts], slot("mixT", t)[:, HALF:D].rearrange("p (k c) -> p k c", k=4), Uhi[:, 4:8, ts], ("mixT", t))
            run_stage(stages["mem"])
            run_stage(stages["mix2"], ("w_out2", 1))

            def cross_max(n):
                wait_full(dve, "cs", n)
                dve.tensor_reduce(nmax[:, n % 2, 0:4], slot("cs", n)[:, :].rearrange("p (j c) -> p j c", j=4), axis=AX.X, op=ALU.max,
                                  negate=True).then_inc(c_max, 1)

            def cross_norm(u):
                b = u % 2
                dve.wait_ge(c_exp, 4 * (u + 1))
                dve.sem_inc(free[plan.slot(("cs", u))], 1)
                own(dve.reciprocal(rsum[:, b, 0:4], lsum[:, b, 0:4]))
                tt(pC[:, b, :, :], pC[:, b, :, :], rsum[:, b, 0:4].unsqueeze(2).to_broadcast([P, 4, MEM]), ALU.mult).then_inc(c_norm, 1)

            cross_max(0)
            cross_max(1)
            cross_norm(0)
            for u in range(len(CU)):
                hf, h = CU[u]
                if u + 1 < len(CU):
                    cross_norm(u + 1)
                if u + 2 < len(CU):
                    cross_max(u + 2)
                dve.wait_ge(c_hi, u + 1)
                lo_of(Ulo[:, 2 * h:2 * h + 2, hf * HALF:hf * HALF + HALF], slot("co", u)[:, :].rearrange("p (k n) -> p k n", k=2),
                      Uhi[:, 2 * h:2 * h + 2, hf * HALF:hf * HALF + HALF], ("co", u))
            run_stage(stages["cross"], ("w_o", 1))
            clear_acc(stages["cross"])

            def convolved(gate, value, i):
                k, j = (0, 0) if i is None else (i, i * 2 + 2)

                def column(x, n):
                    return x[:, n:n + 1] if i is None else x[:, bass.ds(i * 2 + (n + 2), 1)]

                for c in range(2):
                    for part, dst, n in ((gate, hg, c), (value, hv, FC + c)):
                        o = slot("f2", part, c)
                        wait_full(dve, "f2", part, c, i=k)
                        if part == gate and i is not None:
                            dve.wait_ge(hid_lo, i * 2 + hid_base["f2"] + c + 1)
                        own(dve.tensor_scalar(dst[:, c, :], o[:, :], column(colB, n), column(colB, n + 44), ALU.mult, ALU.add))
                        own(stt(dst[:, c, 1:SEQ], o[:, 0:SEQ - 1], column(colA, n + 44), dst[:, c, 1:SEQ], ALU.mult, ALU.add))
                        freed(stt(dst[:, c, 2:SEQ], o[:, 0:SEQ - 2], column(colA, n), dst[:, c, 2:SEQ], ALU.mult, ALU.add), "f2", part, c)
                        wait_freed(dve, "f2", part, c, i=k)
                        if part == gate:
                            dve.sem_inc(conv_done, 1)
                for c in range(2):
                    dve.wait_ge(act_done, j + c + 1)
                    own(tt(hg[:, c, :], hg[:, c, :], hv[:, c, :], ALU.mult))
                    dve.sem_inc(hid_prod, 1)

            convolved("first g", "first u", None)
            for c in range(2):
                hidden_lo("f2", c, None)
            with dve.Fori(0, PAIRS - 1) as i:
                own.loop(i, 10)
                convolved("g", "u", i)
                add_down("f2", i)
                for c in range(2):
                    hidden_lo("f2", c, i)
            own.end(PAIRS - 1)
            run_stage(stages["ffn2"], ("f2", "last d"))


_INS = ['x', 'w_in', 'pool_mix', 'pool_scale', 'w_branch_a', 'lam_q1', 'lam_k1', 'lam_q2', 'lam_k2', 'subln_g',
        'w_branch_b', 'w_out', 'mix_pre_g', 'mix_post_g', 'ffn_pre_g', 'ffn_post_g', 'w_ffn_gate', 'w_ffn_up',
        'w_ffn_down', 'mem_2', 'norm_mix_2', 'w_in_2', 'w_alpha_2', 'b_alpha_2', 'gla_gain_2', 'rel_bias_2',
        'sinks_2', 'w_out_2', 'norm_cross_2', 'norm_mem_2', 'w_q_c_2', 'w_k_c_2', 'w_v_c_2', 'w_o_c_2', 'norm_ffn_2',
        'w_up_2', 'conv_w_2', 'conv_b_2', 'w_down_2', 'norm_final_2']


def kernel(**inputs):
    import numpy as _np
    import concourse.bacc as _bacc
    from concourse import mybir as _mybir
    from concourse.bass_utils import run_bass_kernel_spmd as _run

    nc = _bacc.Bacc("TRN2", target_bir_lowering=False, num_devices=1, dynamic_dma_scratch_size=1024)
    arrays, args = {}, {}
    for name in _INS:
        v = _np.ascontiguousarray(inputs[name])
        arrays[f"in_{name}"] = v
        args[name] = nc.dram_tensor(f"in_{name}", v.shape, _mybir.dt.from_np(v.dtype), kind="ExternalInput").ap()
    out = nc.dram_tensor("out_0", (1, SEQ, D), _mybir.dt.float32, kind="ExternalOutput").ap()
    build(nc, args, out)
    r = _run(nc, [arrays], core_ids=[0])
    return r.results[0]["out_0"]
```

```python
import math
from contextlib import ExitStack

import numpy as np
import concourse.bass as bass
from concourse import mybir

P = 128
SEQ = 1024
D = 1024
KT = D // P
NT = SEQ // P
HALF = 512
F = 2816
FC = F // P
EPS = 1e-6
MEM = 256
KB = 1024
BASE = 1152
RING = 144 * KB
CONST = RING + 72 * KB
SBUF_END = 229344
NEG = -3.0e38
N_PARAMS = 15
LAMBDA_INIT = 0.8 - 0.6 * math.exp(-0.3 * 0)


class Plan:

    def __init__(self):
        self.groups, self.n, self.per, self.start = {}, 0, 0, 0
        self.blocks, self.b, self.pieces, self.bper, self.pper = {}, 0, 0, 0, 0
        self.stream, self.order, self.last, self.trip_of = [], [], {}, {}
        self.body = self.stream

    def group(self, *key):
        self.groups[key] = (self.n, self.per)
        self.n += 1

    def block(self, key, pieces):
        self.blocks[key] = (self.b, self.pieces, len(pieces), self.bper, self.pper)
        self.order.append((key, self.b))
        self.body.append((key, pieces))
        self.trip_of[key] = self.trips if self.bper else 1
        self.b += 1
        self.pieces += len(pieces)

    def loop(self, trips, groups, blocks, pieces):
        assert groups % 4 == 0 and blocks % 2 == 0 and pieces % 2 == 0
        self.per, self.bper, self.pper, self.trips = groups, blocks, pieces, trips
        self.marks = (self.n, self.b, self.pieces)
        self.body = []
        self.stream.append((trips, self.body))

    def end(self):
        n, b, p = self.marks
        assert (self.n - n, self.b - b, self.pieces - p) == (self.per, self.bper, self.pper)
        more = self.trips - 1
        self.n, self.b, self.pieces = self.n + more * self.per, self.b + more * self.bper, self.pieces + more * self.pper
        self.per = self.bper = self.pper = 0
        self.body = self.stream

    def reader(self, key):
        b, bper = self.blocks[key][0], self.blocks[key][3]
        if bper:
            return self.last[key], None
        for k, n in self.order:
            per = self.blocks[k][3]
            if (n == b - 2) or (per and b - 2 >= n and (b - 2 - n) % per == 0 and (b - 2 - n) // per < self.trip_of[k]):
                return self.last[k], (b - 2 - n) // per if per else 0
        return None

    def slot(self, key):
        return self.groups[key][0] % 4

    def uses(self, key, i=0):
        n, per = self.groups[key]
        return n // 4 + i * (per // 4) if per else n // 4


class Chain:

    def __init__(self, eng, sem):
        self.eng, self.sem, self.n, self.more = eng, sem, 0, 0

    def __call__(self, ins):
        self.n += 1
        ins.then_inc(self.sem, 1)
        self.eng.wait_ge(self.sem, self.more + self.n)

    def loop(self, i, per):
        self.start, self.per, self.more = self.n, per, i * per

    def end(self, trips):
        assert self.n - self.start == self.per, (self.n - self.start, self.per)
        self.n, self.more = self.start + trips * self.per, 0


def t5_ranges(window):
    out = []
    for dist in range(window):
        b = dist if dist < 16 else min(31, 16 + int(math.log(dist / 16) / math.log(128 / 16) * 16))
        if out and out[-1][0] == b:
            out[-1][2] = dist + 1
        else:
            out.append([b, dist, dist + 1])
    return out


def build(nc, a, out):
    f32, f32r, u32 = mybir.dt.float32, mybir.dt.float32r, mybir.dt.uint32
    ALU, ACT, AX = mybir.AluOpType, mybir.ActivationFunctionType, mybir.AxisListType
    ctx = ExitStack()

    def at(name, kb, shape, dt=f32):
        return nc.alloc_sbuf_tensor_at(name, shape, dt, offset=BASE + int(kb * KB))

    const_end = [CONST]

    def const(name, shape, dt=f32):
        t = nc.alloc_sbuf_tensor_at(name, shape, dt, offset=BASE + const_end[0])
        const_end[0] += (int(np.prod(shape[1:])) * 4 + 31) // 32 * 32
        assert BASE + const_end[0] <= SBUF_END, const_end
        return t

    with ctx:
        def sem(name):
            return ctx.enter_context(nc.semaphore(name))

        Uhi, Ulo = at("Uhi", 0, [P, KT, SEQ], f32r), at("Ulo", 32, [P, KT, SEQ], f32r)
        Whi = nc.alloc_sbuf_tensor_at("Whi", [P, 2, 4096], f32r, offset=BASE + RING)
        Wlo = nc.alloc_sbuf_tensor_at("Wlo", [P, 2, 4096], f32r, offset=BASE + RING + 32 * KB)
        raw = nc.alloc_sbuf_tensor_at("raw", [P, 2, 1024], f32, offset=BASE + RING + 64 * KB)
        ident = const("ident", [P, P])
        colA, colB = const("colA", [P, 96]), const("colB", [P, 88])
        mixw = const("mixw", [P, 4, P])
        relT = nc.alloc_sbuf_tensor_at("relT", [8, 32], f32, offset=BASE + const_end[0] - 2048)
        line = nc.alloc_sbuf_tensor_at("line", [8, 384], f32, offset=BASE + const_end[0] - 1536)
        walpha = const("walpha", [16, 2, P])
        causal = const("causal", [P, P])
        eps = const("eps", [P, 1])
        tiny = const("tiny", [P, 2])
        cnt = const("cnt", [P, 16])
        lam2, nlam, lame = const("lam2", [P, 2]), const("nlam", [P, 1]), const("lame", [P, 2])
        ss, rt, rs = (const(x, [P, 4]) for x in ("ss", "rt", "rs"))
        ssp, rtp, rsp = (const(x, [P, 4]) for x in ("ssp", "rtp", "rsp"))
        ssA, rtA, rsA = (const(x, [P, 32]) for x in ("ssA", "rtA", "rsA"))
        nmax, lsum, rsum, c2 = (const(x, [P, 2, 8]) for x in ("nmax", "lsum", "rsum", "c2"))
        sink, smax, sexp = const("sink", [P, 8]), const("smax", [P, 2, 8]), const("sexp", [P, 2, 8])
        decay = const("decay", [P, 2, 16])
        rowA, rowB = at("rowA", 96, [96, P]), at("rowB", 96.5, [88, P])
        lamr, lamj = at("lamr", 97, [P, 4, 64]), at("lamj", 98, [P, 2, 64])
        pT, pS, pX = at("pT", 64, [P, 4, SEQ]), at("pS", 80, [P, 4, SEQ]), at("pX", 124, [P, SEQ])
        poolhi, poollo = at("poolhi", 96, [P, 4, SEQ], f32r), at("poollo", 112, [P, 4, SEQ], f32r)
        qT = at("qT", 112, [P, 4, SEQ])
        sgA, mst = at("sgA", 64, [P, 2, SEQ]), at("mst", 72, [P, 2, SEQ])
        kTt, vt = at("kTt", 96, [P, 4, SEQ]), at("vt", 128, [P, NT, 512])
        pp, aT, dist = at("pp", 64, [P, 3, 2, SEQ]), at("aT", 88, [P, SEQ]), at("dist", 92, [P, SEQ])
        oThi, oTlo = at("oThi", 96, [P, 4, SEQ], f32r), at("oTlo", 128, [P, 4, SEQ], f32r)
        M, sgB, prB = at("M", 64, [P, KT, SEQ]), at("sgB", 112, [P, 2, SEQ]), at("prB", 120, [P, 2, SEQ])
        Hhi, Hlo = at("Hhi", 64, [P, 2, SEQ], f32r), at("Hlo", 72, [P, 2, SEQ], f32r)
        hg, hv = at("hg", 80, [P, 2, SEQ]), at("hv", 88, [P, 2, SEQ])
        acc = at("acc", 96, [P, NT, D])
        gq, gk, gv = at("gq", 64, [P, 2, SEQ]), at("gk", 72, [P, 2, SEQ]), at("gv", 80, [P, NT, 512])
        gx, gt = at("gx", 80, [P, 2, SEQ]), at("gt", 88, [P, 2, SEQ])
        rT, sq, sk = at("rT", 96, [P, 4, SEQ]), at("sq", 112, [P, 4, SEQ]), at("sk", 128, [P, SEQ])
        sv, aL, reset, kend = at("sv", 132, [P, NT, P]), at("aL", 136, [16, SEQ]), at("reset", 140, [P, SEQ]), at("kend", 136, [P, 2, SEQ])
        kendt, S, attS = at("kendt", 0, [P, NT, 256]), at("S", 8, [P, 8, 2, P]), at("attS", 16, [P, 2, 4, P])
        bias, sS, pTs = at("bias", 21, [P, 8, 256]), at("sS", 29, [P, 3, 8, 256]), at("pTs", 53, [P, 8, 2, P])
        gj = at("gj", 20, [P, P])
        sw = at("sw", 140, [P, SEQ])
        mixt = at("mixt", 136, [P, 2, 4, P])
        memhi, memlo = at("memhi", 64, [P, KT, MEM], f32r), at("memlo", 72, [P, KT, MEM], f32r)
        kC, vC, qC = at("kC", 80, [P, KT, MEM]), at("vC", 88, [P, 2, D]), at("qC", 96, [P, KT, SEQ])
        pC, pTC = at("pC", 128, [P, 2, 4, MEM]), at("pTC", 136, [P, 2, 2, HALF])

        slots = [ctx.enter_context(nc.psum_tensor(f"slot{s}", [P, SEQ], f32)) for s in range(4)]
        hd = [nc.dram_tensor(f"h{n}", (SEQ, D), f32).ap() for n in range(4)]
        m_dram = nc.dram_tensor("m_part", (D, SEQ), f32).ap()
        line_dram = nc.dram_tensor("rel_line", (P, 8, 384), f32).ap()

        loaded = [sem(f"piece_loaded{n}") for n in range(2)]
        w_hi, w_split, raw_free, dist_made = sem("weight_hi"), sem("weight_split"), sem("raw_free"), sem("dist_made")
        full = [sem(f"slot_full{s}") for s in range(4)]
        free = [sem(f"slot_free{s}") for s in range(4)]
        act_own, dve_own, pool_own = sem("act_own"), sem("dve_own"), sem("pool_own")
        consts_made, params_in, cols_in = sem("consts_made"), sem("params_in"), sem("rows_turned")
        h_loaded = [sem(f"h_loaded{n}") for n in range(NT)]
        h_stored = [sem(f"h_stored{n}") for n in range(3)]
        gains_in, post_root, h_new, pre_root, xn_done, tr_hi = (sem(x) for x in (
            "gains_in", "post_root", "h_new", "pre_root", "xn_done", "turned_hi"))
        y_scaled, acc_added = sem("post_normed"), sem("acc_added")
        out_stored = [sem(f"out_stored{n}") for n in range(2)]
        lam_sum, lam_exp, pool_ready, pool_hi = (sem(x) for x in ("lam_sum", "lam_exp", "pool_ready", "pool_hi"))
        m_stored, m_loaded, m_final, m_hi, m_lo = [sem("m_stored0"), sem("m_stored1")], sem("m_loaded"), sem("m_final"), sem("m_hi"), sem("m_lo")
        neg_max, p_exp, a_done, o_root, o_scaled, o_hi = (sem(x) for x in (
            "neg_max", "p_exp", "a_done", "o_root", "o_scaled", "o_hi"))
        conv_done, act_done, hid_prod, hid_hi, hid_lo = (sem(x) for x in ("conv_done", "gate_act", "hidden_prod", "hidden_hi", "hidden_lo"))
        g_abs, g_ln, g_cum, g_e1, g_d, g_e2, g_e3, k_end, q_dec = (sem(x) for x in (
            "gla_abs", "gla_ln", "gla_cumsum", "gla_exp_q", "gla_to_end", "gla_exp_end", "gla_exp_k",
            "k_end_done", "q_k_decayed"))
        att_ok, g_ss, g_root, g_out, states = (sem(x) for x in (
            "att_masked", "gla_squares", "gla_root", "gla_out", "states_done"))
        line_ok, line_in, bias_in, s_max, s_exp, s_sexp = (sem(x) for x in (
            "line_made", "line_stored", "bias_in", "swa_max", "swa_exp", "swa_sink_exp"))
        s_shift, keys_swapped = sem("swa_shift"), sem("keys_swapped")
        mix_t, mix_hi = sem("mix_gated"), sem("mix_hi")
        c_max, c_exp, c_norm, c_hi = (sem(x) for x in ("cross_max", "cross_exp", "cross_normed", "cross_hi"))

        plan = Plan()

        def view(x):
            return x.rearrange("(k p) n -> p k n", p=P)

        def cols(w, k0, k1, c0, step, width):
            v = view(w)
            if step:
                return (lambda i, eng: v[:, k0:k1, bass.ds(eng.snap(i * step + c0), width)]), k1 - k0, width
            return (lambda i, eng: v[:, k0:k1, c0:c0 + width]), k1 - k0, width

        def wide(w, c0):
            return [cols(w, 2 * j, 2 * j + 2, c0, 0, HALF) for j in range(4)]

        w_in, w_in2 = a["w_in"][0], a["w_in_2"][0]
        stages = {}
        loads, stores, tiles = [0] * NT, [0, 0, 0], 0

        def stage(name, n, kind, hin, xn, gpre, gpost=None, src=None, dst=None, Y=None, gnames=(), dest=None, fused=None, bufs=3):
            nonlocal tiles
            st = dict(name=name, n=n, kind=kind, src=src, dst=dst, Y=Y, gnames=gnames, dest=dest, fused=fused, first=tiles, bufs=bufs,
                      hin=at(f"hin_{name}", hin, [P, min(bufs, n), D]), xn=at(f"xn_{name}", xn, [P, 2 if dest else NT, D]),
                      gpre=at(f"gpre_{name}", gpre, [P, D]),
                      gpost=None if gpost is None else at(f"gpost_{name}", gpost, [P, D]), load={}, store={})
            for t in range(n):
                loads[t % bufs] += 1
                st["load"][t] = loads[t % bufs]
                if dst is not None:
                    stores[t % 3] += 1
                    st["store"][t] = stores[t % 3]
            st["gains"] = sum(len(s["gnames"]) for s in stages.values()) + len(gnames)
            st["posts"] = sum(s["n"] for s in stages.values() if s["kind"] == "post")
            st["news"] = sum(s["n"] for s in stages.values() if s["kind"] != "load")
            st["turns"] = sum(s["n"] for s in stages.values() if s["dest"] is not None)
            stages[name] = st
            tiles += n

        def plan_stage(st, mm=None, early=(), inner=None):
            for s in range(st["n"] + 2):
                if mm and s < st["n"]:
                    plan.group(*mm, s)
                if s == 1 and inner:
                    plan_stage(inner)
                if s == st["n"]:
                    for key in early:
                        plan.group(*key)
                if s >= 2 and st["dest"] is not None:
                    plan.group("T", st["name"], s - 2)

        U = (Uhi, Ulo)
        x_t = a["x"][0].rearrange("(t p) d -> t p d", p=P)
        hd_t = [h.rearrange("(t p) d -> t p d", p=P) for h in hd]
        mem_t = a["mem_2"][0].rearrange("(t p) d -> t p d", p=P)
        out_t = out[0].rearrange("(t p) d -> t p d", p=P)
        yM = at("yM", 64, [P, NT, D])
        y3, y4 = at("y3", 80, [P, NT, HALF]), at("y4", 64, [P, NT, HALF])
        stage("x", 8, "load", 64, 76, 84, src=x_t, gnames=("mix_pre_g",), dest=U)
        stage("mix1", 8, "post", 96, 108, 116, 120, src=x_t, dst=hd_t[0], Y=yM, gnames=("ffn_pre_g", "mix_post_g"), dest=U, fused="copy")
        stage("ffn1", 8, "post", 128, 80, 140, 88, src=hd_t[0], dst=hd_t[1], Y=acc, gnames=("norm_mix_2", "ffn_post_g"), dest=U, fused="down")
        stage("mem", 2, "load", 128, 104, 140, src=mem_t, gnames=("norm_mem_2",), dest=(memhi, memlo))
        stage("mix2", 8, "add", 112, 124, 96, src=hd_t[1], dst=hd_t[2], Y=y3, gnames=("norm_cross_2",), dest=U, fused="add")
        stage("cross", 8, "add", 112, 104, 96, src=hd_t[2], dst=hd_t[3], Y=y4, gnames=("norm_ffn_2",), dest=U, fused="add")
        stage("ffn2", 8, "add", 0, 32, 140, src=hd_t[3], Y=acc, gnames=("norm_final_2",), fused="down", bufs=8)

        UNITS = [(h, i) for h in range(4) for i in (0, 5, 1, 7, 2, 6, 3, 4)]

        def stat(u, m):
            return slice(2 * (u % 4) + m, 2 * (u % 4) + m + 1)

        def filler(u):
            c, n = (u + 2) // NT + 1, (u + 2) % NT
            if c >= 4 or (c == 1 and n % 2 == 0):
                return None
            return ("qk"[n % 2], c, n // 2)

        CU = [(hf, h) for hf in range(2) for h in range(4)]

        plan_stage(stages["x"], early=(("p", 0), ("p", 1)))
        plan.block("p", wide(w_in, 0))
        for c in range(2, 4):
            plan.group("p", c)
        plan.group("cols")
        plan.block("v", wide(w_in, 1536))
        for t in range(NT):
            plan.group("v", t)
        plan.last.update({k: (k, 3) for k in ("p", "gqk", "sq", "r")})
        plan.last.update({"v": ("v", 7), "q": ("q", 3, 3), "k": ("k", 3, 3), "gv": ("gv", 7), "misc": ("sv",)})
        plan.last.update({("gate", half, d): ("y", half, d) for half in "ab" for d in range(2)})
        plan.last.update({(n, cb): (n, cb, 7) for n in ("w_out", "w_out2", "w_o") for cb in range(2)})
        plan.last.update({(n, cb): (n, cb) for n in ("wk", "wv") for cb in range(2)})
        plan.last.update({("wq", cb): ("wq", cb, 3) for cb in range(2)})
        for n in ("f1", "f2"):
            plan.last.update({(n, "first up"): (n, "first u", 1), (n, "up"): (n, "d", 1), (n, "down"): (n, "d", 7), (n, "last down"): (n, "last d", 7)})
        hid_base = {"f1": 0, "f2": FC}
        for g in range(4):
            plan.group("pool", g)
        for half, gcol, branch in (("a", 2048, a["w_branch_a"][0]), ("b", 3072, a["w_branch_b"][0])):
            plan.loop(4, 4, 2, 4)
            for d in range(2):
                plan.block(("gate", half, d), [cols(w_in, 0, KT, gcol + P * d, 256, P), cols(branch, 0, 4, P * d, 256, P)])
                plan.group("gate", half, d)
                plan.group("y", half, d)
            plan.end()
            if half == "a":
                plan.block("q", wide(w_in, 512))
                plan.block("k", wide(w_in, 1024))
                plan.group("q", 0)
                plan.group("q", 1)
                plan.group("k", 0)
                for u in range(-2, len(UNITS)):
                    if u >= 0:
                        plan.group("aT", u)
                    if u + 2 < len(UNITS):
                        plan.group("sc", u + 2, 0)
                        plan.group("sc", u + 2, 1)
                    if u >= 0:
                        plan.group("pv", u)
                    if filler(u):
                        plan.group(*filler(u))
                for h in range(4):
                    plan.group("oT", h)

        def first_ffn(name):
            return ((name, "first g", 0), (name, "first u", 0))

        for cb in range(2):
            plan.block(("w_out", cb), wide(a["w_out"][0], cb * HALF))
        for t in range(NT):
            plan.group("w_out", 0, t)
        plan_stage(stages["mix1"], ("w_out", 1), first_ffn("f1"))

        PAIRS = FC // 2

        def plan_ffn(name, up_src, down, st, early):
            plan.block((name, "first up"), [cols(w, 4 * j, 4 * j + 4, c0, 0, 256) for w, c0 in up_src for j in range(2)])
            plan.group(name, "first g", 1)
            plan.group(name, "first u", 1)
            plan.loop(PAIRS - 1, 12, 2, 6)
            plan.block((name, "up"), [cols(w, 4 * j, 4 * j + 4, c0 + 256, 256, 256) for w, c0 in up_src for j in range(2)])
            for c in range(2):
                plan.group(name, "g", c)
                plan.group(name, "u", c)
            dv = down.rearrange("(c p) n -> p c n", p=P)
            plan.block((name, "down"), [((lambda i, eng, j=j: dv[:, bass.ds(eng.snap(i * 2 + j), 1), :]), 1, D) for j in range(2)])
            for t in range(NT):
                plan.group(name, "d", t)
            plan.end()
            plan.block((name, "last down"), [((lambda i, eng, j=j: dv[:, FC - 2 + j:FC - 1 + j, :]), 1, D) for j in range(2)])
            plan_stage(st, (name, "last d"), early)

        plan_ffn("f1", ((a["w_ffn_gate"][0], 0), (a["w_ffn_up"][0], 0)), a["w_ffn_down"][0], stages["ffn1"], (("ga",), ("sk",)))
        plan.block("misc", [cols(w_in2, 0, KT, 1536, 0, P), cols(w_in2, 0, 4, 2064, 0, 256), cols(w_in2, 4, KT, 2064, 0, 256)])
        plan.block("gqk", wide(w_in2, 0))
        plan.group("sv")
        for c in range(4):
            plan.group("gqk", c)
        plan.group("svT")
        plan.group("alpha", 0)
        plan.group("alpha", 1)
        plan.block("sq", wide(w_in2, 1552))
        plan.block("r", wide(w_in2, 1024))
        plan.block("gv", wide(w_in2, 512))
        for key in ("sq", "r"):
            for c in range(4):
                plan.group(key, c)
        for t in range(NT):
            plan.group("gv", t)
        for j in range(2):
            plan.group("kendT", j)
        for t in range(-2, NT):
            if 0 <= t + 1 < NT:
                plan.group("att", t + 1)
            if t + 2 < NT:
                plan.group("ssc", t + 2, 0)
                plan.group("ssc", t + 2, 1)
            if 0 <= t + 1 < NT and t % 2:
                plan.group("kv", (t + 1) // 2)
            if t >= 0:
                plan.group("spT", t, 0)
                plan.group("spT", t, 1)
                plan.group("go", t)
                plan.group("so", t)
        for cb in range(2):
            plan.block(("w_out2", cb), wide(a["w_out_2"][0], cb * HALF))
        for t in range(-2, NT):
            if t + 2 < NT:
                plan.group("mixT", t + 2)
            if t >= 0:
                plan.group("w_out2", 0, t)
        plan_stage(stages["mix2"], ("w_out2", 1), (("wk", 0),), stages["mem"])
        CROSS = (("wk", 0), ("wq", 0), ("wv", 0), ("wq", 1), ("wk", 1), ("wv", 1))
        for key, cb in CROSS:
            plan.block((key, cb), wide(a[{"wk": "w_k_c_2", "wq": "w_q_c_2", "wv": "w_v_c_2"}[key]][0], cb * HALF))
            if key == "wq":
                for c in range(4):
                    plan.group(key, cb, c)
            elif (key, cb) not in (("wk", 0), ("wv", 1)):
                plan.group(key, cb)
        for cb in range(2):
            plan.block(("w_o", cb), wide(a["w_o_c_2"][0], cb * HALF))
        for u in range(-2, len(CU)):
            if u >= 0:
                plan.group("cT", u)
            if u + 2 < len(CU):
                plan.group("cs", u + 2)
            if u == -1:
                plan.group("wv", 1)
            if u >= 0:
                plan.group("co", u)
            if u >= 4:
                plan.group("w_o", 0, u - 4)
        for t in range(4, NT):
            plan.group("w_o", 0, t)
        plan_stage(stages["cross"], ("w_o", 1), first_ffn("f2"))
        plan_ffn("f2", ((a["w_up_2"][0], 0), (a["w_up_2"][0], F)), a["w_down_2"][0], stages["ffn2"], ())

        def slot(*key):
            return slots[plan.slot(key)]

        def wait_full(eng, *key, i=0):
            eng.wait_ge(full[plan.slot(key)], plan.uses(key, i) + 1)

        def wait_freed(eng, *key, i=0):
            eng.wait_ge(free[plan.slot(key)], plan.uses(key, i) + 1)

        def freed(ins, *key):
            ins.then_inc(free[plan.slot(key)], 1)

        block = ctx.enter_context(nc.Block())

        @block.sync
        def _(sp):
            def load(src, n, w, p, i, per):
                s = p % 2
                src = src(i, sp)
                if p >= 2 or per:
                    sp.wait_ge(w_split, i * per + p - 1)
                    sp.sem_inc(raw_free, 1)
                sp.dma_start(raw[:, s, 0:n * w].rearrange("p (k c) -> p k c", k=n), src).then_inc(loaded[s], 16)

            cw, cb = a["conv_w_2"][0], a["conv_b_2"][0]
            params = [(rowA[0:44, :], cw[0].rearrange("(r c) -> r c", c=P)), (rowA[44:88, :], cw[1].rearrange("(r c) -> r c", c=P)),
                      (rowA[88:92, :], a["pool_scale"][0].rearrange("(r c) -> r c", c=P)), (rowA[92:93, :], a["subln_g"]),
                      (rowA[93:94, :], a["gla_gain_2"]), (rowA[94:96, :], a["b_alpha_2"][0].rearrange("(r c) -> r c", c=P)),
                      (rowB[0:44, :], cw[2].rearrange("(r c) -> r c", c=P)), (rowB[44:88, :], cb.rearrange("(r c) -> r c", c=P)),
                      (mixw[:, :, :], a["pool_mix"][0].rearrange("g c d -> c g d")),
                      (walpha[:, :, :], a["w_alpha_2"][0].rearrange("r (h c) -> r h c", c=P)),
                      (sink[:, :], a["sinks_2"][0].partition_broadcast(P))]
            params += [(lamr[:, n, :], a[x][0].partition_broadcast(P)) for n, x in enumerate(("lam_q1", "lam_k1", "lam_q2", "lam_k2"))]
            assert len(params) == N_PARAMS

            p = 0
            for entry in plan.stream:
                if isinstance(entry[0], int):
                    trips, body = entry
                    per = sum(len(pieces) for _, pieces in body)
                    with sp.Fori(0, trips) as i:
                        q = p
                        for _, pieces in body:
                            for src, n, w in pieces:
                                load(src, n, w, q, i, per)
                                q += 1
                    p += trips * per
                else:
                    for src, n, w in entry[1]:
                        if p == 2:
                            for dst, row in params:
                                sp.dma_start(dst, row).then_inc(params_in, 16)
                        load(src, n, w, p, 0, 0)
                        p += 1

        @block.gpsimd
        def _(pool):
            own = Chain(pool, pool_own)
            own(pool.memset(ident[:, :], 0.0))
            pool.affine_select(out=ident[:, :], in_=ident[:, :], compare_op=ALU.not_equal, fill=1.0, base=0,
                               pattern=[[-1, P]], channel_multiplier=1).then_inc(consts_made, 1)
            pool.memset(eps[:, :], EPS).then_inc(consts_made, 1)
            own(pool.memset(causal[:, :], 1.0))
            own(pool.affine_select(out=causal[:, :], in_=causal[:, :], compare_op=ALU.is_ge, fill=0.0, base=0,
                                   pattern=[[1, P]], channel_multiplier=-1))
            pool.memset(causal[0:64, 64:128], 0.0).then_inc(consts_made, 1)
            own(pool.iota(cnt[:, :], pattern=[[1, 16]], base=1, channel_multiplier=0, allow_small_or_imprecise_dtypes=True))
            own(pool.memset(tiny[:, :], 1.0))

            def split(key, dst, first, n, p, b, i, per):
                s = p % 2
                if first and plan.reader(key):
                    group, trip = plan.reader(key)
                    count = plan.uses(group, i) + 1 - plan.groups[group][1] // 4 if trip is None else plan.uses(group, trip) + 1
                    pool.wait_ge(full[plan.slot(group)], count)
                pool.wait_ge(loaded[s], i * (per * 8) + 16 * (p // 2 + 1))
                pool.tensor_tensor(tiny[:, 1:2], tiny[:, 0:1], tiny[:, 0:1], ALU.mult)
                hi, lo = Whi[:, b % 2, dst:dst + n], Wlo[:, b % 2, dst:dst + n]
                pool.tensor_scalar(hi, raw[:, s, 0:n], 1.0, 1.0, ALU.mult, ALU.mult).then_inc(w_hi, 1)
                pool.wait_ge(w_hi, i * per + p + 1)
                pool.tensor_tensor(lo, raw[:, s, 0:n], hi.bitcast(f32), ALU.subtract).then_inc(w_split, 1)

            def make_dist():
                wait_full(pool, "pool", 3)
                own(pool.iota(dist[:, :], pattern=[[1, SEQ]], base=-(SEQ - P), channel_multiplier=-1, allow_small_or_imprecise_dtypes=True))
                pool.affine_select(out=dist[:, :], in_=dist[:, :], compare_op=ALU.is_ge, fill=NEG, base=SEQ - P,
                                   pattern=[[-1, SEQ]], channel_multiplier=1).then_inc(dist_made, 1)

            def add_post(st):
                for t in range(NT):
                    pool.wait_ge(h_loaded[t % st["bufs"]], 16 * st["load"][t])
                    pool.wait_ge(y_scaled, t + 1)
                    h = st["hin"][:, t % st["bufs"], :]
                    pool.tensor_tensor(h, h, st["Y"][:, t, :], ALU.add).then_inc(h_new, 1)

            def add_sum(st):
                for t in range(NT):
                    wait_freed(pool, "f2", "d", t, i=PAIRS - 2)
                    pool.wait_ge(h_loaded[t % st["bufs"]], 16 * st["load"][t])
                    h = st["hin"][:, t % st["bufs"], :]
                    pool.tensor_tensor(h, h, acc[:, t, :], ALU.add).then_inc(acc_added, 1)

            def run(blocks, p, b, i, per):
                for key, pieces in blocks:
                    if key == "gqk":
                        add_post(stages["ffn1"])
                    dst = 0
                    for j, (_, n, w) in enumerate(pieces):
                        split(key, dst, j == 0, n * w, p, b, i, per)
                        dst += n * w
                        p += 1
                    b += 1
                    if key == "k":
                        make_dist()
                return p, b

            p = b = 0
            for entry in plan.stream:
                if isinstance(entry[0], int):
                    trips, body = entry
                    per = sum(len(pieces) for _, pieces in body)
                    with pool.Fori(0, trips) as i:
                        run(body, p, b, i, per)
                    p, b = p + trips * per, b + trips * len(body)
                else:
                    p, b = run([entry], p, b, 0, 0)
            add_sum(stages["ffn2"])

        @block.tensor
        def _(pe):
            def begin(*key, i=0):
                if plan.groups[key][0] >= 4 or plan.groups[key][1]:
                    pe.wait_ge(free[plan.slot(key)], plan.uses(key, i))
                return slots[plan.slot(key)]

            def done(ins, *key):
                ins.then_inc(full[plan.slot(key)], 1)

            def weights(key, i=0):
                b, p, n, bper, pper = plan.blocks[key]
                pe.wait_ge(w_split, i * pper + p + n if pper else p + n)
                return Whi[:, b % 2, :], Wlo[:, b % 2, :]

            def mm3(o, l, r, start, stop):
                for j, (x, y) in enumerate(((0, 0), (0, 1), (1, 0))):
                    ins = pe.matmul(o, lhsT=l[x], rhs=r[y], start=start and j == 0, stop=stop and j == 2)
                return ins

            def pair(t, *idx):
                return tuple(x[idx] for x in t)

            def turn(o, src):
                return pe.transpose(o, src, ident[:, :])

            def half(w, off, width, c, src, o, hf, n=KT):
                wv = tuple(x[:, off:off + n * width].rearrange("p (k c) -> p k c", k=n) for x in w)
                ts = slice(hf * HALF, hf * HALF + HALF)
                for k in range(n):
                    ins = mm3(o[:, ts], pair(wv, slice(None), k, slice(c, c + P)), pair(src, slice(None), k, ts), k == 0, k == n - 1)
                return ins

            def features(w, off, width, c, src, key, i=0, n=KT):
                o = begin(*key, i=i)
                half(w, off, width, c, src, o, 0, n)
                return half(w, off, width, c, src, o, 1, n)

            def quarter(w, c, src, o, n):
                wv = tuple(x.rearrange("p (k c) -> p k c", k=KT) for x in w)
                for k in range(KT):
                    ins = mm3(o[:, 0:256], pair(wv, slice(None), k, slice(c, c + P)), pair(src, slice(None), k, slice(256 * n, 256 * n + 256)),
                              k == 0, k == KT - 1)
                return ins

            def early_halves(name, block_key, parts):
                def start(j):
                    def f(o):
                        if j == 0:
                            for t in range(NT // 2):
                                wait_freed(pe, "T", name, t)
                        half(weights(block_key), *parts[j][1:], U, o, 0)
                    return parts[j][0], f

                def finish():
                    u_ready(name)
                    for key, *where in parts:
                        done(half(weights(block_key), *where, U, slot(*key), 1), *key)

                return [start(0), start(1)], finish

            def tokens(w, t, src, o, made=None):
                wv = tuple(x.rearrange("p (k c) -> p k c", k=KT) for x in w)
                for k in range(KT):
                    if made:
                        pe.wait_ge(made, k + 1)
                    ins = mm3(o, pair(src, slice(None), k, slice(t * P, t * P + P)), pair(wv, slice(None), k), k == 0, k == KT - 1)
                return ins

            def wide_features(key, src, block_key=None, first=0):
                w = weights(block_key or key[0])
                for c in range(first, 4):
                    k = (*key, c)
                    done(features(w, 0, HALF, c * P, src, k), *k)

            def run_stage(st, mm=None, product=None, early=(), inner=None):
                n = st["n"]
                for s in range(n + 2):
                    if mm and s < n:
                        key = (*mm, s)
                        done(product(s, begin(*key)), *key)
                    if s == 1 and inner:
                        run_stage(inner)
                    if s == n:
                        for key, start in early:
                            start(begin(*key))
                    t = s - 2
                    if t >= 0 and st["dest"] is not None:
                        pe.wait_ge(xn_done, st["first"] + t + 1)
                        o = begin("T", st["name"], t)
                        for k in range(KT):
                            ins = turn(o[:, k * P:k * P + P], st["xn"][:, t % 2, k * P:k * P + P])
                        done(ins, "T", st["name"], t)

            def u_ready(name, n=NT):
                for t in range(n):
                    wait_freed(pe, "T", name, t)

            def first_up(name, st):
                return early_halves(st, (name, "first up"), [((name, "first g", 0), 0, 256, 0), ((name, "first u", 0), 2048, 256, 0)])

            def ffn(name, st, early):
                def up(w, gate, value, i=0, first=0):
                    for c in range(first, 2):
                        for j, part in enumerate((gate, value)):
                            done(features(w, 2048 * j, 256, c * P, U, (name, part, c), i), name, part, c)

                def down_weights(part, i=0):
                    return tuple(x[:, 0:2 * D].rearrange("p (c n) -> p c n", c=2) for x in weights((name, part), i))

                def down(w, t, o, split=None):
                    for c in range(2):
                        if split is not None:
                            pe.wait_ge(hid_lo, split + c + 1)
                        for half in range(2):
                            cs = slice(half * HALF, half * HALF + HALF)
                            ins = mm3(o[:, cs], (Hhi[:, c, t * P:t * P + P], Hlo[:, c, t * P:t * P + P]),
                                      pair(w, slice(None), c, cs), c == 0, c == 1)
                    return ins

                base = hid_base[name]
                up(weights((name, "first up")), "first g", "first u", first=1)
                with pe.Fori(0, PAIRS - 1) as i:
                    up(weights((name, "up"), i), "g", "u", i)
                    w = down_weights("down", i)
                    pe.wait_ge(hid_lo, i * 2 + base + 2)
                    for t in range(NT):
                        done(down(w, t, begin(name, "d", t, i=i)), name, "d", t)
                w = down_weights("last down")
                run_stage(st, (name, "last d"), lambda t, o: down(w, t, o, base + FC - 2 if t == 0 else None), early)

            pe.wait_ge(consts_made, 3)
            early, finish = early_halves("x", "p", [(("p", c), 0, HALF, c * P) for c in range(2)])
            run_stage(stages["x"], early=early)
            finish()
            wide_features(("p",), U, first=2)
            pe.wait_ge(params_in, 16 * N_PARAMS)
            o = begin("cols")
            pe.transpose(o[:, 0:96], rowA[:, :], ident[0:96, 0:96])
            done(pe.transpose(o[:, HALF:HALF + 88], rowB[:, :], ident[0:88, 0:88]), "cols")
            w = weights("v")
            for t in range(NT):
                done(tokens(w, t, U, begin("v", t)[:, 0:HALF]), "v", t)
            for g in range(4):
                pe.wait_ge(pool_ready, g + 1)
                o = begin("pool", g)
                for hf in range(2):
                    ins = pe.matmul(o[:, hf * HALF:hf * HALF + HALF], lhsT=mixw[:, g, :],
                                    rhs=pS[:, g, hf * HALF:hf * HALF + HALF], start=True, stop=True)
                done(ins, "pool", g)

            def gates(half, src):
                with pe.Fori(0, 4) as i:
                    for d in range(2):
                        w = weights(("gate", half, d), i)
                        done(features(w, 0, P, 0, U, ("gate", half, d), i), "gate", half, d)
                        done(features(w, D, P, 0, src, ("y", half, d), i, n=4), "y", half, d)

            for g in range(4):
                wait_freed(pe, "pool", g)
            gates("a", (poolhi, poollo))
            for name, c in (("q", 0), ("q", 1), ("k", 0)):
                done(features(weights(name), 0, HALF, c * P, U, (name, c)), name, c)
            for name in ("q", "k"):
                wait_freed(pe, name, 0)
            for t in range(NT):
                wait_freed(pe, "v", t)
            for u in range(-2, len(UNITS)):
                if u >= 0:
                    h, i = UNITS[u]
                    pe.wait_ge(a_done, u + 1)
                    o = begin("aT", u)
                    for j in range(i + 1):
                        ins = turn(o[:, j * P:j * P + P], pp[:, u % 3, 0, j * P:j * P + P])
                    done(ins, "aT", u)
                if u + 2 < len(UNITS):
                    h, i = UNITS[u + 2]
                    if h and (u + 2) % NT == 0:
                        for f in range(u - NT, u):
                            if filler(f):
                                wait_freed(pe, *filler(f))
                        if h == 1:
                            wait_freed(pe, "q", 1)
                    for m in range(2):
                        o = begin("sc", u + 2, m)
                        r = slice(64 * m, 64 * m + 64)
                        for c0 in range(0, P * (i + 1), HALF):
                            c1 = min(c0 + HALF, P * (i + 1))
                            ins = pe.matmul(o[:, c0:c1], lhsT=qT[r, h, i * P:i * P + P], rhs=kTt[r, h, c0:c1], start=True, stop=True)
                        done(ins, "sc", u + 2, m)
                if u >= 0:
                    h, i = UNITS[u]
                    wait_freed(pe, "aT", u)
                    o = begin("pv", u)
                    for j in range(i + 1):
                        ins = pe.matmul(o[:, 0:P], lhsT=aT[:, j * P:j * P + P], rhs=vt[:, j, h * P:h * P + P],
                                        start=j == 0, stop=j == i)
                    done(ins, "pv", u)
                if filler(u):
                    name, c, n = filler(u)
                    done(quarter(weights(name), c * P, U, begin(name, c, n), n), name, c, n)
            for h in range(4):
                pe.wait_ge(o_scaled, h + 1)
                o = begin("oT", h)
                for i in range(NT):
                    ins = turn(o[:, i * P:i * P + P], qT[:, h, i * P:i * P + P])
                done(ins, "oT", h)
            for h in range(4):
                wait_freed(pe, "oT", h)
            gates("b", (oThi, oTlo))
            w = weights(("w_out", 0))
            for t in range(NT):
                done(tokens(w, t, U, begin("w_out", 0, t)[:, 0:HALF], m_lo if t == 0 else None), "w_out", 0, t)
            w = weights(("w_out", 1))
            early, finish = first_up("f1", "mix1")
            run_stage(stages["mix1"], ("w_out", 1), lambda t, o: tokens(w, t, U, o[:, 0:HALF]), early)
            finish()
            early, finish = early_halves("ffn1", "misc", [(("ga",), 0, P, 0), (("sk",), D, 256, 0)])
            ffn("f1", stages["ffn1"], early)
            finish()
            w = weights("misc")
            done(features(w, D, 256, P, U, ("sv",)), "sv")
            wide_features(("gqk",), U)
            wait_freed(pe, "sv")
            o = begin("svT")
            for t in range(NT):
                ins = turn(o[:, t * P:t * P + P], rT[:, 0, t * P:t * P + P])
            done(ins, "svT")
            wait_freed(pe, "ga")
            for hp in range(2):
                o = begin("alpha", hp)
                for hf in range(2):
                    ins = pe.matmul(o[:, hf * HALF:hf * HALF + HALF], lhsT=walpha[:, hp, :],
                                    rhs=aL[:, hf * HALF:hf * HALF + HALF], start=True, stop=True)
                done(ins, "alpha", hp)
            wide_features(("sq",), U)
            wide_features(("r",), U)
            w = weights("gv")
            for t in range(NT):
                done(tokens(w, t, U, begin("gv", t)[:, 0:HALF]), "gv", t)
            pe.wait_ge(q_dec, 1)
            for j in range(2):
                o = begin("kendT", j)
                for tt in range(4):
                    for hp in range(2):
                        t = 4 * j + tt
                        c = tt * 256 + hp * P
                        ins = turn(o[:, c:c + P], kend[:, hp, t * P:t * P + P])
                done(ins, "kendT", j)
            for j in range(2):
                wait_freed(pe, "kendT", j)
            for t in range(NT):
                wait_freed(pe, "gv", t)
            pe.wait_ge(keys_swapped, 32)
            for t in range(-2, NT):
                if 0 <= t + 1 < NT:
                    n = t + 1
                    o = begin("att", n)
                    for h in range(4):
                        hp, hh = h // 2, h % 2
                        r = slice(64 * hh, 64 * hh + 64)
                        c = hh * HALF + hp * P
                        ins = pe.matmul(o[:, c:c + P], lhsT=gk[r, hp, n * P:n * P + P], rhs=gq[r, hp, n * P:n * P + P], start=True, stop=True)
                    done(ins, "att", n)
                if t + 2 < NT:
                    n = t + 2
                    k0 = max(n - 1, 0) * P
                    off = P if n == 0 else 0
                    for g in range(2):
                        o = begin("ssc", n, g)
                        for hh in range(2):
                            r = slice(64 * hh, 64 * hh + 64)
                            keys = sk if hh == g else sw
                            for c in range(2):
                                c1 = hh * HALF + c * 256
                                ins = pe.matmul(o[:, c1 + off:c1 + 256], lhsT=sq[r, 2 * g + c, n * P:n * P + P],
                                                rhs=keys[r, k0:n * P + P], start=True, stop=True)
                        done(ins, "ssc", n, g)
                if 0 <= t + 1 < NT and t % 2:
                    n = t + 1
                    o = begin("kv", n // 2)
                    for tt in range(2):
                        for par in range(2):
                            r = slice(64 * par, 64 * par + 64)
                            for h in range(4):
                                hp, hh = h // 2, h % 2
                                c = par * HALF + tt * 256 + hp * P
                                ins = pe.matmul(o[64 * hh:64 * hh + 64, c:c + P], lhsT=kendt[r, n + tt, h * 64:h * 64 + 64],
                                                rhs=gv[r, n + tt, h * P:h * P + P], start=True, stop=True)
                    done(ins, "kv", n // 2)
                if t >= 0:
                    kts = (1,) if t == 0 else (0, 1)
                    pe.wait_ge(s_exp, 8 * (t + 1))
                    for g in range(2):
                        o = begin("spT", t, g)
                        for c in range(4):
                            for kt in kts:
                                cc = c * 256 + kt * P
                                ins = turn(o[:, cc:cc + P], sS[:, t % 3, 4 * g + c, kt * P:kt * P + P])
                        done(ins, "spT", t, g)
                    pe.wait_ge(states, 2 * t + 1)
                    pe.wait_ge(att_ok, 2 + t + 1)
                    o = begin("go", t)
                    for h in range(4):
                        hp, hh = h // 2, h % 2
                        r = slice(64 * hh, 64 * hh + 64)
                        c = hh * HALF + hp * P
                        ins = pe.matmul(o[:, c:c + P], lhsT=attS[:, t % 2, h, :], rhs=gv[:, t, h * P:h * P + P], start=True, stop=False,
                                        skip_group_check=True)
                        for par in range(2):
                            n = 2 * t + par
                            if n:
                                ins = pe.matmul(o[64 * par:64 * par + 64, c:c + P], lhsT=gq[r, hp, n * 64:n * 64 + 64],
                                                rhs=S[r, n % 8, hp, :], start=False, stop=par == 1, skip_group_check=True)
                    done(ins, "go", t)
                    o = begin("so", t)
                    for g in range(2):
                        wait_freed(pe, "spT", t, g)
                        for c in range(4):
                            h = 4 * g + c
                            for kt in kts:
                                ins = pe.matmul(o[:, h * 64:h * 64 + 64], lhsT=pTs[:, h, kt, :],
                                                rhs=sv[:, t - 1 + kt, g * 64:g * 64 + 64], start=kt == kts[0], stop=kt == 1)
                    done(ins, "so", t)
            w = weights(("w_out2", 0))
            for t in range(-2, NT):
                if t + 2 < NT:
                    n = t + 2
                    pe.wait_ge(g_out, n + 1)
                    wait_freed(pe, "so", n)
                    if n == 0:
                        wait_freed(pe, "so", NT - 1)
                    o = begin("mixT", n)
                    for k in range(4):
                        turn(o[:, k * P:k * P + P], gv[:, n, k * P:k * P + P])
                    for k in range(4):
                        ins = turn(o[:, HALF + k * P:HALF + k * P + P], sq[:, k, n * P:n * P + P])
                    done(ins, "mixT", n)
                if t >= 0:
                    wait_freed(pe, "mixT", t)
                    done(tokens(w, t, U, begin("w_out2", 0, t)[:, 0:HALF]), "w_out2", 0, t)
            w = weights(("w_out2", 1))


            def memory_keys(cb):
                def f(o):
                    if cb == 0:
                        u_ready("mem", 2)
                    wv = tuple(x.rearrange("p (k c) -> p k c", k=KT) for x in weights(("wk", cb)))
                    for c in range(4):
                        for k in range(KT):
                            ins = mm3(o[:, c * MEM:c * MEM + MEM], pair(wv, slice(None), k, slice(c * P, c * P + P)),
                                      (memhi[:, k, :], memlo[:, k, :]), k == 0, k == KT - 1)
                    done(ins, "wk", cb)
                return ("wk", cb), f

            run_stage(stages["mix2"], ("w_out2", 1), lambda t, o: tokens(w, t, U, o[:, 0:HALF]), [memory_keys(0)],
                      stages["mem"])
            u_ready("mix2")
            def memory_values(cb):
                w = weights(("wv", cb))
                o = begin("wv", cb)
                for t in range(2):
                    ins = tokens(w, t, (memhi, memlo), o[:, t * HALF:t * HALF + HALF])
                done(ins, "wv", cb)

            for key, cb in CROSS[1:-1]:
                if key == "wq":
                    wide_features((key, cb), U, (key, cb))
                elif key == "wk":
                    memory_keys(cb)[1](begin(key, cb))
                else:
                    memory_values(cb)
            for cb in range(2):
                wait_freed(pe, "wk", cb)
                for c in range(4):
                    wait_freed(pe, "wq", cb, c)
            for u in range(-2, len(CU)):
                if u >= 0:
                    pe.wait_ge(c_norm, u + 1)
                    o = begin("cT", u)
                    for kt in range(2):
                        for j in range(4):
                            c = kt * HALF + j * P
                            ins = turn(o[:, c:c + P], pC[:, u % 2, j, kt * P:kt * P + P])
                    done(ins, "cT", u)
                if u + 2 < len(CU):
                    hf, h = CU[u + 2]
                    o = begin("cs", u + 2)
                    for j in range(4):
                        t = 4 * hf + j
                        for k in range(2):
                            ins = pe.matmul(o[:, j * MEM:j * MEM + MEM], lhsT=qC[:, 2 * h + k, t * P:t * P + P],
                                            rhs=kC[:, 2 * h + k, :], start=k == 0, stop=k == 1)
                    done(ins, "cs", u + 2)
                if u == -1:
                    memory_values(1)
                if u >= 0:
                    hf, h = CU[u]
                    if u == 0:
                        for cb in range(2):
                            wait_freed(pe, "wv", cb)
                    wait_freed(pe, "cT", u)
                    o = begin("co", u)
                    for dt in range(2):
                        for kt in range(2):
                            f0 = h * 256 + dt * P
                            ins = pe.matmul(o[:, dt * HALF:dt * HALF + HALF], lhsT=vC[:, kt, f0:f0 + P],
                                            rhs=pTC[:, u % 2, kt, :], start=kt == 0, stop=kt == 1)
                    done(ins, "co", u)
                if u >= 4:
                    if u == 4:
                        for v in range(4):
                            wait_freed(pe, "co", v)
                    done(tokens(weights(("w_o", 0)), u - 4, U, begin("w_o", 0, u - 4)[:, 0:HALF]), "w_o", 0, u - 4)
            for u in range(4, len(CU)):
                wait_freed(pe, "co", u)
            w = weights(("w_o", 0))
            for t in range(4, NT):
                done(tokens(w, t, U, begin("w_o", 0, t)[:, 0:HALF]), "w_o", 0, t)
            w = weights(("w_o", 1))
            early, finish = first_up("f2", "cross")
            run_stage(stages["cross"], ("w_o", 1), lambda t, o: tokens(w, t, U, o[:, 0:HALF]), early)
            finish()
            ffn("f2", stages["ffn2"], ())

        @block.scalar
        def _(act):
            own = Chain(act, act_own)

            def load_h(st, t):
                b = t % st["bufs"]
                if t >= st["bufs"]:
                    act.wait_ge(xn_done, st["first"] + t - 2)
                    if st["dst"] is not None:
                        act.wait_ge(h_stored[b], 16 * st["store"][t - 3])
                act.dma_start(st["hin"][:, b, :], st["src"][t]).then_inc(h_loaded[b], 16)

            def begin_stage(st):
                load_h(st, 0)
                gains = (st["gpre"], st["gpost"])
                for g, name in zip(gains, st["gnames"]):
                    v = a[name] if name == "norm_final_2" else a[name][0]
                    act.dma_start(g[:, :], v.partition_broadcast(P)).then_inc(gains_in, 16)
                for t in range(1, min(st["n"], st["bufs"])):
                    load_h(st, t)

            def run_stage(st, mm=None):
                n, hin, xn, Y = st["n"], st["hin"], st["xn"], st["Y"]
                nx = 2 if st["dest"] else NT
                for s in range(n + 2):
                    if s < n and st["kind"] == "post":
                        if st["fused"] == "copy":
                            wait_full(act, *mm, s)
                            wait_freed(act, mm[0], 0, s)
                            freed(act.activation(Y[:, s, HALF:D], slot(*mm, s)[:, 0:HALF], ACT.Copy), *mm, s)
                            wait_freed(act, *mm, s)
                        else:
                            wait_freed(act, *mm, s)
                        if s >= 2:
                            act.wait_ge(xn_done, st["first"] + s - 1)
                            wait_full(act, "T", st["name"], s - 2)
                        own(act.activation(xn[:, s % 2, :], Y[:, s, :], ACT.Square, accum_out=ssp[:, s % 4:s % 4 + 1]))
                        if s >= 4:
                            act.wait_ge(h_new, st["news"] + s - 3)
                        act.activation(rtp[:, s % 4:s % 4 + 1], ssp[:, s % 4:s % 4 + 1], ACT.Sqrt, bias=eps[:, :], scale=1.0 / D).then_inc(post_root, 1)
                    t = s - 1
                    if 0 <= t < n:
                        b = t % st["bufs"]
                        if st["kind"] == "load":
                            act.wait_ge(h_loaded[b], 16 * st["load"][t])
                        else:
                            act.wait_ge(h_new, st["news"] + t + 1)
                            if st["dst"] is not None:
                                act.dma_start(st["dst"][t], hin[:, b, :]).then_inc(h_stored[t % 3], 16)
                        if t >= 2:
                            if st["dest"] is not None:
                                wait_full(act, "T", st["name"], t - 2)
                        own(act.activation(xn[:, t % nx, :], hin[:, b, :], ACT.Square, accum_out=ss[:, t % 4:t % 4 + 1]))
                        if t >= 4:
                            act.wait_ge(xn_done, st["first"] + t - 3)
                        act.activation(rt[:, t % 4:t % 4 + 1], ss[:, t % 4:t % 4 + 1], ACT.Sqrt, bias=eps[:, :], scale=1.0 / D).then_inc(pre_root, 1)
                    t = s - 2
                    if t >= 0:
                        if st["dest"] is not None:
                            wait_full(act, "T", st["name"], t)
                            act.activation(st["dest"][0][:, :, t * P:t * P + P],
                                           slot("T", st["name"], t)[:, :].rearrange("p (k c) -> p k c", k=KT), ACT.Copy).then_inc(tr_hi, 1)
                        else:
                            act.wait_ge(xn_done, st["first"] + t + 1)
                            act.dma_start(out_t[t], xn[:, t % nx, :]).then_inc(out_stored[t % 2], 16)
                    if st["bufs"] <= s + 1 < n:
                        load_h(st, s + 1)
                if st["dst"] is not None:
                    for t in range(n - 3, n):
                        act.wait_ge(h_stored[t % 3], 16 * st["store"][t])

            def copy_out(dst, src, key, scale=1.0):
                wait_full(act, *key)
                freed(act.activation(dst, src, ACT.Copy, scale=scale), *key)

            def first_half(name, Y, start=0, end=NT):
                for t in range(start, end):
                    copy_out(Y[:, t, 0:HALF], slot(name, 0, t)[:, 0:HALF], (name, 0, t))

            begin_stage(stages["x"])
            act.wait_ge(consts_made, 2)
            own(act.activation(rtA[:, 0:1], eps[:, :], ACT.Sqrt))
            for s in m_stored:
                act.sem_inc(s, 16)
            act.wait_ge(consts_made, 3)
            run_stage(stages["x"])
            for c in range(4):
                copy_out(pT[:, c, :], slot("p", c)[:, :], ("p", c))
            wait_full(act, "cols")
            act.activation(colA[:, :], slot("cols")[:, 0:96], ACT.Copy).then_inc(cols_in, 1)
            freed(act.activation(colB[:, :], slot("cols")[:, HALF:HALF + 88], ACT.Copy), "cols")
            act.wait_ge(lam_sum, 2)
            act.activation(lame[:, :], lam2[:, :], ACT.Exp).then_inc(lam_exp, 1)
            for t in range(NT):
                copy_out(vt[:, t, :], slot("v", t)[:, 0:HALF], ("v", t))
            act.wait_ge(cols_in, 1)
            for g in range(4):
                wait_full(act, "pool", g)
                act.activation(poolhi[:, g, :], slot("pool", g)[:, :], ACT.Copy, scale=colA[:, 88 + g:89 + g]).then_inc(pool_hi, 1)

            with act.Fori(0, 4) as i:
                for d in range(2):
                    wait_full(act, "gate", "a", d, i=i)
                    act.wait_ge(free[plan.slot(("y", "a", d))], plan.uses(("y", "a", d), i))
                    freed(act.activation(sgA[:, d, :], slot("gate", "a", d)[:, :], ACT.Sigmoid), "gate", "a", d)
                    wait_freed(act, "y", "a", d, i=i)
                    act.dma_start(m_dram[bass.ds(i * 256 + d * P, P), :], mst[:, d, :]).then_inc(m_stored[d], 16)
            for c in range(2):
                copy_out(qT[:, c, :], slot("q", c)[:, :], ("q", c), scale=0.125)
            copy_out(kTt[:, 0, :], slot("k", 0)[:, :], ("k", 0))
            for d in range(2):
                act.wait_ge(m_stored[d], 16 * 5)
            for u in range(-2, len(UNITS)):
                if u >= 0:
                    h, i = UNITS[u]
                    w = P * (i + 1)
                    if u >= 1:
                        wait_full(act, "pv", u - 1)
                    copy_out(aT[:, 0:w], slot("aT", u)[:, 0:w], ("aT", u))
                if u + 2 < len(UNITS):
                    n = u + 2
                    w = P * (UNITS[n][1] + 1)
                    for m in range(2):
                        act.wait_ge(neg_max, 2 * n + m + 1)
                        act.activation(pp[:, n % 3, m, 0:w], pp[:, n % 3, m, 0:w], ACT.Exp, bias=nmax[:, 0, stat(n, m)],
                                       accum_out=lsum[:, 0, stat(n, m)]).then_inc(p_exp, 1)
                if u >= 0:
                    wait_full(act, "pv", u)
                    own(act.activation(slot("pv", u)[:, P:2 * P], slot("pv", u)[:, 0:P], ACT.Square, scale=rsum[:, 0, stat(u, 0)],
                                       accum_out=ssA[:, NT * h + i:NT * h + i + 1]))
                    freed(act.activation(qT[:, h, i * P:i * P + P], slot("pv", u)[:, 0:P], ACT.Copy, scale=rsum[:, 0, stat(u, 0)]), "pv", u)
                if filler(u):
                    name, c, n = filler(u)
                    copy_out((qT if name == "q" else kTt)[:, c, 256 * n:256 * n + 256], slot(*filler(u))[:, 0:256], filler(u),
                             scale=0.125 if name == "q" else 1.0)
            act.dma_start(M[:, :, :], m_dram.rearrange("(k p) n -> p k n", p=P)).then_inc(m_loaded, 16)
            act.activation(rtA[:, :], ssA[:, :], ACT.Sqrt, bias=eps[:, :], scale=1.0 / P).then_inc(o_root, 1)
            for h in range(4):
                wait_full(act, "oT", h)
                act.activation(oThi[:, h, :], slot("oT", h)[:, :], ACT.Copy, scale=colA[:, 92:93]).then_inc(o_hi, 1)
            with act.Fori(0, 4) as i:
                for d in range(2):
                    wait_full(act, "gate", "b", d, i=i)
                    act.wait_ge(free[plan.slot(("y", "b", d))], plan.uses(("y", "b", d), i))
                    freed(act.activation(sgB[:, d, :], slot("gate", "b", d)[:, :], ACT.Sigmoid), "gate", "b", d)
            for k in range(KT):
                act.wait_ge(m_final, k + 1)
                act.activation(Uhi[:, k, :], M[:, k, :], ACT.Copy).then_inc(m_hi, 1)
            begin_stage(stages["mix1"])
            act.wait_ge(m_lo, KT)
            first_half("w_out", yM)
            run_stage(stages["mix1"], ("w_out", 1))

            def hidden(name, parts, i):
                k, j = (0, 0) if i is None else (i, i * 2 + 2)
                base = hid_base[name]
                for c in range(2):
                    if name == "f1":
                        wait_full(act, name, parts[0], c, i=k)
                        if i is not None:
                            act.wait_ge(hid_lo, i * 2 + base + c + 1)
                        freed(act.activation(hg[:, c, :], slot(name, parts[0], c)[:, :], ACT.Silu), name, parts[0], c)
                    else:
                        act.wait_ge(conv_done, j + c + 1)
                        act.activation(hg[:, c, :], hg[:, c, :], ACT.Silu).then_inc(act_done, 1)
                for c in range(2):
                    if name == "f1":
                        wait_freed(act, name, parts[1], c, i=k)
                    else:
                        act.wait_ge(hid_prod, j + c + 1)
                    if i is not None:
                        wait_full(act, name, "d", 7, i=i)
                    act.activation(Hhi[:, c, :], hg[:, c, :], ACT.Copy).then_inc(hid_hi, 1)

            def ffn(name, st):
                hidden(name, ("first g", "first u"), None)
                if name == "f1":
                    begin_stage(st)
                    act.dma_start(relT[:, :], a["rel_bias_2"].rearrange("b h -> h b"), allow_slow_non_contiguous=True).then_inc(line_in, 16)
                with act.Fori(0, PAIRS - 1) as i:
                    hidden(name, ("g", "u"), i)
                if name == "f1":
                    act.wait_ge(line_ok, 1)
                    act.dma_start(line_dram.rearrange("q h j -> h q j"), line[:, :].unsqueeze(1).to_broadcast([8, P, 384])).then_inc(line_in, 16)
                if name == "f2":
                    wait_full(act, name, "u", 1, i=PAIRS - 2)
                    begin_stage(st)
                act.wait_ge(hid_lo, hid_base[name] + FC)
                run_stage(st, (name, "last d"))

            ffn("f1", stages["ffn1"])
            copy_out(aL[:, :], slot("ga")[0:16, :], ("ga",))
            copy_out(sk[:, :], slot("sk")[:, :], ("sk",))
            copy_out(rT[:, 0, :], slot("sv")[:, :], ("sv",))
            for c in range(4):
                copy_out((gq, gq, gk, gk)[c][:, c % 2, :], slot("gqk", c)[:, :], ("gqk", c), scale=0.125 if c < 2 else 1.0)
            copy_out(sv[:, :, :], slot("svT")[:, :].rearrange("p (t c) -> p t c", c=P), ("svT",))
            act.wait_ge(g_abs, 1)
            own(act.activation(gt[:, :, :], gt[:, :, :], ACT.Exp, scale=-1.0))
            act.activation(gt[:, :, :], gt[:, :, :], ACT.Ln, bias=1.0).then_inc(g_ln, 1)
            act.wait_ge(g_cum, 1)
            act.activation(gx[:, :, :], gt[:, :, :], ACT.Exp, scale=1.0 / 16).then_inc(g_e1, 1)
            act.wait_ge(g_d, 1)
            act.activation(gx[:, :, :], gx[:, :, :], ACT.Exp, scale=1.0 / 16).then_inc(g_e2, 1)
            act.wait_ge(k_end, 1)
            act.activation(decay[:, :, :], gt[:, :, 63::64], ACT.Exp, scale=1.0 / 16).then_inc(g_e3, 1)
            act.activation(gx[:, :, :], gt[:, :, :], ACT.Exp, scale=-1.0 / 16).then_inc(g_e3, 1)
            for c in range(4):
                copy_out(sq[:, c, :], slot("sq", c)[:, :], ("sq", c), scale=0.125)
            for c in range(4):
                wait_full(act, "r", c)
                freed(act.activation(rT[:, c, :], slot("r", c)[:, :], ACT.Silu), "r", c)
            act.wait_ge(q_dec, 1)
            for t in range(NT):
                copy_out(gv[:, t, :], slot("gv", t)[:, 0:HALF], ("gv", t))
            for j in range(2):
                copy_out(kendt[:, 4 * j:4 * j + 4, :], slot("kendT", j)[:, :].rearrange("p (t c) -> p t c", t=4), ("kendT", j))
            act.dma_start(sw[0:64, :], sk[64:128, :]).then_inc(keys_swapped, 16)
            act.dma_start(sw[64:128, :], sk[0:64, :]).then_inc(keys_swapped, 16)
            act.wait_ge(line_in, 32)
            act.dma_start(bias[:, :, :], bass.AP(tensor=line_dram.tensor, offset=P - 1, ap=[[8 * 384 - 1, P], [384, 8], [1, 256]])).then_inc(bias_in, 16)
            for t in range(-2, NT):
                if t >= 0:
                    k0 = 1 if t == 0 else 0
                    if t >= 1:
                        wait_full(act, "so", t - 1)
                    for g in range(2):
                        copy_out(pTs[:, 4 * g:4 * g + 4, k0:2, :],
                                 slot("spT", t, g)[:, :].rearrange("p (h k c) -> p h k c", h=4, k=2)[:, :, k0:2, :], ("spT", t, g))
                if t >= 0:
                    wait_full(act, "go", t)
                    for h in range(4):
                        c = (h % 2) * HALF + (h // 2) * P
                        ins = act.activation(gj[:, :], slot("go", t)[:, c:c + P], ACT.Square, accum_out=ssA[:, 4 * t + h:4 * t + h + 1])
                        if h < 3:
                            own(ins)
                        else:
                            ins.then_inc(g_ss, 1)
                            act.wait_ge(g_ss, t + 1)
                if t + 2 < NT:
                    n = t + 2
                    c0 = P if n == 0 else 0
                    act.wait_ge(s_max, n + 1)
                    for h in range(8):
                        act.activation(sS[:, n % 3, h, c0:256], sS[:, n % 3, h, c0:256], ACT.Exp, bias=smax[:, n % 2, h:h + 1],
                                       accum_out=lsum[:, n % 2, h:h + 1]).then_inc(s_exp, 1)
                    act.wait_ge(s_shift, n + 1)
                    act.activation(sexp[:, n % 2, :], sexp[:, n % 2, :], ACT.Exp).then_inc(s_sexp, 1)
            act.activation(rtA[:, :], ssA[:, :], ACT.Sqrt, bias=eps[:, :], scale=1.0 / P).then_inc(g_root, 1)
            wait_full(act, "so", NT - 1)
            begin_stage(stages["mem"])
            for t in range(NT):
                act.wait_ge(mix_t, t + 1)
                wait_full(act, "mixT", t)
                act.activation(Uhi[:, 0:4, t * P:t * P + P], mixt[:, t % 2, :, :], ACT.Copy).then_inc(mix_hi, 1)
                act.activation(Uhi[:, 4:8, t * P:t * P + P], slot("mixT", t)[:, HALF:D].rearrange("p (k c) -> p k c", k=4), ACT.Copy).then_inc(mix_hi, 1)
                if t >= 2:
                    first_half("w_out2", y3, t - 2, t - 1)
            first_half("w_out2", y3, NT - 2)
            for t in range(2):
                act.wait_ge(h_loaded[t], 16 * stages["mem"]["load"][t])
            act.wait_ge(gains_in, 16 * stages["mem"]["gains"])
            begin_stage(stages["mix2"])
            run_stage(stages["mem"])
            run_stage(stages["mix2"], ("w_out2", 1))
            def values_out(cb):
                copy_out(vC[:, :, cb * HALF:cb * HALF + HALF], slot("wv", cb)[:, :].rearrange("p (t n) -> p t n", t=2), ("wv", cb))

            for key, cb in CROSS[:-1]:
                if key == "wk":
                    copy_out(kC[:, 4 * cb:4 * cb + 4, :], slot(key, cb)[:, :].rearrange("p (c n) -> p c n", c=4), (key, cb))
                elif key == "wv":
                    values_out(cb)
                else:
                    for c in range(4):
                        copy_out(qC[:, 4 * cb + c, :], slot(key, cb, c)[:, :], (key, cb, c), scale=0.0625)
            for u in range(-2, len(CU)):
                if u >= 0:
                    if u >= 2:
                        wait_full(act, "co", u - 2)
                    copy_out(pTC[:, u % 2, :, :], slot("cT", u)[:, :].rearrange("p (k n) -> p k n", k=2), ("cT", u))
                if u + 2 < len(CU):
                    n = u + 2
                    act.wait_ge(c_max, n + 1)
                    if n >= 2:
                        wait_full(act, "cT", n - 2)
                        act.wait_ge(c_norm, n - 1)
                    for j in range(4):
                        act.activation(pC[:, n % 2, j, :], slot("cs", n)[:, j * MEM:j * MEM + MEM], ACT.Exp, bias=nmax[:, n % 2, j:j + 1],
                                       accum_out=lsum[:, n % 2, j:j + 1]).then_inc(c_exp, 1)
                if u == -1:
                    values_out(1)
                if u >= 0:
                    hf, h = CU[u]
                    wait_full(act, "co", u)
                    act.activation(Uhi[:, 2 * h:2 * h + 2, hf * HALF:hf * HALF + HALF],
                                   slot("co", u)[:, :].rearrange("p (k n) -> p k n", k=2), ACT.Copy).then_inc(c_hi, 1)
                if u >= 5:
                    first_half("w_o", y4, u - 5, u - 4)
            begin_stage(stages["cross"])
            first_half("w_o", y4, 3)
            run_stage(stages["cross"], ("w_o", 1))
            ffn("f2", stages["ffn2"])
            for n in range(2):
                act.wait_ge(out_stored[n], 16 * (NT // 2))

        @block.vector
        def _(dve):
            own = Chain(dve, dve_own)

            def tt(o, x, y, op):
                return dve.tensor_tensor(o, x, y, op)

            def stt(o, x, s, y, op0, op1):
                return dve.scalar_tensor_tensor(out=o, in0=x, scalar=s, in1=y, op0=op0, op1=op1)

            def lo_of(dst, src, hi, key):
                freed(tt(dst, src, hi.bitcast(f32), ALU.subtract), *key)

            def run_stage(st, mm=None):
                n, hin, xn, Y = st["n"], st["hin"], st["xn"], st["Y"]
                nx = 2 if st["dest"] else NT
                dve.wait_ge(gains_in, 16 * st["gains"])

                def add_last(t):
                    wait_full(dve, *mm, t)
                    freed(tt(Y[:, t, :], Y[:, t, :], slot(*mm, t)[:, :], ALU.add), *mm, t)

                down = st["fused"] == "down" and st["kind"] == "post"
                if down:
                    add_last(0)
                for s in range(n + 2):
                    if s < n and st["kind"] != "load":
                        b = s % st["bufs"]
                        if st["kind"] == "post":
                            dve.wait_ge(post_root, st["posts"] + s + 1)
                            own(dve.reciprocal(rsp[:, s % 4:s % 4 + 1], rtp[:, s % 4:s % 4 + 1]))
                            ins = stt(Y[:, s, :], Y[:, s, :], rsp[:, s % 4:s % 4 + 1], st["gpost"][:, :], ALU.mult, ALU.mult)
                            if down:
                                ins.then_inc(y_scaled, 1)
                            else:
                                own(ins)
                                dve.wait_ge(h_loaded[b], 16 * st["load"][s])
                                tt(hin[:, b, :], hin[:, b, :], Y[:, s, :], ALU.add).then_inc(h_new, 1)
                        elif st["fused"] == "add":
                            dve.wait_ge(h_loaded[b], 16 * st["load"][s])
                            wait_full(dve, *mm, s)
                            freed(tt(hin[:, b, HALF:D], hin[:, b, HALF:D], slot(*mm, s)[:, 0:HALF], ALU.add), *mm, s)
                            wait_freed(dve, *mm, s)
                            wait_freed(dve, mm[0], 0, s)
                            tt(hin[:, b, 0:HALF], hin[:, b, 0:HALF], Y[:, s, :], ALU.add).then_inc(h_new, 1)
                        else:
                            dve.wait_ge(acc_added, s + 1)
                            wait_full(dve, *mm, s)
                            freed(tt(hin[:, b, :], hin[:, b, :], slot(*mm, s)[:, :], ALU.add), *mm, s)
                            wait_freed(dve, *mm, s)
                            dve.sem_inc(h_new, 1)
                    t = s - 1
                    if 0 <= t < n:
                        b = t % st["bufs"]
                        dve.wait_ge(pre_root, st["first"] + t + 1)
                        own(dve.reciprocal(rs[:, t % 4:t % 4 + 1], rt[:, t % 4:t % 4 + 1]))
                        stt(xn[:, t % nx, :], hin[:, b, :], rs[:, t % 4:t % 4 + 1], st["gpre"][:, :], ALU.mult, ALU.mult).then_inc(xn_done, 1)
                    if down and s + 1 < n:
                        add_last(s + 1)
                    t = s - 2
                    if t >= 0 and st["dest"] is not None:
                        hi, lo = st["dest"]
                        dve.wait_ge(tr_hi, st["turns"] + t + 1)
                        lo_of(lo[:, :, t * P:t * P + P], slot("T", st["name"], t)[:, :].rearrange("p (k c) -> p k c", k=KT),
                              hi[:, :, t * P:t * P + P], ("T", st["name"], t))

            run_stage(stages["x"])
            dve.wait_ge(params_in, 16 * N_PARAMS)
            for m in range(2):
                dve.tensor_tensor_reduce(out=lamj[:, m, :], in0=lamr[:, 2 * m, :], in1=lamr[:, 2 * m + 1, :], scale=1.0, scalar=0.0,
                                         op0=ALU.mult, op1=ALU.add, accum_out=lam2[:, m:m + 1]).then_inc(lam_sum, 1)
            dve.wait_ge(pool_own, 4)
            own(dve.reciprocal(cnt[:, :], cnt[:, :]))
            for g in range(4):
                w = 2 << g
                wait_freed(dve, "p", g)
                for j in range(g + 1):
                    sh = 1 << j
                    dst = pS if j % 2 == 0 else pX
                    s_ap = pT[:, g, :] if j == 0 else (pS[:, g, :] if j % 2 == 1 else pX[:, :])
                    d_ap = pS[:, g, :] if j % 2 == 0 else pX[:, :]
                    own(dve.tensor_copy(d_ap[:, 0:sh], s_ap[:, 0:sh]))
                    own(tt(d_ap[:, sh:SEQ], s_ap[:, sh:SEQ], s_ap[:, 0:SEQ - sh], ALU.add))
                last = pS[:, g, :] if g % 2 == 0 else pX[:, :]
                own(tt(last[:, 0:w - 1], last[:, 0:w - 1], cnt[:, 0:w - 1], ALU.mult))
                own(dve.tensor_scalar(last[:, w - 1:SEQ], last[:, w - 1:SEQ], 1.0 / w, None, ALU.mult))
                tt(pS[:, g, :], last, pT[:, g, :], ALU.subtract).then_inc(pool_ready, 1)
                dve.wait_ge(pool_ready, g + 1)
            dve.wait_ge(lam_exp, 1)
            own(tt(nlam[:, :], lame[:, 1:2], lame[:, 0:1], ALU.subtract))
            own(dve.tensor_scalar(nlam[:, :], nlam[:, :], -LAMBDA_INIT, None, ALU.add))
            dve.wait_ge(cols_in, 1)
            own(dve.tensor_scalar(colA[:, 92:93], colA[:, 92:93], 1.0 - LAMBDA_INIT, None, ALU.mult))
            for g in range(4):
                dve.wait_ge(pool_hi, g + 1)
                freed(stt(poollo[:, g, :], slot("pool", g)[:, :], colA[:, 88 + g:89 + g], poolhi[:, g, :].bitcast(f32),
                          ALU.mult, ALU.subtract), "pool", g)
            with dve.Fori(0, 4) as i:
                for d in range(2):
                    wait_freed(dve, "gate", "a", d, i=i)
                    wait_full(dve, "y", "a", d, i=i)
                    dve.wait_ge(m_stored[d], i * 16 + 16)
                    freed(tt(mst[:, d, :], sgA[:, d, :], slot("y", "a", d)[:, :], ALU.mult), "y", "a", d)
            for d in range(2):
                dve.wait_ge(m_stored[d], 16 * 5)
            dve.wait_ge(dist_made, 1)

            def scores(u):
                h, i = UNITS[u]
                w = P * (i + 1)
                c0 = SEQ - w
                for m in range(2):
                    wait_full(dve, "sc", u, m)
                    if u >= 3:
                        wait_full(dve, "aT", u - 3)
                    freed(stt(pp[:, u % 3, m, 0:w], dist[:, c0:SEQ], 2.0 ** (-2 * (h + 1)), slot("sc", u, m)[:, 0:w], ALU.mult, ALU.add),
                          "sc", u, m)
                    wait_freed(dve, "sc", u, m)
                    dve.tensor_reduce(nmax[:, 0, stat(u, m)], pp[:, u % 3, m, 0:w], axis=AX.X, op=ALU.max, negate=True).then_inc(neg_max, 1)

            def combine(u):
                w, k = P * (UNITS[u][1] + 1), 2 * (u % 4)
                dve.wait_ge(p_exp, 2 * u + 2)
                own(dve.reciprocal(rsum[:, 0, k:k + 2], lsum[:, 0, k:k + 2]))
                own(stt(c2[:, 0, stat(u, 0)], rsum[:, 0, stat(u, 1)], nlam[:, :], lsum[:, 0, stat(u, 0)], ALU.mult, ALU.mult))
                stt(pp[:, u % 3, 0, 0:w], pp[:, u % 3, 1, 0:w], c2[:, 0, stat(u, 0)], pp[:, u % 3, 0, 0:w], ALU.mult, ALU.add).then_inc(a_done, 1)

            scores(0)
            scores(1)
            combine(0)
            for u in range(len(UNITS)):
                if u + 1 < len(UNITS):
                    combine(u + 1)
                if u + 2 < len(UNITS):
                    scores(u + 2)
            dve.wait_ge(o_root, 1)
            own(dve.reciprocal(rsA[:, :], rtA[:, :]))
            for h in range(4):
                v = qT[:, h, :].rearrange("p (i c) -> p i c", i=NT)
                tt(v, v, rsA[:, 8 * h:8 * h + 8].unsqueeze(2).to_broadcast([P, NT, P]), ALU.mult).then_inc(o_scaled, 1)
            for h in range(4):
                dve.wait_ge(o_hi, h + 1)
                freed(stt(oTlo[:, h, :], slot("oT", h)[:, :], colA[:, 92:93], oThi[:, h, :].bitcast(f32), ALU.mult, ALU.subtract), "oT", h)
            dve.wait_ge(m_loaded, 16)
            with dve.Fori(0, 4) as i:
                own.loop(i, 2)
                for d in range(2):
                    wait_freed(dve, "gate", "b", d, i=i)
                    wait_full(dve, "y", "b", d, i=i)
                    freed(tt(prB[:, d, :], sgB[:, d, :], slot("y", "b", d)[:, :], ALU.mult), "y", "b", d)
                    wait_freed(dve, "y", "b", d, i=i)
                    m = M[:, bass.ds(i * 2 + d, 1), :].rearrange("p o n -> p (o n)")
                    own(tt(m, m, prB[:, d, :], ALU.add))
                    dve.sem_inc(m_final, 1)
            own.end(4)
            for k in range(KT):
                dve.wait_ge(m_hi, k + 1)
                tt(Ulo[:, k, :], M[:, k, :], Uhi[:, k, :].bitcast(f32), ALU.subtract).then_inc(m_lo, 1)
            run_stage(stages["mix1"], ("w_out", 1))

            def hidden_lo(name, c, i):
                dve.wait_ge(hid_hi, hid_base[name] + c + 1 + (0 if i is None else i * 2 + 2))
                tt(Hlo[:, c, :], hg[:, c, :], Hhi[:, c, :].bitcast(f32), ALU.subtract).then_inc(hid_lo, 1)

            def add_down(name, i):
                for t in range(NT):
                    wait_full(dve, name, "d", t, i=i)
                    freed(tt(acc[:, t, :], acc[:, t, :], slot(name, "d", t)[:, :], ALU.add), name, "d", t)

            def clear_acc(st, others=()):
                for t in range(NT - 2, NT):
                    wait_full(dve, "T", st["name"], t)
                for t in range(NT - 3, NT):
                    dve.wait_ge(h_stored[t % 3], 16 * st["store"][t])
                own(dve.memset(acc[:, :, :], 0.0))

            clear_acc(stages["mix1"])
            def gated(gate, value, i=0):
                for c in range(2):
                    wait_freed(dve, "f1", gate, c, i=i)
                    wait_full(dve, "f1", value, c, i=i)
                    freed(tt(hg[:, c, :], hg[:, c, :], slot("f1", value, c)[:, :], ALU.mult), "f1", value, c)

            gated("first g", "first u")
            for c in range(2):
                hidden_lo("f1", c, None)
            own(dve.memset(line[:, :], NEG))
            dve.wait_ge(line_in, 16)
            for bk, d0, d1 in t5_ranges(P):
                own(dve.tensor_copy(line[:, 256 - d1:256 - d0], relT[:, bk:bk + 1].to_broadcast([8, d1 - d0])))
            dve.sem_inc(line_ok, 1)
            with dve.Fori(0, PAIRS - 1) as i:
                gated("g", "u", i)
                add_down("f1", i)
                for c in range(2):
                    hidden_lo("f1", c, i)
            run_stage(stages["ffn1"], ("f1", "last d"))
            for hp in range(2):
                wait_full(dve, "alpha", hp)
                freed(dve.tensor_scalar(gx[:, hp, :], slot("alpha", hp)[:, :], colA[:, 94 + hp:95 + hp], None, ALU.add), "alpha", hp)
            wait_freed(dve, "alpha", 0)
            wait_freed(dve, "alpha", 1)
            stt(gt[:, :, :], gx[:, :, :], -1.0, gx[:, :, :], ALU.mult, ALU.max).then_inc(g_abs, 1)
            own(dve.memset(reset[:, :], 1.0))
            own(dve.memset(reset[:, 0::64], 0.0))
            dve.wait_ge(g_ln, 1)
            own(stt(gx[:, :, :], gx[:, :, :], 0.0, gt[:, :, :], ALU.min, ALU.subtract))
            own(dve.tensor_tensor_scan(gt[:, 0, :], reset[:, :], gx[:, 0, :], 0.0, ALU.mult, ALU.add))
            own(dve.tensor_tensor_scan(gt[:, 1, :], reset[:, :], gx[:, 1, :], 0.0, ALU.mult, ALU.add))
            dve.sem_inc(g_cum, 1)
            for c in range(4):
                wait_freed(dve, "gqk", c)
            dve.wait_ge(g_e1, 1)
            own(tt(gq[:, :, :], gq[:, :, :], gx[:, :, :], ALU.mult))
            for hp in range(2):
                last = gt[:, hp, 63::64].unsqueeze(2).to_broadcast([P, 16, 64])
                own(tt(gx[:, hp, :].rearrange("p (n c) -> p n c", c=64), last, gt[:, hp, :].rearrange("p (n c) -> p n c", c=64), ALU.subtract))
            dve.sem_inc(g_d, 1)
            dve.wait_ge(g_e2, 1)
            tt(kend[:, :, :], gk[:, :, :], gx[:, :, :], ALU.mult).then_inc(k_end, 1)
            dve.wait_ge(g_e3, 2)
            dve.wait_ge(k_end, 1)
            tt(gk[:, :, :], gk[:, :, :], gx[:, :, :], ALU.mult).then_inc(q_dec, 1)
            def kv_ap(n, hp):
                t, par = n // 2, n % 2
                return slot("kv", t // 2)[:, par * HALF + (t % 2) * 256 + hp * P:par * HALF + (t % 2) * 256 + hp * P + P]

            def chunk_states(j):
                wait_full(dve, "kv", j)
                for n in range(4 * j, min(4 * j + 4, 15)):
                    if n == 0:
                        o = slot("kv", 0)[:, 0:256].rearrange("p (h c) -> p h c", h=2)
                        dve.tensor_copy(S[:, 1, :, :], o).then_inc(states, 1)
                    else:
                        dve.wait_ge(states, n)
                        own(stt(S[:, (n + 1) % 8, 0, :], S[:, n % 8, 0, :], decay[:, 0, n:n + 1], kv_ap(n, 0), ALU.mult, ALU.add))
                        stt(S[:, (n + 1) % 8, 1, :], S[:, n % 8, 1, :], decay[:, 1, n:n + 1], kv_ap(n, 1), ALU.mult, ALU.add).then_inc(states, 1)
                dve.wait_ge(states, min(4 * j + 4, 15))
                dve.sem_inc(free[plan.slot(("kv", j))], 1)

            wait_full(dve, "kendT", 1)
            for b in range(2):
                dve.memset(attS[:, b, :, :], 0.0).then_inc(att_ok, 1)
            dve.wait_ge(att_ok, 2)
            mask = causal[:, :].bitcast(u32).unsqueeze(1).to_broadcast([P, 2, P])

            def masked(t):
                wait_full(dve, "att", t)
                if t >= 2:
                    wait_full(dve, "go", t - 2)
                for hh in range(2):
                    src = slot("att", t)[:, hh * HALF:hh * HALF + 256].rearrange("p (h c) -> p h c", h=2)
                    ins = dve.copy_predicated(attS[:, t % 2, hh::2, :], mask, src)
                    if hh == 0:
                        own(ins)
                    else:
                        ins.then_inc(att_ok, 1)
                dve.wait_ge(att_ok, 2 + t + 1)
                dve.sem_inc(free[plan.slot(("att", t))], 1)

            def gla_output(t):
                dve.wait_ge(g_ss, t + 1)
                for hh in range(2):
                    src = slot("go", t)[:, hh * HALF:hh * HALF + 256].rearrange("p (h c) -> p h c", h=2)
                    dst = gv[:, t, :].rearrange("p (h c) -> p h c", h=4)[:, hh::2, :]
                    ins = dve.tensor_copy(dst, src)
                    if hh == 0:
                        own(ins)
                    else:
                        freed(ins, "go", t)

            def gla_norm(t):
                v = gv[:, t, :].rearrange("p (h c) -> p h c", h=4)
                tt(v, v, rsA[:, 4 * t:4 * t + 4].unsqueeze(2).to_broadcast([P, 4, P]), ALU.mult).then_inc(g_out, 1)

            dve.wait_ge(bias_in, 16)

            def windowed(n):
                b, c0 = n % 2, P if n == 0 else 0
                for g in range(2):
                    wait_full(dve, "ssc", n, g)
                    if n >= 3:
                        wait_full(dve, "spT", n - 3, g)
                    src = slot("ssc", n, g)[:, :].rearrange("p (h c k) -> p h c k", h=2, c=2)[:, :, :, c0:256]
                    dst, bs = (x.rearrange("p (c h) k -> p h c k", h=2)[:, :, :, c0:256] for x in (sS[:, n % 3, 4 * g:4 * g + 4, :], bias[:, 4 * g:4 * g + 4, :]))
                    freed(tt(dst, src, bs, ALU.add), "ssc", n, g)
                wait_freed(dve, "ssc", n, 0)
                wait_freed(dve, "ssc", n, 1)
                own(dve.tensor_reduce(smax[:, b, :], sS[:, n % 3, :, c0:256], axis=AX.X, op=ALU.max))
                own(tt(smax[:, b, :], smax[:, b, :], sink[:, :], ALU.max))
                tt(sexp[:, b, :], sink[:, :], smax[:, b, :], ALU.subtract).then_inc(s_shift, 1)
                dve.wait_ge(s_shift, n + 1)
                dve.tensor_scalar(smax[:, b, :], smax[:, b, :], -1.0, None, ALU.mult).then_inc(s_max, 1)

            for t in range(-2, NT):
                if t >= 0:
                    b = t % 2
                    dve.wait_ge(s_exp, 8 * (t + 1))
                    dve.wait_ge(s_sexp, t + 1)
                    own(tt(lsum[:, b, :], lsum[:, b, :], sexp[:, b, :], ALU.add))
                    own(dve.reciprocal(rsum[:, b, :], lsum[:, b, :]))
                if 0 <= t + 1 < NT:
                    masked(t + 1)
                if t + 2 < NT:
                    windowed(t + 2)
                if 0 <= t + 1 < NT and t % 2:
                    chunk_states((t + 1) // 2)
                if t >= 0:
                    gla_output(t)
                    wait_full(dve, "so", t)
                    for j in range(2):
                        ins = tt(sq[:, :, t * P + 64 * j:t * P + 64 * j + 64], slot("so", t)[:, 0:HALF].rearrange("p (c h d) -> p h c d", c=4, h=2)[:, j],
                                 rsum[:, b, j::2].unsqueeze(2).to_broadcast([P, 4, 64]), ALU.mult)
                        if j == 0:
                            own(ins)
                        else:
                            freed(ins, "so", t)

            def gated_mix(t):
                wait_full(dve, "mixT", t)
                if t >= 2:
                    dve.wait_ge(mix_hi, 2 * t - 2)
                stt(mixt[:, t % 2, :, :], slot("mixT", t)[:, 0:HALF].rearrange("p (k c) -> p k c", k=4), colA[:, 93:94],
                    rT[:, :, t * P:t * P + P], ALU.mult, ALU.mult).then_inc(mix_t, 1)

            dve.wait_ge(g_root, 1)
            own(dve.reciprocal(rsA[:, :], rtA[:, :]))
            wait_freed(dve, "go", NT - 1)
            for t in range(3):
                gla_norm(t)
            gated_mix(0)
            for t in range(NT):
                ts = slice(t * P, t * P + P)
                if t + 3 < NT:
                    gla_norm(t + 3)
                if t + 1 < NT:
                    gated_mix(t + 1)
                dve.wait_ge(mix_t, t + 1)
                dve.wait_ge(mix_hi, 2 * t + 1)
                own(tt(Ulo[:, 0:4, ts], mixt[:, t % 2, :, :], Uhi[:, 0:4, ts].bitcast(f32), ALU.subtract))
                dve.wait_ge(mix_hi, 2 * t + 2)
                lo_of(Ulo[:, 4:8, ts], slot("mixT", t)[:, HALF:D].rearrange("p (k c) -> p k c", k=4), Uhi[:, 4:8, ts], ("mixT", t))
            run_stage(stages["mem"])
            run_stage(stages["mix2"], ("w_out2", 1))

            def cross_max(n):
                wait_full(dve, "cs", n)
                dve.tensor_reduce(nmax[:, n % 2, 0:4], slot("cs", n)[:, :].rearrange("p (j c) -> p j c", j=4), axis=AX.X, op=ALU.max,
                                  negate=True).then_inc(c_max, 1)

            def cross_norm(u):
                b = u % 2
                dve.wait_ge(c_exp, 4 * (u + 1))
                dve.sem_inc(free[plan.slot(("cs", u))], 1)
                own(dve.reciprocal(rsum[:, b, 0:4], lsum[:, b, 0:4]))
                tt(pC[:, b, :, :], pC[:, b, :, :], rsum[:, b, 0:4].unsqueeze(2).to_broadcast([P, 4, MEM]), ALU.mult).then_inc(c_norm, 1)

            cross_max(0)
            cross_max(1)
            cross_norm(0)
            for u in range(len(CU)):
                hf, h = CU[u]
                if u + 1 < len(CU):
                    cross_norm(u + 1)
                if u + 2 < len(CU):
                    cross_max(u + 2)
                dve.wait_ge(c_hi, u + 1)
                lo_of(Ulo[:, 2 * h:2 * h + 2, hf * HALF:hf * HALF + HALF], slot("co", u)[:, :].rearrange("p (k n) -> p k n", k=2),
                      Uhi[:, 2 * h:2 * h + 2, hf * HALF:hf * HALF + HALF], ("co", u))
            run_stage(stages["cross"], ("w_o", 1))
            clear_acc(stages["cross"])

            def convolved(gate, value, i):
                k, j = (0, 0) if i is None else (i, i * 2 + 2)

                def column(x, n):
                    return x[:, n:n + 1] if i is None else x[:, bass.ds(i * 2 + (n + 2), 1)]

                for c in range(2):
                    for part, dst, n in ((gate, hg, c), (value, hv, FC + c)):
                        o = slot("f2", part, c)
                        wait_full(dve, "f2", part, c, i=k)
                        if part == gate and i is not None:
                            dve.wait_ge(hid_lo, i * 2 + hid_base["f2"] + c + 1)
                        own(dve.tensor_scalar(dst[:, c, :], o[:, :], column(colB, n), column(colB, n + 44), ALU.mult, ALU.add))
                        own(stt(dst[:, c, 1:SEQ], o[:, 0:SEQ - 1], column(colA, n + 44), dst[:, c, 1:SEQ], ALU.mult, ALU.add))
                        freed(stt(dst[:, c, 2:SEQ], o[:, 0:SEQ - 2], column(colA, n), dst[:, c, 2:SEQ], ALU.mult, ALU.add), "f2", part, c)
                        wait_freed(dve, "f2", part, c, i=k)
                        if part == gate:
                            dve.sem_inc(conv_done, 1)
                for c in range(2):
                    dve.wait_ge(act_done, j + c + 1)
                    own(tt(hg[:, c, :], hg[:, c, :], hv[:, c, :], ALU.mult))
                    dve.sem_inc(hid_prod, 1)

            convolved("first g", "first u", None)
            for c in range(2):
                hidden_lo("f2", c, None)
            with dve.Fori(0, PAIRS - 1) as i:
                own.loop(i, 10)
                convolved("g", "u", i)
                add_down("f2", i)
                for c in range(2):
                    hidden_lo("f2", c, i)
            own.end(PAIRS - 1)
            run_stage(stages["ffn2"], ("f2", "last d"))


_INS = ['x', 'w_in', 'pool_mix', 'pool_scale', 'w_branch_a', 'lam_q1', 'lam_k1', 'lam_q2', 'lam_k2', 'subln_g',
        'w_branch_b', 'w_out', 'mix_pre_g', 'mix_post_g', 'ffn_pre_g', 'ffn_post_g', 'w_ffn_gate', 'w_ffn_up',
        'w_ffn_down', 'mem_2', 'norm_mix_2', 'w_in_2', 'w_alpha_2', 'b_alpha_2', 'gla_gain_2', 'rel_bias_2',
        'sinks_2', 'w_out_2', 'norm_cross_2', 'norm_mem_2', 'w_q_c_2', 'w_k_c_2', 'w_v_c_2', 'w_o_c_2', 'norm_ffn_2',
        'w_up_2', 'conv_w_2', 'conv_b_2', 'w_down_2', 'norm_final_2']


def kernel(**inputs):
    import numpy as _np
    import concourse.bacc as _bacc
    from concourse import mybir as _mybir
    from concourse.bass_utils import run_bass_kernel_spmd as _run

    nc = _bacc.Bacc("TRN2", target_bir_lowering=False, num_devices=1, dynamic_dma_scratch_size=1024)
    arrays, args = {}, {}
    for name in _INS:
        v = _np.ascontiguousarray(inputs[name])
        arrays[f"in_{name}"] = v
        args[name] = nc.dram_tensor(f"in_{name}", v.shape, _mybir.dt.from_np(v.dtype), kind="ExternalInput").ap()
    out = nc.dram_tensor("out_0", (1, SEQ, D), _mybir.dt.float32, kind="ExternalOutput").ap()
    build(nc, args, out)
    r = _run(nc, [arrays], core_ids=[0])
    return r.results[0]["out_0"]
```
